# Optimizing a Trainium2 kernel written in Bass

```python
import math
import jax, jax.numpy as jnp
from jax import lax
import numpy as np
import jax
import jax.numpy as jnp

D_MODEL = 1024
BATCH = 1
SEQ = 512
DEPTH = 1

RET_HEADS = 4
RET_QK_DIM = 128
RET_V_DIM = 256
RET_CHUNK = 128
RET_QK_WIDTH = RET_HEADS * RET_QK_DIM
RET_V_WIDTH = RET_HEADS * RET_V_DIM
ROPE_BASE = 10000.0
SGU_GROUPS = 4
SGU_GROUP_DIM = 256
SGU_CHUNK = 128
SGU_WIDTH = SGU_GROUPS * SGU_GROUP_DIM
IN_WIDTHS = (RET_QK_WIDTH, RET_QK_WIDTH, RET_V_WIDTH, RET_V_WIDTH, SGU_WIDTH, SGU_WIDTH, D_MODEL, D_MODEL)
IN_WIDTH = 7168
IN_SPLITS = (512, 1024, 2048, 3072, 4096, 5120, 6144)
PEER_HEADS = 8
PEER_N_KEYS = 128
PEER_N_EXPERTS = PEER_N_KEYS * PEER_N_KEYS
PEER_KEY_DIM = 256
PEER_HALF = PEER_KEY_DIM // 2
PEER_TOPK = 16
PEER_TOKEN_BLOCK = 128
N_MOD = 6
EPS = 1e-6


def rms_norm(x, gain):
    xf = x.astype(jnp.float32)
    y = xf * lax.rsqrt(jnp.mean(xf * xf, axis=-1, keepdims=True) + EPS)
    return (y * gain.astype(jnp.float32)).astype(x.dtype)

def modulate(h, shift, scale):
    return h * (1 + scale[:, None, :]) + shift[:, None, :]

def rotary(x, pos):
    d = x.shape[-1]
    half = d // 2
    inv = ROPE_BASE ** (-jnp.arange(half, dtype=jnp.float32) * 2.0 / d)
    ang = pos[:, None] * inv[None, :]
    cos = jnp.cos(ang)[None, :, None, :].astype(x.dtype)
    sin = jnp.sin(ang)[None, :, None, :].astype(x.dtype)
    x1, x2 = x[..., :half], x[..., half:]
    return jnp.concatenate([x1 * cos - x2 * sin, x1 * sin + x2 * cos], axis=-1)

def retention(q, k, v):
    B, S, H, dk = q.shape
    dv = v.shape[-1]
    C = RET_CHUNK
    nc = S // C
    gamma = 1.0 - 2.0 ** (-5.0 - jnp.arange(H, dtype=jnp.float32))
    log_g = jnp.log(gamma)
    idx = jnp.arange(C, dtype=jnp.float32)
    diff = idx[:, None] - idx[None, :]
    decay_in = jnp.where((diff >= 0)[None], jnp.exp(log_g[:, None, None] * jnp.maximum(diff, 0.0)[None]), 0.0).astype(q.dtype)
    decay_q = jnp.exp(log_g[None, :] * (idx[:, None] + 1.0)).astype(q.dtype)[None, :, :, None]
    decay_k = jnp.exp(log_g[None, :] * (C - 1.0 - idx[:, None])).astype(q.dtype)[None, :, :, None]
    decay_chunk = jnp.exp(log_g * C).astype(q.dtype)[None, :, None, None]

    def to_chunks(t):
        return t.reshape(B, nc, C, H, t.shape[-1]).transpose(1, 0, 2, 3, 4)

    def step(state, inp):
        qi, ki, vi = inp
        s = jnp.einsum('bihd,bjhd->bhij', qi, ki) * decay_in
        inner = jnp.einsum('bhij,bjhv->bihv', s, vi)
        cross = jnp.einsum('bihd,bhdv->bihv', qi, state) * decay_q
        new_state = state * decay_chunk + jnp.einsum('bjhd,bjhv->bhdv', ki * decay_k, vi)
        return new_state, inner + cross

    state0 = jnp.zeros((B, H, dk, dv), q.dtype)
    _, y = lax.scan(step, state0, (to_chunks(q), to_chunks(k), to_chunks(v)))
    return y.transpose(1, 0, 2, 3, 4).reshape(B, S, H, dv)

def head_norm(y, gain):
    B, S = y.shape[:2]
    yf = y.astype(jnp.float32)
    mu = jnp.mean(yf, axis=-1, keepdims=True)
    var = jnp.mean(jnp.square(yf - mu), axis=-1, keepdims=True)
    yn = ((yf - mu) * lax.rsqrt(var + EPS)).reshape(B, S, -1)
    return (yn * gain.astype(jnp.float32)).astype(y.dtype)

def spatial_gating(u, sv, ln_g, ln_b, w_s, b_s):
    B, S, _ = u.shape
    vf = sv.astype(jnp.float32)
    mu = jnp.mean(vf, axis=-1, keepdims=True)
    var = jnp.mean(jnp.square(vf - mu), axis=-1, keepdims=True)
    vn = ((vf - mu) * lax.rsqrt(var + EPS) * ln_g.astype(jnp.float32) + ln_b.astype(jnp.float32)).astype(sv.dtype)
    nck = S // SGU_CHUNK
    vn = vn.reshape(B, nck, SGU_CHUNK, SGU_GROUPS, SGU_GROUP_DIM)
    mask = jnp.tril(jnp.ones((SGU_CHUNK, SGU_CHUNK), dtype=bool))
    ws = jnp.where(mask[None], w_s, jnp.zeros_like(w_s))
    mixed = jnp.einsum('gts,bnsgc->bntgc', ws, vn) + b_s.T[None, None, :, :, None]
    return u * mixed.reshape(B, S, SGU_WIDTH)

def peer(h, w_q, sub_keys, expert_u, expert_v):
    B, S, D = h.shape
    blocks = h.reshape(-1, PEER_TOKEN_BLOCK, D)
    K = PEER_TOPK

    def block(hb):
        T = hb.shape[0]
        q = (hb @ w_q).reshape(T, PEER_HEADS, 2, PEER_HALF)
        s = jnp.einsum('thpc,hpnc->thpn', q, sub_keys)
        sub_s, sub_i = lax.top_k(s, K)
        cand = (sub_s[:, :, 0, :, None] + sub_s[:, :, 1, None, :]).reshape(T, PEER_HEADS, K * K)
        top_s, top_i = lax.top_k(cand, K)
        k1 = jnp.take_along_axis(sub_i[:, :, 0], top_i // K, axis=-1)
        k2 = jnp.take_along_axis(sub_i[:, :, 1], top_i % K, axis=-1)
        expert = k1 * PEER_N_KEYS + k2
        g = jax.nn.softmax(top_s.astype(jnp.float32), axis=-1).astype(hb.dtype)
        ue = expert_u[expert]
        act = jax.nn.gelu(jnp.einsum('td,thkd->thk', hb, ue), approximate=False) * g
        ve = expert_v[expert]
        return jnp.einsum('thk,thkd->td', act, ve)

    return lax.map(block, blocks).reshape(B, S, D)

def first_inputs(seed: int = 0) -> dict:
    key = jax.random.key(seed)
    ks = jax.random.split(key, 21)
    L, D = DEPTH, D_MODEL
    f32 = jnp.float32
    nrm = lambda k, shape, s: jax.random.normal(k, shape, f32) * s
    return {
        "x": nrm(ks[0], (BATCH, SEQ, D), 1.0),
        "c": nrm(ks[1], (BATCH, D), 1.0),
        "w_ada": nrm(ks[2], (L, D, N_MOD * D), 0.5 * D ** -0.5),
        "b_ada": nrm(ks[3], (L, N_MOD * D), 0.01),
        "norm1_g": 1.0 + nrm(ks[4], (L, D), 0.02),
        "w_in": nrm(ks[5], (L, D, IN_WIDTH), D ** -0.5),
        "ret_gn_g": 1.0 + nrm(ks[6], (L, RET_V_WIDTH), 0.02),
        "sgu_ln_g": 1.0 + nrm(ks[7], (L, SGU_WIDTH), 0.02),
        "sgu_ln_b": nrm(ks[8], (L, SGU_WIDTH), 0.01),
        "sgu_w": nrm(ks[9], (L, SGU_GROUPS, SGU_CHUNK, SGU_CHUNK), 0.5 * SGU_CHUNK ** -0.5),
        "sgu_b": 1.0 + nrm(ks[10], (L, SGU_GROUPS, SGU_CHUNK), 0.01),
        "w_ret_out": nrm(ks[11], (L, RET_V_WIDTH, D), RET_V_WIDTH ** -0.5),
        "w_sgu_out": nrm(ks[12], (L, SGU_WIDTH, D), SGU_WIDTH ** -0.5),
        "w_out": nrm(ks[13], (L, D, D), D ** -0.5),
        "norm2_g": 1.0 + nrm(ks[14], (L, D), 0.02),
        "peer_w_q": nrm(ks[15], (L, D, PEER_HEADS * PEER_KEY_DIM), D ** -0.5),
        "peer_sub_keys": nrm(ks[16], (L, PEER_HEADS, 2, PEER_N_KEYS, PEER_HALF), PEER_HALF ** -0.5),
        "peer_u": nrm(ks[17], (L, PEER_N_EXPERTS, D), D ** -0.5),
        "peer_v": nrm(ks[18], (L, PEER_N_EXPERTS, D), 1.0),
        "final_g": 1.0 + nrm(ks[19], (D,), 0.02),
    }

def first_block(x, c, w_ada, b_ada, norm1_g, w_in, ret_gn_g, sgu_ln_g, sgu_ln_b, sgu_w, sgu_b, w_ret_out, w_sgu_out, w_out, norm2_g, peer_w_q, peer_sub_keys, peer_u, peer_v, final_g):
    B, S, D = x.shape
    pos = jnp.arange(S, dtype=jnp.float32)
    c_act = jax.nn.silu(c)
    for l in range(DEPTH):
        mod = c_act @ w_ada[l] + b_ada[l]
        shift1, scale1, gate1, shift2, scale2, gate2 = jnp.split(mod, N_MOD, axis=-1)

        h = modulate(rms_norm(x, norm1_g[l]), shift1, scale1)
        proj = h @ w_in[l]
        q, k, v, g_ret, u, sv, gate_a, gate_b = jnp.split(proj, IN_SPLITS, axis=-1)

        q = rotary(q.reshape(B, S, RET_HEADS, RET_QK_DIM), pos)
        k = rotary(k.reshape(B, S, RET_HEADS, RET_QK_DIM), pos) * (RET_QK_DIM ** -0.5)
        v = v.reshape(B, S, RET_HEADS, RET_V_DIM)
        y_ret = head_norm(retention(q, k, v), ret_gn_g[l])
        branch_a = (jax.nn.silu(g_ret) * y_ret) @ w_ret_out[l]

        y_sgu = spatial_gating(jax.nn.gelu(u, approximate=False), jax.nn.gelu(sv, approximate=False),
                               sgu_ln_g[l], sgu_ln_b[l], sgu_w[l], sgu_b[l])
        branch_b = y_sgu @ w_sgu_out[l]

        merged = jax.nn.sigmoid(gate_a) * branch_a + jax.nn.sigmoid(gate_b) * branch_b
        x = x + gate1[:, None, :] * (merged @ w_out[l])

        h2 = modulate(rms_norm(x, norm2_g[l]), shift2, scale2)
        x = x + gate2[:, None, :] * peer(h2, peer_w_q[l], peer_sub_keys[l], peer_u[l], peer_v[l])
    return rms_norm(x, final_g)


_first_inputs = first_inputs


def first_inputs(seed=0):
    import zlib

    import numpy as np

    out = dict(_first_inputs(seed))
    spreads = {}
    factors = {'norm1_g': 4.22,
     'ret_gn_g': 187.671,
     'sgu_ln_g': 200.0,
     'sgu_ln_b': 200.0,
     'sgu_b': 200.0,
     'final_g': 20.429,
     'norm2_g': 64.0}
    for name, (base, spread) in spreads.items():
        noise = np.random.default_rng([zlib.crc32(name.encode()), seed]).standard_normal(out[name].shape)
        drawn = base * np.exp(spread * noise) if base else spread * noise
        out[name] = __import__('jax').numpy.asarray(drawn.astype(out[name].dtype))
    for name, factor in factors.items():
        out[name] = (out[name] * factor).astype(out[name].dtype)
    return out


_narrow_inputs = first_inputs


def first_inputs(seed=0):

    out = dict(_narrow_inputs(seed))
    wider = {'sgu_ln_g': 5.28, 'sgu_ln_b': 11.04, 'sgu_b': 3.48, 'final_g': 3.04}
    for name, times in wider.items():
        mean = out[name].mean()
        out[name] = (mean + times * (out[name] - mean)).astype(out[name].dtype)
    return out


DEPTH_2 = 2

CTX_LEN = 256
GRID_W = 64
BLOCK = 128
WINDOW = 128
NEG_INF = -1e30

H_A = 8
HKV_A = 2
G_A = H_A // HKV_A
HD_A = 64
SCALE_A = HD_A ** -0.5

H_B = 8
Q_LORA = 384
KV_LORA = 256
NOPE_B = 64
ROPE_B = 32
V_B = 64
SCALE_B = (NOPE_B + ROPE_B) ** -0.5

W_C = 512
CONV_K = 3

W_BRANCH = 512

IN_SIZES = (H_A * HD_A, HKV_A * HD_A, HKV_A * HD_A, W_BRANCH,
            Q_LORA, KV_LORA, ROPE_B, W_BRANCH,
            W_C, W_C, W_C, W_BRANCH,
            D_MODEL, D_MODEL, D_MODEL)
D_IN = sum(IN_SIZES)


def rms_norm_2(x, g):
    xf = x.astype(jnp.float32)
    y = xf * lax.rsqrt(jnp.mean(xf * xf, axis=-1, keepdims=True) + EPS)
    return (y * g.astype(jnp.float32)).astype(x.dtype)

def axial_rope_angles(rows, rot_dim):
    row = jnp.repeat(jnp.arange(rows, dtype=jnp.float32), GRID_W)
    col = jnp.tile(jnp.arange(GRID_W, dtype=jnp.float32), rows)
    axis_dim = rot_dim // 2
    inv = ROPE_BASE ** (-jnp.arange(0, axis_dim, 2, dtype=jnp.float32) / axis_dim)
    ang = jnp.concatenate([row[:, None] * inv, col[:, None] * inv], axis=-1)
    return jnp.cos(ang), jnp.sin(ang)

def apply_rope(x, cos, sin):
    xf = x.astype(jnp.float32)
    x1, x2 = jnp.split(xf, 2, axis=-1)
    c = cos[None, :, None, :]
    s = sin[None, :, None, :]
    return jnp.concatenate([x1 * c - x2 * s, x2 * c + x1 * s], axis=-1).astype(x.dtype)

def in_proj(h, w_in):
    splits = np.cumsum(IN_SIZES)[:-1].tolist()
    return jnp.split(h @ w_in, splits, axis=-1)

def window_attn_latent(q, k, v, k_ctx, v_ctx, sink):
    B, S = q.shape[:2]
    nb = S // BLOCK
    qb = q.reshape(B, nb, BLOCK, HKV_A, G_A, HD_A)
    pad = ((0, 0), (BLOCK, BLOCK), (0, 0), (0, 0))
    kp = jnp.pad(k, pad).reshape(B, nb + 2, BLOCK, HKV_A, HD_A)
    vp = jnp.pad(v, pad).reshape(B, nb + 2, BLOCK, HKV_A, HD_A)
    kw = jnp.concatenate([kp[:, :-2], kp[:, 1:-1], kp[:, 2:]], axis=2)
    vw = jnp.concatenate([vp[:, :-2], vp[:, 1:-1], vp[:, 2:]], axis=2)
    s_loc = jnp.einsum('bnqhgd,bnkhd->bnhgqk', qb, kw).astype(jnp.float32) * SCALE_A
    qi = jnp.arange(BLOCK)[:, None] + BLOCK
    kj = jnp.arange(3 * BLOCK)[None, :]
    band = jnp.abs(kj - qi) <= WINDOW
    kabs = jnp.arange(nb)[:, None] * BLOCK + jnp.arange(3 * BLOCK)[None, :] - BLOCK
    valid = (kabs >= 0) & (kabs < S)
    mask = band[None, :, :] & valid[:, None, :]
    s_loc = jnp.where(mask[None, :, None, None], s_loc, NEG_INF)
    s_ctx = jnp.einsum('bnqhgd,blhd->bnhgql', qb, k_ctx).astype(jnp.float32) * SCALE_A
    s_sink = jnp.broadcast_to(sink.astype(jnp.float32).reshape(1, 1, HKV_A, G_A, 1, 1),
                              s_loc.shape[:-1] + (1,))
    p = jax.nn.softmax(jnp.concatenate([s_loc, s_ctx, s_sink], axis=-1), axis=-1)
    p_loc = p[..., :3 * BLOCK].astype(v.dtype)
    p_ctx = p[..., 3 * BLOCK:3 * BLOCK + k_ctx.shape[1]].astype(v.dtype)
    o = (jnp.einsum('bnhgqk,bnkhd->bnqhgd', p_loc, vw)
         + jnp.einsum('bnhgql,blhd->bnqhgd', p_ctx, v_ctx))
    return o.reshape(B, S, H_A * HD_A)

def ctx_gqa_attn(q, k, v, sink):
    B, L = q.shape[:2]
    qg = q.reshape(B, L, HKV_A, G_A, HD_A)
    s = jnp.einsum('blhgd,bmhd->bhglm', qg, k).astype(jnp.float32) * SCALE_A
    sk = jnp.broadcast_to(sink.astype(jnp.float32).reshape(1, HKV_A, G_A, 1, 1), (B, HKV_A, G_A, L, 1))
    p = jax.nn.softmax(jnp.concatenate([s, sk], axis=-1), axis=-1)[..., :L]
    o = jnp.einsum('bhglm,bmhd->blhgd', p.astype(v.dtype), v)
    return o.reshape(B, L, H_A * HD_A)

def mla_project(q_lat, kv_lat, g_qa, w_qb, g_kva, w_kvb):
    B, T = q_lat.shape[:2]
    q = (rms_norm_2(q_lat, g_qa) @ w_qb).reshape(B, T, H_B, NOPE_B + ROPE_B)
    kv = (rms_norm_2(kv_lat, g_kva) @ w_kvb).reshape(B, T, H_B, NOPE_B + V_B)
    return q[..., :NOPE_B], q[..., NOPE_B:], kv[..., :NOPE_B], kv[..., NOPE_B:]

def mla_attn_latent(qn, qr, kn, kr, v, kn_c, kr_c, v_c):
    B, S = qn.shape[:2]
    nb = S // BLOCK
    keys_n = jnp.concatenate([kn, kn_c], axis=1)
    keys_r = jnp.concatenate([kr, kr_c], axis=1)
    vals = jnp.concatenate([v, v_c], axis=1)

    def block(qs):
        q_n, q_r = qs
        s = (jnp.einsum('bqhd,bkhd->bhqk', q_n, keys_n)
             + jnp.einsum('bqhd,bkd->bhqk', q_r, keys_r))
        p = jax.nn.softmax(s.astype(jnp.float32) * SCALE_B, axis=-1)
        return jnp.einsum('bhqk,bkhd->bqhd', p.astype(vals.dtype), vals)

    qn_b = qn.reshape(B, nb, BLOCK, H_B, NOPE_B).swapaxes(0, 1)
    qr_b = qr.reshape(B, nb, BLOCK, H_B, ROPE_B).swapaxes(0, 1)
    o = lax.map(block, (qn_b, qr_b))
    return o.swapaxes(0, 1).reshape(B, S, H_B * V_B)

def ctx_mla_attn(qn, qr, kn, kr, v):
    B, L = qn.shape[:2]
    s = jnp.einsum('blhd,bmhd->bhlm', qn, kn) + jnp.einsum('blhd,bmd->bhlm', qr, kr)
    p = jax.nn.softmax(s.astype(jnp.float32) * SCALE_B, axis=-1)
    o = jnp.einsum('bhlm,bmhd->blhd', p.astype(v.dtype), v)
    return o.reshape(B, L, H_B * V_B)

def short_gated_conv(b_gate, c_gate, u, conv_w):
    z = jnp.pad(c_gate * u, ((0, 0), (1, 1), (0, 0)))
    y = conv_w[0] * z[:, :-2] + conv_w[1] * z[:, 1:-1] + conv_w[2] * z[:, 2:]
    return b_gate * y

def merge_branches(ya, yb, yc, za, zb, zc, ga, gb, gc, w_branch, w_o):
    m = (jax.nn.sigmoid(ga) * ((ya * jax.nn.silu(za)) @ w_branch[0])
         + jax.nn.sigmoid(gb) * ((yb * jax.nn.silu(zb)) @ w_branch[1])
         + jax.nn.sigmoid(gc) * ((yc * jax.nn.silu(zc)) @ w_branch[2]))
    return m @ w_o

def mixer_layer(x, ctx, mod_x, mod_c, rope_a, rope_b, g_pre, g_post, w_in, sink,
                g_qa, w_qb, g_kva, w_kvb, conv_w, w_branch, w_o, update_ctx):
    B, S, _ = x.shape
    L = ctx.shape[1]
    shift_x, scale_x, gate_x = [m[:, None, :] for m in jnp.split(mod_x, 3, axis=-1)]
    shift_c, scale_c, gate_c = jnp.split(mod_c, 3, axis=-1)
    hx = rms_norm_2(x, g_pre) * (1.0 + scale_x) + shift_x
    hc = rms_norm_2(ctx, g_pre) * (1.0 + scale_c) + shift_c
    (qa_x, ka_x, va_x, za_x, qlb_x, kvlb_x, krb_x, zb_x,
     bc_x, cc_x, uc_x, zc_x, ga_x, gb_x, gc_x) = in_proj(hx, w_in)
    (qa_c, ka_c, va_c, za_c, qlb_c, kvlb_c, krb_c, zb_c,
     bc_c, cc_c, uc_c, zc_c, ga_c, gb_c, gc_c) = in_proj(hc, w_in)

    cos_a, sin_a = rope_a
    qa = apply_rope(qa_x.reshape(B, S, H_A, HD_A), cos_a, sin_a)
    ka = apply_rope(ka_x.reshape(B, S, HKV_A, HD_A), cos_a, sin_a)
    va = va_x.reshape(B, S, HKV_A, HD_A)
    kac = ka_c.reshape(B, L, HKV_A, HD_A)
    vac = va_c.reshape(B, L, HKV_A, HD_A)
    ya_x = window_attn_latent(qa, ka, va, kac, vac, sink)

    cos_b, sin_b = rope_b
    qn_x, qr_x, kn_x, vb_x = mla_project(qlb_x, kvlb_x, g_qa, w_qb, g_kva, w_kvb)
    qr_x = apply_rope(qr_x, cos_b, sin_b)
    kr_x = apply_rope(krb_x[:, :, None, :], cos_b, sin_b)[:, :, 0]
    qn_c, qr_c, kn_c, vb_c = mla_project(qlb_c, kvlb_c, g_qa, w_qb, g_kva, w_kvb)
    yb_x = mla_attn_latent(qn_x, qr_x, kn_x, kr_x, vb_x, kn_c, krb_c, vb_c)

    yc_x = short_gated_conv(bc_x, cc_x, uc_x, conv_w)

    out_x = merge_branches(ya_x, yb_x, yc_x, za_x, zb_x, zc_x, ga_x, gb_x, gc_x, w_branch, w_o)
    x = x + gate_x * rms_norm_2(out_x, g_post)

    if update_ctx:
        ya_c = ctx_gqa_attn(qa_c.reshape(B, L, H_A, HD_A), kac, vac, sink)
        yb_c = ctx_mla_attn(qn_c, qr_c, kn_c, krb_c, vb_c)
        yc_c = short_gated_conv(bc_c, cc_c, uc_c, conv_w)
        out_c = merge_branches(ya_c, yb_c, yc_c, za_c, zb_c, zc_c, ga_c, gb_c, gc_c, w_branch, w_o)
        ctx = ctx + gate_c * rms_norm_2(out_c, g_post)
    return x, ctx

def second_inputs(seed: int = 0) -> dict:
    key = jax.random.key(seed)
    ks = jax.random.split(key, 17)
    f32 = jnp.float32

    def nrm(k, shape, scale):
        return jax.random.normal(k, shape, f32) * scale

    return {
        "x": nrm(ks[0], (BATCH, SEQ, D_MODEL), 1.0),
        "c": nrm(ks[1], (BATCH, D_MODEL), 1.0),
        "ctx": nrm(ks[2], (BATCH, CTX_LEN, D_MODEL), 1.0),
        "c_ctx": nrm(ks[3], (D_MODEL,), 1.0),
        "w_mod": nrm(ks[4], (DEPTH_2, D_MODEL, 3 * D_MODEL), 0.5 * D_MODEL ** -0.5),
        "b_mod": nrm(ks[5], (DEPTH_2, 3 * D_MODEL), 0.01),
        "g_pre": 1.0 + nrm(ks[6], (DEPTH_2, D_MODEL), 0.05),
        "g_post": 1.0 + nrm(ks[7], (DEPTH_2, D_MODEL), 0.05),
        "w_in": nrm(ks[8], (DEPTH_2, D_MODEL, D_IN), D_MODEL ** -0.5),
        "sink": nrm(ks[9], (DEPTH_2, H_A), 1.0),
        "g_qa": 1.0 + nrm(ks[10], (DEPTH_2, Q_LORA), 0.05),
        "w_qb": nrm(ks[11], (DEPTH_2, Q_LORA, H_B * (NOPE_B + ROPE_B)), Q_LORA ** -0.5),
        "g_kva": 1.0 + nrm(ks[12], (DEPTH_2, KV_LORA), 0.05),
        "w_kvb": nrm(ks[13], (DEPTH_2, KV_LORA, H_B * (NOPE_B + V_B)), KV_LORA ** -0.5),
        "conv_w": nrm(ks[14], (DEPTH_2, CONV_K, W_C), CONV_K ** -0.5),
        "w_branch": nrm(ks[15], (DEPTH_2, 3, W_BRANCH, D_MODEL), W_BRANCH ** -0.5),
        "w_o": nrm(ks[16], (DEPTH_2, D_MODEL, D_MODEL), D_MODEL ** -0.5),
    }

def second_block(x, c, ctx, c_ctx, w_mod, b_mod, g_pre, g_post, w_in, sink,
              g_qa, w_qb, g_kva, w_kvb, conv_w, w_branch, w_o):
    rows = x.shape[1] // GRID_W
    rope_a = axial_rope_angles(rows, HD_A)
    rope_b = axial_rope_angles(rows, ROPE_B)
    sc = jax.nn.silu(c)
    scc = jax.nn.silu(c_ctx)
    for i in range(DEPTH_2):
        mod_x = sc @ w_mod[i] + b_mod[i]
        mod_c = scc @ w_mod[i] + b_mod[i]
        x, ctx = mixer_layer(x, ctx, mod_x, mod_c, rope_a, rope_b, g_pre[i], g_post[i],
                             w_in[i], sink[i], g_qa[i], w_qb[i], g_kva[i], w_kvb[i],
                             conv_w[i], w_branch[i], w_o[i], update_ctx=(i < DEPTH_2 - 1))
    return x


def setup_inputs(seed=0):
    out = dict(first_inputs(seed))
    for name, value in second_inputs(seed + 1).items():
        if name != "x":
            out[name + "_2"] = value
    return out


def reference(
    x, c, w_ada, b_ada, norm1_g, w_in, ret_gn_g, sgu_ln_g, sgu_ln_b, sgu_w, sgu_b, w_ret_out,
    w_sgu_out, w_out, norm2_g, peer_w_q, peer_sub_keys, peer_u, peer_v, final_g, c_2, ctx_2,
    c_ctx_2, w_mod_2, b_mod_2, g_pre_2, g_post_2, w_in_2, sink_2, g_qa_2, w_qb_2, g_kva_2,
    w_kvb_2, conv_w_2, w_branch_2, w_o_2,
):
    x = first_block(
        x, c, w_ada, b_ada, norm1_g, w_in, ret_gn_g, sgu_ln_g, sgu_ln_b, sgu_w, sgu_b,
        w_ret_out, w_sgu_out, w_out, norm2_g, peer_w_q, peer_sub_keys, peer_u, peer_v, final_g,
    )
    return second_block(
        x, c_2, ctx_2, c_ctx_2, w_mod_2, b_mod_2, g_pre_2, g_post_2, w_in_2, sink_2, g_qa_2,
        w_qb_2, g_kva_2, w_kvb_2, conv_w_2, w_branch_2, w_o_2,
    )


_drawn_inputs = setup_inputs


def setup_inputs(seed=0):
    import zlib

    import numpy as np

    out = dict(_drawn_inputs(seed))
    spreads = {}
    factors = {'c_2': 2.751,
     'ctx_2': 42.282,
     'c_ctx_2': 41.87,
     'b_mod_2': 8.0,
     'g_pre_2': 8.0,
     'g_post_2': 8.0,
     'sink_2': 8.0,
     'g_qa_2': 64.0,
     'w_qb_2': 37.139,
     'g_kva_2': 64.0,
     'w_kvb_2': 36.604,
     'conv_w_2': 2.753}
    for name, (base, spread) in spreads.items():
        noise = np.random.default_rng([zlib.crc32(name.encode()), seed]).standard_normal(out[name].shape)
        drawn = base * np.exp(spread * noise) if base else spread * noise
        out[name] = jnp.asarray(drawn.astype(out[name].dtype))
    for name, factor in factors.items():
        out[name] = (out[name] * factor).astype(out[name].dtype)
    return out
```

```python
import numpy as np
import concourse.bass as bass
from concourse import mybir
from contextlib import ExitStack

P = 128
D = 1024
T = 512
C = 256
A = T + C
KD = D // P
TX, TA = T // P, A // P
EPS = 1e-6
RET_H, RET_DK, RET_DV = 4, 128, 256
PH, PK, NK = 8, 16, 128
NEG = -3.0e38
MASKED = -1e30
LAYERS = 2
HA, HDA, HB, NOPE, ROPE, VB = 8, 64, 8, 64, 32, 64
QKB = NOPE + ROPE
QL, KVL = 3, 2
IN_SIZES = (512, 128, 128, 512, 384, 256, 32, 512, 512, 512, 512, 512, 1024, 1024, 1024)
IN_NAMES = ("qa", "ka", "va", "za", "qlb", "kvlb", "krb", "zb", "bc", "cc", "uc", "zc", "ga", "gb", "gc")
IN_AT = dict(zip(IN_NAMES, np.concatenate([[0], np.cumsum(IN_SIZES)[:-1]]).tolist()))
GROUP = 4
GROUPS = NK // GROUP
RING = 8
TB = 32
NTB = T // TB

VEC = {}
_at = 0
for _name, _n in [("c3", 24), ("bias", 96), ("norm1", 8), ("retg", 8), ("norm2", 8), ("final", 8),
                  ("sink", 16), ("pre0", 8), ("post0", 8), ("qa0", 3), ("kva0", 2), ("conv0", 12),
                  ("pre1", 8), ("post1", 8), ("qa1", 3), ("kva1", 2), ("conv1", 12)]:
    VEC[_name] = _at
    _at += _n
NVEC = _at

CONSTS = [("ident", 128), ("perm128", 128), ("permA", 128), ("permB", 96), ("iota128", 128), ("iota16", 16)]
TAB1 = [("cosR", T), ("sinR", T), ("decay", RET_H * T)]
TAB2 = [("cosA", T), ("sinA", T), ("cosB", T), ("sinB", T), ("band", 3 * P)]


class Job:
    pass


class Plan:

    def __init__(self):
        self.jobs, self.by_key, self.ranks = [], {}, {"A": 0, "V": 0}
        self.chunks, self.free, self.chunk_at = [], [], {}

    def chunk(self, key, what):
        self.chunk_at[key] = len(self.chunks)
        self.chunks.append(what)
        self.free.append(None)

    def job(self, key, owner, frees=()):
        j = Job()
        j.key, j.owner, j.fill, j.rank = key, owner, len(self.jobs), self.ranks[owner]
        j.bank = j.fill % RING
        j.before = self.jobs[j.fill - RING] if j.fill >= RING else None
        self.ranks[owner] += 1
        self.jobs.append(j)
        assert key not in self.by_key
        self.by_key[key] = j
        for c in frees:
            self.free[self.chunk_at[c]] = j.fill + 1


def units(kind, l):
    out = []
    for h in range(HA):
        for qb in range(TX):
            lo, hi = (max(qb - 1, 0), min(qb + 2, TX)) if kind == "A" else (0, TX)
            out.append((h, qb, lo, hi))
        if l == 0:
            out += [(h, TX + c, 0, 0) for c in range(C // P)]
    return out


def make_plan():
    p = Plan()

    def lin(key, what, owner, n, cols=("x",)):
        for f in range(n):
            p.chunk((key, f), (*what, f))
            for c in cols:
                p.job((key, f, c), owner, [(key, f)] if c == cols[-1] else [])

    def rows(key, what, owner):
        for half in range(2):
            for s in range(4):
                p.chunk((key, 4 * half + s), (*what, 4 * half + s))
            for t in range(TX):
                p.job((key, half, t), owner, [(key, 4 * half + s) for s in range(4)] if t == TX - 1 else [])

    for f in range(96):
        p.chunk(("mod", f), ("mod", f))
        p.job(("mod", f), "V", [("mod", f)])
    p.job(("norm1", "x"), "A")
    for f in range(9):
        if f < 8:
            p.chunk(("qk", f), ("w_in", 0, f))
            p.job(("qk", f), "A", [("qk", f)])
        if f:
            p.job(("qkp", f - 1), "V")
    rows("v", ("w_in", 1024), "A")
    for h in range(RET_H):
        for jt in range(TX):
            p.job(("s", h, jt), "V")
        if h:
            for e in range(2):
                p.job(("y", h - 1, e), "A")
    for e in range(2):
        p.job(("y", RET_H - 1, e), "A")
    rows("sv", ("w_in", 4096), "A")
    for h in range(RET_H):
        p.job(("mean", h), "V")
    for h in range(RET_H):
        p.job(("var", h), "A")
    lin("g_ret", ("w_in", 2048), "A", 8)
    lin("gate_a", ("w_in", 5120), "A", 8)
    lin("ret_out", ("w_ret_out", 0), "V", 8)
    lin("u", ("w_in", 3072), "A", 8)
    for f in range(8):
        p.job(("mix", f), "V")
    lin("gate_b", ("w_in", 6144), "A", 8)
    lin("sgu_out", ("w_sgu_out", 0), "V", 8)
    lin("w_out", ("w_out", 0), "V", 8)
    p.job(("norm2", "x"), "A")
    for f in range(17):
        if f < 16:
            p.chunk(("pq", f), ("peer_w_q", 0, f))
            p.job(("pq", f), "A", [("pq", f)])
        if f:
            p.job(("sc", f - 1), "A")
    for tt in range(TX):
        p.job(("kt", tt), "V")
        for q in range(P // 4):
            p.job(("g", tt, q), "A")
    for g in range(GROUPS + 1):
        if g < GROUPS:
            for j in range(GROUP):
                p.chunk(("U", g, j), ("U", g * GROUP + j))
                p.job(("U", g, j), "A", [("U", g, j)])
        if g:
            for j in range(GROUP):
                p.chunk(("V", g - 1, j), ("V", (g - 1) * GROUP + j))
            for d in range(KD):
                p.job(("V", g - 1, d), "V", [("V", g - 1, j) for j in range(GROUP)] if d == KD - 1 else [])
    p.job(("final", "x"), "A")
    for l in range(LAYERS):
        upd = l < LAYERS - 1
        xc = ("x", "c") if upd else ("x",)
        p.job(("pre", l, "x"), "A")
        p.job(("pre", l, "c"), "A")
        for f in range(6):
            if f < 5:
                p.chunk(("qa", l, f), ("qa", l, f))
                both = upd or f == 4
                p.job(("qa", l, f, "x"), "A", [] if both else [("qa", l, f)])
                if both:
                    p.job(("qa", l, f, "c"), "A", [("qa", l, f)])
            if f:
                p.job(("qap", l, f - 1), "V")
        p.chunk(("va", l), ("in2", l, IN_AT["va"]))
        p.job(("va", l, "x"), "A")
        p.job(("va", l, "c"), "A", [("va", l)])

        def attend(kind, after=None):
            us = units(kind, l)
            n = len(us)
            for s in range(n + 2):
                if s < n:
                    if kind == "B" and us[s][1] == 0:
                        heads(us[s][0])
                    if us[s][3] > us[s][2]:
                        p.job(("S", kind, l, s, 0), "V")
                    p.job(("S", kind, l, s, 1), "V")
                if 1 <= s <= n:
                    _, _, lo, hi = us[s - 1]
                    p.job(("T", kind, l, s - 1, 0), "A")
                    if hi - lo + 2 > 4:
                        p.job(("T", kind, l, s - 1, 1), "A")
                if s >= 2:
                    p.job(("Y", kind, l, s - 2), "V")

        def heads(h):
            if h == 0:
                project(0)
            if h + 1 < HB:
                project(h + 1)

        def project(h):
            p.chunk(("hb", l, h), ("hb", l, h))
            p.job(("hq", l, h, "x"), "A")
            if upd:
                p.job(("hq", l, h, "c"), "A")
            p.job(("hk", l, h, "x"), "A")
            p.job(("hk", l, h, "c"), "A", [("hb", l, h)])
            p.job(("hqp", l, h), "V")

        def branch(b, zname):
            lin(("z", b, l), ("in2", l, IN_AT[zname]), "A", 4, xc)
            if b < 2:
                for f in range(4):
                    for c in xc:
                        p.job(("yt", b, l, f, c), "V")
            merge(b)

        def merge(b):
            for f in range(8):
                p.chunk(("gate", b, l, f), ("in2", l, IN_AT["ga"] + b * D, f))
                for c in xc:
                    p.job(("gate", b, l, f, c), "A", [("gate", b, l, f)] if c == xc[-1] else [])
                if f % 2 == 0:
                    p.chunk(("br", b, l, f // 2), ("br", l, b, f // 2))
                for c in xc:
                    last = f % 2 == 1 and c == xc[-1]
                    p.job(("br", b, l, f, c), "V", [("br", b, l, f // 2)] if last else [])

        attend("A")
        branch(0, "za")
        lin(("lat", l), ("in2", l, IN_AT["qlb"]), "A", 3, xc)
        lin(("latkv", l), ("in2", l, IN_AT["kvlb"]), "A", 2, ("x", "c"))
        p.chunk(("krb", l), ("krb", l))
        p.job(("krb", l, "x"), "A")
        p.job(("krb", l, "c"), "A", [("krb", l)])
        p.job(("krbp", l), "V")
        for c in xc:
            p.job(("qn", l, c), "A")
        for c in ("x", "c"):
            p.job(("kvn", l, c), "A")
        p.chunk(("vb", l), ("vb", l))
        for t in range(TA):
            p.job(("vb", l, t), "A", [("vb", l)] if t == TA - 1 else [])
        attend("B")
        branch(1, "zb")
        for f in range(4):
            for name, owner in (("cc", "A"), ("uc", "V"), ("bc", "V"), ("zc", "A")):
                p.chunk((name, l, f), ("in2", l, IN_AT[name], f))
                for c in xc:
                    p.job((name, l, f, c), owner, [(name, l, f)] if c == xc[-1] else [])
        merge(2)
        lin(("wo", l), ("w_o", l), "A", 8, xc)
        for c in xc:
            p.job(("post", l, c), "A")
    return p


class Counts:

    def __init__(self, eng, plan):
        self.eng, self.plan = eng, plan
        self.made, self.taken, self.last = {}, {}, None
        self.turn, self.moves = None, {}

    def at(self, sem, value):
        assert value > 0
        return value if self.turn is None else self.turn * self.moves.get(sem.name, 0) + value

    def inc(self, sem):
        self.made[sem.name] = self.made.get(sem.name, 0) + 1
        self.last = sem
        return 1

    def own(self):
        return self.last, self.at(self.last, self.made[self.last.name])

    def next(self, sem, n=1):
        self.taken[sem.name] = self.taken.get(sem.name, 0) + n
        return self.at(sem, self.taken[sem.name])

    def filling(self, filled, key):
        return self.at(filled, self.plan.by_key[key].fill + 1)

    def reading(self, sem, key):
        return self.at(sem, self.plan.by_key[key].rank + 1)

    def loop(self, turns, moves):
        made, taken = dict(self.made), dict(self.taken)
        self.moves = {sem.name: n for sem, n in moves.items()}
        with self.eng.Fori(0, turns) as i:
            self.turn = i
            yield i
        self.turn = None
        for now, before in ((self.made, made), (self.taken, taken)):
            for name in now:
                step = now[name] - before.get(name, 0)
                assert step == 0 or step == self.moves.get(name, 0), (name, step)
                now[name] = before.get(name, 0) + turns * step


def build(nc, plan, d, out):
    f32, u32, i32 = mybir.dt.float32, mybir.dt.uint32, mybir.dt.int32
    ALU, ACT, AX = mybir.AluOpType, mybir.ActivationFunctionType, mybir.AxisListType.X
    gates_dram = nc.dram_tensor("gates_by_expert", [NTB, P, NK, TB], f32, kind="Internal").ap()

    ctx = ExitStack()
    with ctx:
        def sb(name, shape, dt=f32):
            return ctx.enter_context(nc.sbuf_tensor(name, shape, dt))

        XT = sb("XT", [P, KD, A])
        HT = sb("HT", [P, KD, A])
        WR = sb("WR", [P, RING, KD, P])
        vec = sb("vec", [P, NVEC])
        consts = {n: sb(n, [P, w]) for n, w in CONSTS}
        ones = sb("ones", [P, P])
        epsc = sb("epsc", [P, 1])
        cs = sb("cs", [P, KD, 3])
        mod = sb("mod", [P, 96, 3])
        scl1 = sb("scl1", [P, KD])
        scl2 = sb("scl2", [P, KD])
        pre = sb("pre", [P, LAYERS, 2, KD])
        post = sb("post", [P, LAYERS, 2, KD])
        rt = sb("rt", [P, A])
        rk = sb("rk", [P, A])
        tab = sb("tab", [P, 4096])
        mx = sb("mx", [P, 4])
        nm = sb("nm", [P, 4])
        es = sb("es", [P, 4])
        sm = sb("sm", [P, 4])
        ri = sb("ri", [P, 4])
        stats = sb("stats", [P, TX, 2, 6])
        mv = sb("mv", [P, TX, 2])
        rs = sb("rs", [P, TX])
        ARENA = 25600
        arena = sb("arena", [P, ARENA])

        class Cut:
            def __init__(self, at=0):
                self.at = at

            def __call__(self, *dims):
                n = int(np.prod(dims))
                v = arena[:, self.at:self.at + n]
                self.at += n
                assert self.at <= ARENA, self.at
                if len(dims) == 2:
                    v = v.rearrange("p (a b) -> p a b", a=dims[0])
                if len(dims) == 3:
                    v = v.rearrange("p (a b c) -> p a b c", a=dims[0], b=dims[1])
                return v

        bank = [ctx.enter_context(nc.psum_tensor(f"bank{b}", [P, 512], f32)) for b in range(RING)]

        def sem(name):
            return ctx.enter_context(nc.semaphore(name))

        filled = sem("filled")
        act_read, dve_read = sem("act_read"), sem("dve_read")
        act_step, dve_step = sem("act_step"), sem("dve_step")
        w_loaded = [sem(f"w_loaded{s}") for s in range(RING)]
        g_loaded = [sem(f"g_loaded{b}") for b in range(2)]
        g_stored = [sem(f"g_stored{b}") for b in range(2)]
        x_loaded, ctx_loaded = sem("x_loaded"), sem("ctx_loaded")
        small_loaded, tab_loaded, tab2_loaded = sem("small_loaded"), sem("tab_loaded"), sem("tab2_loaded")
        sgu_loaded, sub_loaded, out_done = sem("sgu_loaded"), sem("sub_loaded"), sem("out_done")
        cs_ready = sem("cs_ready")
        mod_ready = sem("mod_ready")
        sq_ready = sem("sq_ready")
        xr_ready = sem("xr_ready")
        h_ready = sem("h_ready")
        keys_ready = sem("keys_ready")
        ws_ready = sem("ws_ready")
        ln_row, r_done = sem("ln_row"), sem("r_done")
        vn_ready = sem("vn_ready")
        ysq_ready = sem("ysq_ready")
        g_used = sem("g_used")
        ug_ready = sem("ug_ready")
        gated = sem("gated")
        soft_in, exp_ready = sem("soft_in"), sem("exp_ready")
        kt_ready = sem("kt_ready")
        hot_a, hot_b = sem("hot_a"), sem("hot_b")
        a_ready = sem("a_ready")
        res_ready = sem("res_ready")
        qk_ready = sem("qk_ready")
        kr_ready = sem("kr_ready")
        row_ready, p_ready = sem("row_ready"), sem("p_ready")
        lat_ready = sem("lat_ready")
        c_ready = sem("c_ready")
        block = ctx.enter_context(nc.Block())

        def V(name, k=0, n=1):
            return vec[:, VEC[name] + k:VEC[name] + k + n]

        def col(t, tt):
            return t[:, tt * P:(tt + 1) * P]

        c1 = Cut()
        qT, kT = c1(4, T), c1(4, T)
        Vr = c1(TX, D)
        ST = c1(2, TX, T)
        yT1 = c1(8, T)
        M1 = c1(8, T)
        R1 = c1(3, T)
        G1 = c1(2, T)
        lng, lnb = c1(1, D), c1(1, D)
        SV = arena[:, 0:4096].rearrange("p (a b) -> p a b", a=TX)
        uT = arena[:, 4096:8192].rearrange("p (a b) -> p a b", a=8)
        SB = yT1
        cosR, sinR = tab[:, 0:T], tab[:, T:2 * T]
        decay = tab[:, 2 * T:6 * T].rearrange("p (h t) -> p h t", h=RET_H)
        bs = tab[:, 3072:3584]
        ws = tab[:, 3584:4096].rearrange("p (g t) -> p g t", g=4)

        c2 = Cut()
        S2 = c2(TX, 16, P)
        hotA, hotB = c2(2, 4, P), c2(2, 4, P)
        Q2 = arena[:, 8192:8192 + 2 * T].rearrange("p (a b) -> p a b", a=2)
        Rw = c2(16, P)
        cand = c2(PH, PK * PK)
        top = c2(16, PK)
        topi = c2(16, PK)
        topf = c2(16, PK)
        cv, ca, cb = c2(PH, PK), c2(PH, PK), c2(PH, PK)
        kk1, kk2, gg = c2(PH, PK), c2(PH, PK), c2(PH, PK)
        cpos, cpa = c2(PH, PK), c2(PH, PK)
        gsum, KT = c2(1, 16), c2(2, 3, P)
        Gs = c2(2, NK, TB)
        SUBW = c2(1, 2048) if c2.at + 2048 <= ARENA else tab[:, 0:2048].unsqueeze(1)
        sub = SUBW[:, 0, :].rearrange("p (s n) -> p s n", s=16)

        c3 = Cut()
        aT = c3(2, GROUP, T)
        Gt = [c3(NTB, GROUP, TB) for _ in range(2)]
        ACC = c3(KD, T)

        c4 = Cut()
        M4 = c4(KD, A)
        R4 = c4(3, T)
        Srow = c4(3, A)
        PT = c4(2, TA, P)
        Y4 = c4(TA, 512)
        top4 = c4.at
        qA, kA, vA, yTA = c4(4, A), c4(1, A), c4(TA, P), c4(4, A)
        SGA = c4(2, A)
        c5 = Cut(top4)
        LAT = c5(QL + KVL, A)
        KR = c5(1, A)
        QH, KH = c5(2, A), c5(2, A)
        vB = c5(TA, 512)
        yTB = arena[:, top4:top4 + 4 * A].rearrange("p (a b) -> p a b", a=4)
        SGB = QH
        c6 = Cut(top4)
        yTC = c6(4, A)
        SGC = c6(2, A)
        C1, C2 = c6(2, A), c6(2, A)
        ZP = c6(2, A + 4)
        YT = [yTA, yTB, yTC]
        SG = [SGA, SGB, SGC]
        cosA, sinA, cosB, sinB = (tab[:, k * T:(k + 1) * T] for k in range(4))
        band = tab[:, 4 * T:4 * T + 3 * P]

        def lat_sq(j):
            return Srow[:, j, :] if j < 3 else PT.rearrange("p a b c -> p a (b c)")[:, j - 3, :]

        def xcols(c):
            return slice(0, T) if c == "x" else slice(T, A)

        @block.sync
        def _(sp):
            k = Counts(sp, plan)

            def load(n, src, gate=None):
                if n >= RING:
                    sp.wait_ge(filled, k.at(filled, plan.free[n - RING]))
                sp.dma_start(WR[:, n % RING, :, :].rearrange("p a b -> p (a b)"), src)\
                    .then_inc(w_loaded[n % RING], 16)

            W = d["weights"]
            for n in range(RING):
                load(n, W[n, :, :])
            for i in k.loop(11, {filled: RING}):
                for s in range(RING):
                    load(RING + s, W[i * RING + (RING + s), :, :])
            first_u = plan.chunk_at[("U", 0, 0)]
            for n in range(96, first_u):
                load(n, W[n, :, :])

            def load_gates(g, i=None):
                if g >= 2 or i is not None:
                    sp.wait_ge(a_ready, k.at(a_ready, GROUP * (g - 1)))
                row = g * GROUP if i is None else i * (2 * GROUP) + g * GROUP
                sp.dma_start(Gt[g % 2].rearrange("p n k t -> p n (k t)"),
                             gates_dram[:, :, bass.ds(row, GROUP), :].rearrange("n p k t -> p n (k t)"))\
                    .then_inc(g_loaded[g % 2], 16)

            for j in range(GROUP):
                load(first_u + j, W[first_u + j, :, :])
            for b in range(2):
                sp.wait_ge(g_stored[b], k.at(g_stored[b], 16 * (NTB // 2)))
            load_gates(0)
            load_gates(1)
            for c in range(8):
                load(first_u + 4 + c, W[first_u + 4 + c, :, :])
            loop0 = first_u + 12
            for i in k.loop(15, {filled: 24, a_ready: 2 * GROUP}):
                for gg_ in range(2):
                    load_gates(2 + gg_, i)
                    for c in range(8):
                        n = loop0 + 8 * gg_ + c
                        load(n, W[i * 16 + n, :, :])
            for n in range(loop0 + 15 * 16, len(plan.chunks)):
                load(n, W[n, :, :])

        @block.gpsimd
        def _(pool):
            k = Counts(pool, plan)
            pool.wait_ge(sgu_loaded, 64)
            nc.gpsimd.affine_select(out=ws, in_=ws, pattern=[[0, 4], [1, P]], compare_op=ALU.is_ge,
                                           fill=0.0, base=0, channel_multiplier=-1).then_inc(ws_ready, k.inc(ws_ready))
            for tt in range(TX):
                pool.wait_ge(dve_read, k.reading(dve_read, ("kt", tt)))
                for q in range(P // 4):
                    n = tt * (P // 4) + q
                    if n >= 2:
                        pool.wait_ge(filled, k.filling(filled, ("g", (n - 2) // 32, (n - 2) % 32)))
                    for t in range(4):
                        c = 4 * q + t
                        nc.gpsimd.tensor_scalar(hotB[:, n % 2, t, :], consts["iota128"][:, :],
                                                       KT[:, tt % 2, 1, c:c + 1], None, ALU.is_equal).then_inc(hot_b, k.inc(hot_b))

        @block.tensor
        def _(pe):
            k = Counts(pe, plan)

            def arrived(key):
                n = plan.chunk_at[key]
                pe.wait_ge(w_loaded[n % RING], k.at(w_loaded[n % RING], 16 * (n // RING + 1)))
                return WR[:, n % RING, :, :]

            def fill(key, calls):
                before = plan.by_key[key].before
                if before:
                    free = act_read if before.owner == "A" else dve_read
                    pe.wait_ge(free, k.reading(free, before.key))
                b = bank[plan.by_key[key].bank]
                for c in calls(b):
                    last = c
                last.then_inc(filled, 1)

            def product(key, out_cols, pairs, rows=P):
                def calls(b):
                    for n, (a, r) in enumerate(pairs):
                        yield nc.tensor.matmul(b[0:rows, out_cols], a, r, start=n == 0, stop=n == len(pairs) - 1)
                fill(key, calls)

            def linear(key, chunk, src, cols, nk=KD, rows=P, off=0, w=None):
                w = arrived(chunk) if w is None else w
                n = cols.stop - cols.start
                product(key, slice(0, n), [(w[:, j, off:off + rows], src(j)[:, cols]) for j in range(nk)], rows)

            def HTs(j):
                return HT[:, j, :]

            def token_rows(key, chunk0, src):
                for half in range(2):
                    for s in range(4):
                        arrived((chunk0, 4 * half + s))
                    s0 = plan.chunk_at[(chunk0, 4 * half)] % RING
                    assert s0 % 4 == 0
                    for t in range(TX):
                        product((key, half, t), slice(0, 512),
                                [(col(src(j), t), WR[:, s0:s0 + 4, j, :]) for j in range(KD)])

            def sum_squares(keys_cols, src, n):
                pe.wait_ge(sq_ready, k.next(sq_ready, n))
                for key, cols in keys_cols:
                    w = cols.stop - cols.start
                    product(key, slice(0, w), [(ones[:, :], src(j)[:, cols]) for j in range(n)])

            pe.wait_ge(cs_ready, k.next(cs_ready))

            def modulation(f, slot):
                w = WR[:, slot, :, :]
                pe.wait_ge(w_loaded[slot], k.at(w_loaded[slot], 16 * (f // RING + 1)))
                if f >= RING:
                    pe.wait_ge(dve_read, k.reading(dve_read, ("mod", f - RING)))
                product_mod(f, w)

            def product_mod(f, w):
                b = bank[f % RING]
                for j in range(KD):
                    last = nc.tensor.matmul(b[:, 0:3], w[:, j, :], cs[:, j, :], start=j == 0, stop=j == KD - 1)
                last.then_inc(filled, 1)

            for f in range(RING):
                modulation(f, f)
            moves = {dve_read: RING}
            moves.update({w_loaded[s]: 16 for s in range(RING)})
            for i in k.loop(11, moves):
                for s in range(RING):
                    modulation(RING + s, s)

            sum_squares([(("norm1", "x"), slice(0, T))], HTs, KD)
            pe.wait_ge(h_ready, k.next(h_ready, KD))
            for f in range(9):
                if f < 8:
                    linear(("qk", f), ("qk", f), HTs, slice(0, T))
                if f:
                    pe.wait_ge(act_read, k.reading(act_read, ("qk", f - 1)))
                    product(("qkp", f - 1), slice(0, T), [(consts["perm128"][:, :], R1[:, (f - 1) % 3, :])])
            token_rows("v", "v", HTs)
            def ret_values(h):
                pe.wait_ge(dve_read, k.reading(dve_read, ("s", h, TX - 1)))
                for e in range(2):
                    def calls(b, h=h, e=e):
                        for jt in range(TX):
                            yield nc.tensor.matmul(
                                b[:, jt * P:T], Vr[:, jt, h * RET_DV + e * P:h * RET_DV + (e + 1) * P],
                                ST[:, h % 2, jt, jt * P:T], start=jt == 0, stop=jt == TX - 1)
                    fill(("y", h, e), calls)
            pe.wait_ge(act_read, k.reading(act_read, ("v", 1, TX - 1)))
            pe.wait_ge(keys_ready, k.next(keys_ready))
            for h in range(RET_H):
                for jt in range(TX):
                    product(("s", h, jt), slice(0, T - jt * P), [(col(kT[:, h, :], jt), qT[:, h, jt * P:T])])
                if h:
                    ret_values(h - 1)
            ret_values(RET_H - 1)
            token_rows("sv", "sv", HTs)
            pe.wait_ge(act_read, k.reading(act_read, ("y", RET_H - 1, 1)))
            for h in range(RET_H):
                product(("mean", h), slice(0, T), [(ones[:, :], yT1[:, 2 * h + e, :]) for e in range(2)])
            for h in range(RET_H):
                pe.wait_ge(ysq_ready, k.next(ysq_ready, 2))
                product(("var", h), slice(0, T), [(ones[:, :], M1[:, 2 * h + e, :]) for e in range(2)])
            for f in range(8):
                linear(("g_ret", f, "x"), ("g_ret", f), HTs, slice(0, T))
            for f in range(8):
                linear(("gate_a", f, "x"), ("gate_a", f), HTs, slice(0, T))
            pe.wait_ge(g_used, k.at(g_used, 8))
            pe.wait_ge(act_read, k.reading(act_read, ("gate_a", 7, "x")))
            for f in range(8):
                linear(("ret_out", f, "x"), ("ret_out", f), lambda j: yT1[:, j, :], slice(0, T))
            for f in range(8):
                linear(("u", f, "x"), ("u", f), HTs, slice(0, T))
            pe.wait_ge(ws_ready, k.next(ws_ready))
            pe.wait_ge(vn_ready, k.next(vn_ready, TX))
            for f in range(8):
                def calls(b, f=f):
                    for n in range(TX):
                        yield nc.tensor.matmul(col(b, n), SV[:, n, f * P:(f + 1) * P], ws[:, f // 2, :],
                                               start=True, stop=True)
                fill(("mix", f), calls)
            for f in range(8):
                linear(("gate_b", f, "x"), ("gate_b", f), HTs, slice(0, T))
            pe.wait_ge(ug_ready, k.next(ug_ready, 8))
            for f in range(8):
                linear(("sgu_out", f, "x"), ("sgu_out", f), lambda j: uT[:, j, :], slice(0, T))
            pe.wait_ge(gated, k.next(gated, 8))
            for f in range(8):
                linear(("w_out", f, "x"), ("w_out", f), lambda j: M1[:, j, :], slice(0, T))

            sum_squares([(("norm2", "x"), slice(0, T))], HTs, KD)
            pe.wait_ge(h_ready, k.next(h_ready, KD))
            pe.wait_ge(sub_loaded, k.at(sub_loaded, 16))
            for f in range(17):
                if f < 16:
                    linear(("pq", f), ("pq", f), HTs, slice(0, T))
                if f:
                    pe.wait_ge(act_read, k.reading(act_read, ("pq", f - 1)))

                    def calls(b, f=f - 1):
                        for t in range(TX):
                            yield nc.tensor.matmul(col(b, t), col(Q2[:, f % 2, :], t), sub[:, f, :],
                                                   start=True, stop=True)
                    fill(("sc", f - 1), calls)
            for tt in range(TX):
                pe.wait_ge(kt_ready, k.next(kt_ready))

                def calls(b):
                    for n, src in enumerate((kk1, kk2, gg)):
                        yield nc.tensor.transpose(col(b, n), src.rearrange("p a b -> p (a b)"), consts["ident"][:, :])
                fill(("kt", tt), calls)
                for q in range(P // 4):
                    pe.wait_ge(hot_a, k.next(hot_a, 4))
                    pe.wait_ge(hot_b, k.next(hot_b, 4))
                    n = tt * (P // 4) + q

                    def calls(b, n=n):
                        for t in range(4):
                            yield nc.tensor.matmul(col(b, t), hotB[:, n % 2, t, :], hotA[:, n % 2, t, :],
                                                   start=True, stop=True)
                    fill(("g", tt, q), calls)

            def up(g):
                for j in range(GROUP):
                    linear(("U", g, j), ("U", g, j), HTs, slice(0, T))

            def down(g):
                for j in range(GROUP):
                    arrived(("V", g, j))
                s0 = plan.chunk_at[("V", g, 0)] % RING
                pe.wait_ge(a_ready, k.next(a_ready, GROUP))
                for dd in range(KD):
                    product(("V", g, dd), slice(0, T),
                            [(WR[:, s0 + j, dd, :], aT[:, g % 2, j, :]) for j in range(GROUP)])
            up(0)
            up(1)
            down(0)
            moves = {act_read: 2 * GROUP, dve_read: 2 * KD, a_ready: 2 * GROUP}
            moves.update({w_loaded[s]: 32 for s in range(RING)})
            for i in k.loop(15, moves):
                up(2)
                down(1)
                up(3)
                down(2)
            down(GROUPS - 1)
            sum_squares([(("final", "x"), slice(0, T))], lambda j: HT[:, j, :], KD)

            xn = 0
            for l in range(LAYERS):
                upd = l < LAYERS - 1
                xc = ("x", "c") if upd else ("x",)
                sum_squares([(("pre", l, c), xcols(c)) for c in ("x", "c")], HTs, KD)
                pe.wait_ge(h_ready, k.next(h_ready, KD))
                for f in range(6):
                    if f < 5:
                        linear(("qa", l, f, "x"), ("qa", l, f), HTs, xcols("x"))
                        if upd or f == 4:
                            linear(("qa", l, f, "c"), ("qa", l, f), HTs, xcols("c"))
                    if f:
                        pe.wait_ge(act_read, k.reading(act_read, ("qa", l, f - 1, "x")))
                        product(("qap", l, f - 1), slice(0, T), [(consts["permA"][:, :], R4[:, (f - 1) % 3, :])])
                w = arrived(("va", l))
                for c, tiles in (("x", range(0, TX)), ("c", range(TX, TA))):
                    def calls(b, tiles=tiles):
                        for n, t in enumerate(tiles):
                            for j in range(KD):
                                yield nc.tensor.matmul(col(b, n), col(HT[:, j, :], t), w[:, j, :],
                                                       start=j == 0, stop=j == KD - 1)
                    fill(("va", l, c), calls)

                def project(h):
                    w = arrived(("hb", l, h)).rearrange("p a b -> p (a b)")
                    wq = w[:, 0:QL * QKB].rearrange("p (k n) -> p k n", k=QL)
                    wk = w[:, QL * QKB:QL * QKB + KVL * NOPE].rearrange("p (k n) -> p k n", k=KVL)
                    for c in xc:
                        linear(("hq", l, h, c), None, lambda j: LAT[:, j, :], xcols(c), QL, QKB, 0, wq)
                    for c in ("x", "c"):
                        linear(("hk", l, h, c), None, lambda j: LAT[:, QL + j, :], xcols(c), KVL, NOPE, 0, wk)
                    pe.wait_ge(act_read, k.reading(act_read, ("hq", l, h, "x")))
                    product(("hqp", l, h), slice(0, T),
                            [(consts["permB"][0:QKB, 0:QKB], R4[0:QKB, h % 3, :])], QKB)

                def attend(kind):
                    us = units(kind, l)
                    n = len(us)
                    for s in range(n + 2):
                        if s < n:
                            h, qb, lo, hi = us[s]
                            if kind == "A":
                                if s == 0:
                                    pe.wait_ge(qk_ready, k.next(qk_ready))
                                p0 = HDA * (h // 4)
                                q, kk = col(qA[p0:p0 + HDA, h % 4, :], qb), kA[p0:p0 + HDA, 0, :]
                            else:
                                if qb == 0:
                                    if h == 0:
                                        project(0)
                                    if h + 1 < HB:
                                        project(h + 1)
                                    pe.wait_ge(qk_ready, k.next(qk_ready))
                                q, kk = col(QH[0:QKB, h % 2, :], qb), KH[0:QKB, h % 2, :]
                            if hi > lo:
                                product(("S", kind, l, s, 0), slice(0, (hi - lo) * P), [(q, kk[:, lo * P:hi * P])])
                            product(("S", kind, l, s, 1), slice(0, C), [(q, kk[:, T:A])])
                        if 1 <= s <= n:
                            u = s - 1
                            _, _, lo, hi = us[u]
                            tiles = hi - lo + 2
                            pe.wait_ge(p_ready, k.next(p_ready))
                            for part in range(2):
                                t0, t1 = 4 * part, min(tiles, 4 * part + 4)
                                if t1 > t0:
                                    def calls(b, t0=t0, t1=t1, u=u):
                                        for t in range(t0, t1):
                                            yield nc.tensor.transpose(col(b, t - t0), col(Srow[:, u % 3, :], t),
                                                                      consts["ident"][:, :])
                                    fill(("T", kind, l, u, part), calls)
                        if s >= 2:
                            u = s - 2
                            h, qb, lo, hi = us[u]
                            tiles = list(range(lo, hi)) + [TX, TX + 1]
                            pe.wait_ge(act_read, k.reading(act_read, ("T", kind, l, u, 1 if len(tiles) > 4 else 0)))
                            v = (lambda t: vA[:, t, HDA * (h // 4):HDA * (h // 4) + HDA]) if kind == "A" else \
                                (lambda t: vB[:, t, h * VB:(h + 1) * VB])
                            product(("Y", kind, l, u), slice(0, 64),
                                    [(PT[:, u % 2, n_, :], v(t)) for n_, t in enumerate(tiles)])

                def branch(b):
                    for f in range(4):
                        for c in xc:
                            linear((("z", b, l), f, c), (("z", b, l), f), HTs, xcols(c))
                    if b < 2:
                        kind = "AB"[b]
                        pe.wait_ge(dve_read, k.reading(dve_read, ("Y", kind, l, len(units(kind, l)) - 1)))
                        for f in range(4):
                            for c in xc:
                                def calls(bk, c=c, f=f):
                                    for n_, t in enumerate(range(0, TX) if c == "x" else range(TX, TA)):
                                        yield nc.tensor.transpose(col(bk, n_), Y4[:, t, f * P:(f + 1) * P],
                                                                  consts["ident"][:, :])
                                fill(("yt", b, l, f, c), calls)
                    merge(b)

                def merge(b):
                    if b == 2:
                        pe.wait_ge(c_ready, k.next(c_ready, 4))
                    for f in range(8):
                        for c in xc:
                            linear(("gate", b, l, f, c), ("gate", b, l, f), HTs, xcols(c))
                        if f == 0 and b < 2:
                            pe.wait_ge(dve_read, k.reading(dve_read, ("yt", b, l, 3, xc[-1])))
                        w = arrived(("br", b, l, f // 2)).rearrange("p a b -> p (a b)")
                        w = w.rearrange("p (k n) -> p k n", k=4)
                        for c in xc:
                            linear(("br", b, l, f, c), None, lambda j: YT[b][:, j, :], xcols(c), 4, P, (f % 2) * P, w)

                attend("A")
                branch(0)
                for f in range(QL):
                    for c in xc:
                        linear((("lat", l), f, c), (("lat", l), f), HTs, xcols(c))
                for f in range(KVL):
                    for c in ("x", "c"):
                        linear((("latkv", l), f, c), (("latkv", l), f), HTs, xcols(c))
                for c in ("x", "c"):
                    linear(("krb", l, c), ("krb", l), HTs, xcols(c), KD, QKB)
                pe.wait_ge(act_read, k.reading(act_read, ("krb", l, "x")))
                product(("krbp", l), slice(0, T), [(consts["permB"][0:QKB, 0:QKB], R4[0:QKB, 0, :])], QKB)
                sum_squares([(("qn", l, c), xcols(c)) for c in xc], lambda j: lat_sq(j), QL)
                sum_squares([(("kvn", l, c), xcols(c)) for c in ("x", "c")], lambda j: lat_sq(QL + j), KVL)
                pe.wait_ge(lat_ready, k.next(lat_ready, QL + KVL))
                wv = arrived(("vb", l)).rearrange("p a b -> p (a b)").rearrange("p (k n) -> p k n", k=KVL)
                for t in range(TA):
                    product(("vb", l, t), slice(0, 512),
                            [(col(LAT[:, QL + j, :], t), wv[:, j, :]) for j in range(KVL)])
                attend("B")
                branch(1)
                for f in range(4):
                    for name in ("cc", "uc", "bc", "zc"):
                        for c in xc:
                            linear((name, l, f, c), (name, l, f), HTs, xcols(c))
                merge(2)
                pe.wait_ge(gated, k.next(gated, 8))
                for f in range(8):
                    for c in xc:
                        linear((("wo", l), f, c), (("wo", l), f), lambda j: M4[:, j, :], xcols(c))
                sum_squares([(("post", l, c), xcols(c)) for c in xc], lambda j: M4[:, j, :], KD)

        @block.scalar
        def _(act):
            k = Counts(act, plan)
            dma = act.dma_start
            dma(vec[:, :], d["vec"][:, :]).then_inc(small_loaded, 16)
            dma(XT[:, :, 0:T], d["x"][:, :, :]).then_inc(x_loaded, 16)
            at = 0
            for name, w in CONSTS:
                dma(consts[name][:, :], d["consts"][:, at:at + w]).then_inc(small_loaded, 16)
                at += w
            dma(tab[:, 0:3072], d["tab1"][:, :]).then_inc(tab_loaded, 16)
            for dst, src in ((bs, "bs"), (ws.rearrange("p g t -> p (g t)"), "ws"), (lng[:, 0, :], "lng"), (lnb[:, 0, :], "lnb")):
                dma(dst, d[src][:, :]).then_inc(sgu_loaded, 16)
            dma(XT[:, :, T:A], d["ctx"][:, :, :]).then_inc(ctx_loaded, 16)
            act.wait_ge(small_loaded, k.at(small_loaded, 16 * (1 + len(CONSTS))))
            act.activation(cs[:, :, :].rearrange("p a b -> p (a b)"), V("c3", 0, 24), ACT.Silu).then_inc(cs_ready, k.inc(cs_ready))

            def out_of(key, dst, src_cols, func=ACT.Copy, rows=P, r0=0, **kw):
                act.wait_ge(filled, k.filling(filled, key))
                j = plan.by_key[key]
                assert j.owner == "A" and k.made.get(act_read.name, 0) == j.rank or k.turn is not None, key
                src = src_cols(bank[j.bank]) if callable(src_cols) else bank[j.bank][r0:r0 + rows, src_cols]
                act.activation(dst, src, func, **kw).then_inc(act_read, k.inc(act_read))

            def squares(src, dst, n, w, cols=None):
                for j in range(n):
                    act.activation(dst(j), src(j), ACT.Square).then_inc(sq_ready, k.inc(sq_ready))

            def root(key, dst, cols, n):
                out_of(key, dst, cols, ACT.Sqrt, scale=1.0 / n, bias=epsc[:, 0:1])

            def shift(scale, bias, cols):
                for j in range(KD):
                    act.wait_ge(xr_ready, k.next(xr_ready))
                    for n, c in enumerate(cols):
                        ins = act.activation(HT[:, j, xcols(c)], HT[:, j, xcols(c)], ACT.Identity,
                                             scale=scale(c, j), bias=bias(c, j))
                        ins.then_inc(sem := (h_ready if n == len(cols) - 1 else act_step), k.inc(sem))

            act.wait_ge(x_loaded, k.at(x_loaded, 16))
            act.wait_ge(mod_ready, k.next(mod_ready))
            squares(lambda j: XT[:, j, 0:T], lambda j: HT[:, j, 0:T], KD, T)
            root(("norm1", "x"), rt[:, 0:T], slice(0, T), D)
            shift(lambda c, j: scl1[:, j:j + 1], lambda c, j: mod[:, j, 0:1], ("x",))
            for f in range(8):
                if f >= 3:
                    act.wait_ge(dve_read, k.reading(dve_read, ("qkp", f - 3)))
                out_of(("qk", f), R1[:, f % 3, :], slice(0, T), scale=1.0 if f < 4 else RET_DK ** -0.5)
            for half in range(2):
                for t in range(TX):
                    out_of(("v", half, t), Vr[:, t, half * 512:(half + 1) * 512], slice(0, 512))
            for h in range(RET_H):
                for e in range(2):
                    out_of(("y", h, e), yT1[:, 2 * h + e, :], slice(0, T))
            for half in range(2):
                for t in range(TX):
                    act.wait_ge(filled, k.filling(filled, ("s", RET_H - 1, TX - 1)))
                    out_of(("sv", half, t), SV[:, t, half * 512:(half + 1) * 512], slice(0, 512), ACT.Gelu)
            act.wait_ge(ln_row, k.next(ln_row))
            act.activation(rs[:, :], mv[:, :, 1], ACT.Sqrt, bias=epsc[:, 0:1]).then_inc(r_done, k.inc(r_done))
            for h in range(RET_H):
                for e in range(2):
                    act.wait_ge(dve_read, k.reading(dve_read, ("mean", h)))
                    act.activation(M1[:, 2 * h + e, :], yT1[:, 2 * h + e, :], ACT.Square).then_inc(ysq_ready, k.inc(ysq_ready))
            for h in range(RET_H):
                out_of(("var", h), ST[:, 0, h, :], slice(0, T), ACT.Sqrt, scale=1.0 / RET_DV, bias=epsc[:, 0:1])
            for f in range(8):
                if f >= 2:
                    act.wait_ge(g_used, k.next(g_used))
                out_of(("g_ret", f, "x"), G1[:, f % 2, :], slice(0, T), ACT.Silu)
            for f in range(8):
                act.wait_ge(filled, k.filling(filled, ("var", f // 2)))
                out_of(("gate_a", f, "x"), M1[:, f, :], slice(0, T), ACT.Sigmoid)
            for f in range(8):
                out_of(("u", f, "x"), uT[:, f, :], slice(0, T), ACT.Gelu)
            for f in range(8):
                act.wait_ge(filled, k.filling(filled, ("ret_out", 7, "x")))
                out_of(("gate_b", f, "x"), SB[:, f, :], slice(0, T), ACT.Sigmoid)
            act.wait_ge(dve_read, k.reading(dve_read, ("w_out", 7, "x")))
            act.wait_ge(filled, k.filling(filled, ("sgu_out", 7, "x")))
            squares(lambda j: XT[:, j, 0:T], lambda j: HT[:, j, 0:T], KD, T)
            root(("norm2", "x"), rt[:, 0:T], slice(0, T), D)
            dma(SUBW[:, 0, :], d["sub"][:, :]).then_inc(sub_loaded, 16)
            shift(lambda c, j: scl2[:, j:j + 1], lambda c, j: mod[:, 24 + j, 0:1], ("x",))
            for f in range(17):
                if f < 16:
                    if f >= 2:
                        act.wait_ge(filled, k.filling(filled, ("sc", f - 2)))
                    out_of(("pq", f), Q2[:, f % 2, :], slice(0, T))
                if f:
                    out_of(("sc", f - 1), S2[:, :, f - 1, :], lambda b: b[:, :].rearrange("p (t n) -> p t n", t=TX))
            dma(tab[:, 0:4 * T + 3 * P], d["tab2"][:, :]).then_inc(tab2_loaded, 16)
            def softmax(tt):
                act.wait_ge(soft_in, k.next(soft_in))
                act.activation(gg, gg, ACT.Exp).then_inc(exp_ready, k.inc(exp_ready))
            softmax(0)
            for tt in range(TX):
                for q in range(P // 4):
                    n = tt * (P // 4) + q
                    tb, sl = n // 8, (n // 8) % 2
                    if n % 8 == 0 and tb >= 2:
                        act.wait_ge(g_stored[sl], k.at(g_stored[sl], 16 * (tb // 2)))
                    out_of(("g", tt, q), Gs[:, sl, :, (n % 8) * 4:(n % 8) * 4 + 4].rearrange("p k t -> p t k"),
                           lambda b: b[:, :].rearrange("p (t n) -> p t n", t=4))
                    if n % 8 == 7:
                        act.wait_ge(*k.own())
                        dma(gates_dram[tb, :, :, :].rearrange("p k t -> p (k t)"),
                            Gs[:, sl, :, :].rearrange("p k t -> p (k t)")).then_inc(g_stored[sl], 16)
                if tt + 1 < TX:
                    softmax(tt + 1)
            for b in range(2):
                act.wait_ge(g_stored[b], k.at(g_stored[b], 16 * (NTB // 2)))

            def inner(g):
                for j in range(GROUP):
                    if g >= 2:
                        act.wait_ge(filled, k.filling(filled, ("V", g - 2, KD - 1)))
                    out_of(("U", g, j), aT[:, g % 2, j, :], slice(0, T), ACT.Gelu)
            inner(0)
            inner(1)
            for i in k.loop(15, {filled: 24, act_read: 2 * GROUP}):
                inner(2)
                inner(3)
            act.wait_ge(res_ready, k.next(res_ready))
            act.wait_ge(filled, k.filling(filled, ("U", GROUPS - 1, GROUP - 1)))
            squares(lambda j: XT[:, j, 0:T], lambda j: HT[:, j, 0:T], KD, T)
            root(("final", "x"), rt[:, 0:T], slice(0, T), D)
            act.wait_ge(ctx_loaded, k.at(ctx_loaded, 16))

            for l in range(LAYERS):
                upd = l < LAYERS - 1
                xc = ("x", "c") if upd else ("x",)
                act.wait_ge(res_ready, k.next(res_ready))
                act.wait_ge(filled, k.filling(filled, ("final", "x") if l == 0 else ("gate", 2, l - 1, 7, "c")))
                squares(lambda j: XT[:, j, :], lambda j: HT[:, j, :], KD, A)
                for c in ("x", "c"):
                    root(("pre", l, c), rt[:, xcols(c)], slice(0, T if c == "x" else C), D)
                shift(lambda c, j: pre[:, l, 0 if c == "x" else 1, j:j + 1],
                      lambda c, j: mod[:, 48 + 24 * l + j, (1 if c == "x" else 2):(2 if c == "x" else 3)], ("x", "c"))
                for f in range(5):
                    if f >= 3:
                        act.wait_ge(dve_read, k.reading(dve_read, ("qap", l, f - 3)))
                    dst = qA[:, f, :] if f < 4 else kA[:, 0, :]
                    out_of(("qa", l, f, "x"), R4[:, f % 3, :], slice(0, T))
                    if upd or f == 4:
                        out_of(("qa", l, f, "c"), dst[:, T:A], slice(0, C))
                out_of(("va", l, "x"), vA[:, 0:TX, :], lambda b: b[:, :].rearrange("p (t n) -> p t n", t=TX))
                out_of(("va", l, "c"), vA[:, TX:TA, :], lambda b: b[:, 0:C].rearrange("p (t n) -> p t n", t=2))

                def project(h):
                    if h >= 2:
                        us = units("B", l)
                        act.wait_ge(filled, k.filling(filled, ("S", "B", l, max(n for n, u in enumerate(us) if u[0] == h - 2), 1)))
                    if h >= 3:
                        act.wait_ge(dve_read, k.reading(dve_read, ("hqp", l, h - 3)))
                    elif h == 0:
                        act.wait_ge(dve_read, k.reading(dve_read, ("krbp", l)))
                    out_of(("hq", l, h, "x"), R4[0:QKB, h % 3, :], slice(0, T), rows=QKB)
                    if upd:
                        out_of(("hq", l, h, "c"), QH[0:QKB, h % 2, T:A], slice(0, C), rows=QKB)
                    for c in ("x", "c"):
                        out_of(("hk", l, h, c), KH[0:NOPE, h % 2, xcols(c)], slice(0, T if c == "x" else C), rows=NOPE)
                    act.activation(KH[NOPE:QKB, h % 2, :], KR[NOPE:QKB, 0, :], ACT.Copy).then_inc(kr_ready, k.inc(kr_ready))

                def attend(kind):
                    us = units(kind, l)
                    n = len(us)
                    for s in range(n + 2):
                        if s < n and kind == "B" and us[s][1] == 0:
                            if us[s][0] == 0:
                                project(0)
                            if us[s][0] + 1 < HB:
                                project(us[s][0] + 1)
                        if 1 <= s <= n:
                            u = s - 1
                            _, _, lo, hi = us[u]
                            tiles = hi - lo + 2
                            if u >= 2:
                                act.wait_ge(filled, k.filling(filled, ("Y", kind, l, u - 2)))
                            for part in range(2):
                                t0, t1 = 4 * part, min(tiles, 4 * part + 4)
                                if t1 > t0:
                                    out_of(("T", kind, l, u, part),
                                           PT[:, u % 2, t0:t1, :].rearrange("p a b -> p (a b)"), slice(0, (t1 - t0) * P))
                        if s < n:
                            h, qb, lo, hi = us[s]
                            W = (hi - lo) * P + C
                            m = s % 4
                            act.wait_ge(row_ready, k.next(row_ready))
                            if kind == "A":
                                act.activation(es[:, m:m + 1], V("sink", l * 8 + h), ACT.Exp,
                                                      bias=nm[:, m:m + 1]).then_inc(act_step, k.inc(act_step))
                            act.activation(Srow[:, s % 3, 0:W], Srow[:, s % 3, 0:W], ACT.Exp,
                                                  bias=nm[:, m:m + 1], accum_out=sm[:, m:m + 1]).then_inc(p_ready, k.inc(p_ready))

                def branch(b):
                    for f in range(4):
                        if b == 1 and f == 0:
                            act.wait_ge(filled, k.filling(filled, ("hk", l, HB - 1, "c")))
                            act.wait_ge(filled, k.filling(filled, ("vb", l, TA - 1)))
                        for c in xc:
                            out_of((("z", b, l), f, c), YT[b][:, f, xcols(c)], slice(0, T if c == "x" else C), ACT.Silu)
                    merge(b)

                def merge(b):
                    if b == 1:
                        act.wait_ge(filled, k.filling(filled, ("S", "B", l, len(units("B", l)) - 1, 1)))
                    for f in range(8):
                        if f >= 2:
                            act.wait_ge(dve_read, k.reading(dve_read, ("br", b, l, f - 2, xc[-1])))
                        for c in xc:
                            out_of(("gate", b, l, f, c), SG[b][:, f % 2, xcols(c)], slice(0, T if c == "x" else C),
                                   ACT.Sigmoid)

                attend("A")
                branch(0)
                act.wait_ge(dve_read, k.reading(dve_read, ("br", 0, l, 7, xc[-1])))
                for f in range(QL):
                    for c in xc:
                        out_of((("lat", l), f, c), LAT[:, f, xcols(c)], slice(0, T if c == "x" else C))
                for f in range(KVL):
                    for c in ("x", "c"):
                        out_of((("latkv", l), f, c), LAT[:, QL + f, xcols(c)], slice(0, T if c == "x" else C))
                act.wait_ge(dve_read, k.reading(dve_read, ("qap", l, 4)))
                out_of(("krb", l, "x"), R4[0:QKB, 0, :], slice(0, T), rows=QKB)
                out_of(("krb", l, "c"), KR[0:QKB, 0, T:A], slice(0, C), rows=QKB)
                act.wait_ge(*k.own())
                for j in range(QL + KVL):
                    w = A if upd or j >= QL else T
                    act.activation(lat_sq(j)[:, 0:w], LAT[:, j, 0:w], ACT.Square).then_inc(sq_ready, k.inc(sq_ready))
                for c in xc:
                    root(("qn", l, c), rt[:, xcols(c)], slice(0, T if c == "x" else C), QL * P)
                for c in ("x", "c"):
                    root(("kvn", l, c), rk[:, xcols(c)], slice(0, T if c == "x" else C), KVL * P)
                for t in range(TA):
                    out_of(("vb", l, t), vB[:, t, :], slice(0, 512))
                act.wait_ge(dve_read, k.reading(dve_read, ("krbp", l)))
                attend("B")
                branch(1)
                act.wait_ge(dve_read, k.reading(dve_read, ("br", 1, l, 7, xc[-1])))
                for f in range(4):
                    if f >= 2:
                        act.wait_ge(c_ready, k.at(c_ready, 4 * l + f - 1))
                    for c in xc:
                        out_of(("cc", l, f, c), C1[:, f % 2, xcols(c)], slice(0, T if c == "x" else C))
                    for c in xc:
                        out_of(("zc", l, f, c), C2[:, f % 2, xcols(c)], slice(0, T if c == "x" else C), ACT.Silu)
                act.wait_ge(c_ready, k.at(c_ready, 4 * l + 4))
                merge(2)
                for f in range(8):
                    act.wait_ge(filled, k.filling(filled, ("gate", 2, l, 7, xc[-1])))
                    for c in xc:
                        out_of((("wo", l), f, c), HT[:, f, xcols(c)], slice(0, T if c == "x" else C))
                act.wait_ge(filled, k.filling(filled, (("wo", l), 7, xc[-1])))
                act.wait_ge(*k.own())
                w = A if upd else T
                squares(lambda j: HT[:, j, 0:w], lambda j: M4[:, j, 0:w], KD, w)
                for c in xc:
                    root(("post", l, c), rt[:, xcols(c)], slice(0, T if c == "x" else C), D)
            act.wait_ge(res_ready, k.next(res_ready))
            dma(out[:, :, :], XT[:, :, 0:T]).then_inc(out_done, 16)
            act.wait_ge(out_done, 16)

        @block.vector
        def _(dve):
            k = Counts(dve, plan)
            v = nc.vector

            def bank_of(key):
                dve.wait_ge(filled, k.filling(filled, key))
                j = plan.by_key[key]
                assert j.owner == "V" and (k.made.get(dve_read.name, 0) == j.rank or k.turn is not None), (key, j.rank, k.made)
                return bank[j.bank]

            v.memset(ones[:, :], 1.0).then_inc(dve_step, k.inc(dve_step))
            v.memset(epsc[:, :], EPS).then_inc(dve_step, k.inc(dve_step))
            dve.wait_ge(small_loaded, k.at(small_loaded, 16 * (1 + len(CONSTS))))

            def modulation(f, dst, bias):
                v.tensor_scalar(dst, bank_of(("mod", f))[:, 0:3], bias, None, ALU.add).then_inc(dve_read, k.inc(dve_read))
            for f in range(RING):
                modulation(f, mod[:, f, :], V("bias", f))
            for i in k.loop(11, {filled: RING, dve_read: RING}):
                for s in range(RING):
                    at = i * RING + (RING + s)
                    modulation(RING + s, mod[:, bass.ds(at, 1), :].rearrange("p a b -> p (a b)"),
                               vec[:, bass.ds(i * RING + (VEC["bias"] + RING + s), 1)])
            dve.wait_ge(*k.own())
            v1 = v.scalar_tensor_tensor
            v1(scl1[:, :], mod[:, 8:16, 0], 1.0, V("norm1", 0, 8), ALU.add, ALU.mult).then_inc(dve_step, k.inc(dve_step))
            v1(scl2[:, :], mod[:, 32:40, 0], 1.0, V("norm2", 0, 8), ALU.add, ALU.mult).then_inc(dve_step, k.inc(dve_step))
            for l in range(LAYERS):
                for c in range(2):
                    b0 = 48 + 24 * l
                    v1(pre[:, l, c, :], mod[:, b0 + 8:b0 + 16, 1 + c], 1.0, V(f"pre{l}", 0, 8), ALU.add, ALU.mult).then_inc(dve_step, k.inc(dve_step))
                    v.tensor_tensor(post[:, l, c, :], mod[:, b0 + 16:b0 + 24, 1 + c], V(f"post{l}", 0, 8), ALU.mult).then_inc(dve_step, k.inc(dve_step))
            v.memset(mx[:, :], 0.0).then_inc(mod_ready, k.inc(mod_ready))

            def normed(keys, w):
                for key in keys:
                    dve.wait_ge(act_read, k.reading(act_read, key))
                v.reciprocal(rt[:, 0:w], rt[:, 0:w]).then_inc(dve_step, k.inc(dve_step))
                dve.wait_ge(*k.own())
                for j in range(KD):
                    v.tensor_tensor(HT[:, j, 0:w], XT[:, j, 0:w], rt[:, 0:w], ALU.mult).then_inc(xr_ready, k.inc(xr_ready))

            normed([("norm1", "x")], T)
            dve.wait_ge(tab_loaded, k.at(tab_loaded, 16))
            for f in range(8):
                dst = qT[:, f, :] if f < 4 else kT[:, f - 4, :]
                dve.wait_ge(act_read, k.reading(act_read, ("qk", f)))
                v.tensor_tensor(dst, R1[:, f % 3, :], cosR, ALU.mult).then_inc(dve_step, k.inc(dve_step))
                b = bank_of(("qkp", f))
                v.tensor_tensor(G1[:, f % 2, :], b[:, :], sinR, ALU.mult).then_inc(dve_read, k.inc(dve_read))
                dve.wait_ge(*k.own())
                v.tensor_tensor(dst, dst, G1[:, f % 2, :], ALU.add).then_inc(sem := (keys_ready if f == 7 else dve_step), k.inc(sem))
            for h in range(RET_H):
                for jt in range(TX):
                    if h >= 2:
                        dve.wait_ge(filled, k.filling(filled, ("y", h - 2, 1)))
                    b = bank_of(("s", h, jt))
                    v.tensor_tensor(ST[:, h % 2, jt, jt * P:T], b[:, 0:T - jt * P], decay[:, h, 0:T - jt * P],
                                         ALU.mult).then_inc(dve_read, k.inc(dve_read))
            for t in range(TX):
                for half in range(2):
                    dve.wait_ge(act_read, k.reading(act_read, ("sv", 1, t)))
                    v.bn_stats(stats[:, t, half, :], SV[:, t, half * 512:(half + 1) * 512]).then_inc(dve_step, k.inc(dve_step))
            dve.wait_ge(*k.own())
            for t in range(TX):
                ins = v.bn_aggr(mv[:, t, :], stats[:, t, :, :].rearrange("p a b -> p (a b)"))
                ins.then_inc(sem := (ln_row if t == TX - 1 else dve_step), k.inc(sem))
            for h in range(RET_H):
                b = bank_of(("mean", h))
                v.scalar_tensor_tensor(yT1[:, 2 * h, :], b[:, :], -1.0 / RET_DV, yT1[:, 2 * h, :], ALU.mult, ALU.add).then_inc(dve_step, k.inc(dve_step))
                v.scalar_tensor_tensor(yT1[:, 2 * h + 1, :], b[:, :], -1.0 / RET_DV, yT1[:, 2 * h + 1, :],
                                            ALU.mult, ALU.add).then_inc(dve_read, k.inc(dve_read))
                dve.wait_ge(*k.own())
            dve.wait_ge(r_done, k.next(r_done))
            v.reciprocal(rs[:, :], rs[:, :]).then_inc(dve_step, k.inc(dve_step))
            dve.wait_ge(sgu_loaded, k.at(sgu_loaded, 64))
            dve.wait_ge(*k.own())
            for t in range(TX):
                v.tensor_scalar(SV[:, t, :], SV[:, t, :], mv[:, t, 0:1], rs[:, t:t + 1], ALU.subtract, ALU.mult).then_inc(dve_step, k.inc(dve_step))
            dve.wait_ge(*k.own())
            for t in range(TX):
                v.tensor_tensor(SV[:, t, :], SV[:, t, :], lng[:, 0, :], ALU.mult).then_inc(dve_step, k.inc(dve_step))
            dve.wait_ge(*k.own())
            for t in range(TX):
                v.tensor_tensor(SV[:, t, :], SV[:, t, :], lnb[:, 0, :], ALU.add).then_inc(vn_ready, k.inc(vn_ready))
            for h in range(RET_H):
                dve.wait_ge(act_read, k.reading(act_read, ("var", h)))
                v.reciprocal(ST[:, 0, h, :], ST[:, 0, h, :]).then_inc(dve_step, k.inc(dve_step))
            dve.wait_ge(*k.own())
            for f in range(8):
                v.scalar_tensor_tensor(yT1[:, f, :], yT1[:, f, :], V("retg", f), ST[:, 0, f // 2, :],
                                            ALU.mult, ALU.mult).then_inc(dve_step, k.inc(dve_step))
            dve.wait_ge(*k.own())
            for f in range(8):
                dve.wait_ge(act_read, k.reading(act_read, ("g_ret", f, "x")))
                v.tensor_tensor(yT1[:, f, :], yT1[:, f, :], G1[:, f % 2, :], ALU.mult).then_inc(g_used, k.inc(g_used))
            dve.wait_ge(*k.own())
            for f in range(8):
                dve.wait_ge(act_read, k.reading(act_read, ("gate_a", f, "x")))
                v.tensor_tensor(M1[:, f, :], bank_of(("ret_out", f, "x"))[:, :], M1[:, f, :], ALU.mult).then_inc(dve_read, k.inc(dve_read))
            for f in range(8):
                b = bank_of(("mix", f))
                g0 = (f // 2) * P
                v.tensor_tensor(ST[:, 1, f % 4, :].rearrange("p (n t) -> p n t", n=TX),
                                     b[:, :].rearrange("p (n t) -> p n t", n=TX),
                                     bs[:, g0:g0 + P].unsqueeze(1).to_broadcast([P, TX, P]), ALU.add).then_inc(dve_read, k.inc(dve_read))
                dve.wait_ge(*k.own())
                dve.wait_ge(act_read, k.reading(act_read, ("u", f, "x")))
                v.tensor_tensor(uT[:, f, :], uT[:, f, :], ST[:, 1, f % 4, :], ALU.mult).then_inc(ug_ready, k.inc(ug_ready))
            for f in range(8):
                dve.wait_ge(act_read, k.reading(act_read, ("gate_b", f, "x")))
                v.tensor_tensor(SB[:, f, :], bank_of(("sgu_out", f, "x"))[:, :], SB[:, f, :], ALU.mult).then_inc(dve_read, k.inc(dve_read))
                dve.wait_ge(*k.own())
                v.tensor_tensor(M1[:, f, :], M1[:, f, :], SB[:, f, :], ALU.add).then_inc(gated, k.inc(gated))
            for f in range(8):
                b = bank_of(("w_out", f, "x"))
                v.scalar_tensor_tensor(XT[:, f, 0:T], b[:, :], mod[:, 16 + f, 0:1], XT[:, f, 0:T],
                                            ALU.mult, ALU.add).then_inc(dve_read, k.inc(dve_read))

            normed([("norm2", "x")], T)
            dve.wait_ge(act_read, k.reading(act_read, ("sc", 15)))

            def choose(tt):
                for i in range(16):
                    v.max(top[:, i, 0:8], S2[:, tt, i, :]).then_inc(dve_step, k.inc(dve_step))
                dve.wait_ge(*k.own())
                for i in range(16):
                    v.max_index(topi[:, i, 0:8].bitcast(u32), top[:, i, 0:8], S2[:, tt, i, :]).then_inc(dve_step, k.inc(dve_step))
                    v.match_replace(Rw[:, i, :], top[:, i, 0:8], S2[:, tt, i, :], NEG).then_inc(dve_step, k.inc(dve_step))
                dve.wait_ge(*k.own())
                for i in range(16):
                    v.max(top[:, i, 8:16], Rw[:, i, :]).then_inc(dve_step, k.inc(dve_step))
                dve.wait_ge(*k.own())
                for i in range(16):
                    v.max_index(topi[:, i, 8:16].bitcast(u32), top[:, i, 8:16], Rw[:, i, :]).then_inc(dve_step, k.inc(dve_step))
                dve.wait_ge(*k.own())
                v.tensor_copy(topf, topi.bitcast(u32)).then_inc(dve_step, k.inc(dve_step))
                halves = top.rearrange("p (h s) k -> p h s k", s=2)
                dve.wait_ge(*k.own())
                for h in range(PH):
                    v.tensor_tensor(cand[:, h, :].rearrange("p (a b) -> p a b", a=PK),
                                         halves[:, h, 0, :].unsqueeze(2).to_broadcast([P, PK, PK]),
                                         halves[:, h, 1, :].unsqueeze(1).to_broadcast([P, PK, PK]), ALU.add).then_inc(dve_step, k.inc(dve_step))
                dve.wait_ge(*k.own())
                rest = Rw.rearrange("p a b -> p (a b)").rearrange("p (h n) -> p h n", h=PH)
                for h in range(PH):
                    v.max(cv[:, h, 0:8], cand[:, h, :]).then_inc(dve_step, k.inc(dve_step))
                dve.wait_ge(*k.own())
                for h in range(PH):
                    v.max_index(cpos[:, h, 0:8].bitcast(u32), cv[:, h, 0:8], cand[:, h, :]).then_inc(dve_step, k.inc(dve_step))
                    v.match_replace(rest[:, h, :], cv[:, h, 0:8], cand[:, h, :], NEG).then_inc(dve_step, k.inc(dve_step))
                dve.wait_ge(*k.own())
                for h in range(PH):
                    v.max(cv[:, h, 8:16], rest[:, h, :]).then_inc(dve_step, k.inc(dve_step))
                dve.wait_ge(*k.own())
                for h in range(PH):
                    v.max_index(cpos[:, h, 8:16].bitcast(u32), cv[:, h, 8:16], rest[:, h, :]).then_inc(dve_step, k.inc(dve_step))
                if tt:
                    dve.wait_ge(filled, k.filling(filled, ("kt", tt - 1)))
                v.tensor_tensor(gg, cv, cv[:, :, 0:1].to_broadcast([P, PH, PK]), ALU.subtract).then_inc(dve_step, k.inc(dve_step))
                dve.wait_ge(*k.own())
                v.tensor_scalar(cpa.bitcast(u32), cpos.bitcast(u32), 4, None, ALU.logical_shift_right).then_inc(soft_in, k.inc(soft_in))
                v.tensor_scalar(cpos.bitcast(u32), cpos.bitcast(u32), 15, None, ALU.bitwise_and).then_inc(dve_step, k.inc(dve_step))
                dve.wait_ge(*k.own())
                v.tensor_copy(ca, cpa.bitcast(u32)).then_inc(dve_step, k.inc(dve_step))
                v.tensor_copy(cb, cpos.bitcast(u32)).then_inc(dve_step, k.inc(dve_step))
                dve.wait_ge(*k.own())
                tf = topf.rearrange("p (h s) k -> p h s k", s=2)
                work = Rw.rearrange("p a b -> p (a b)").rearrange("p (j a) -> p j a", a=PK)
                for s, pos, dst in ((0, ca, kk1), (1, cb, kk2)):
                    v.tensor_tensor(work, consts["iota16"][:, :].unsqueeze(1).to_broadcast([P, PH * PK, PK]),
                                         pos.rearrange("p h j -> p (h j)").unsqueeze(2).to_broadcast([P, PH * PK, PK]),
                                         ALU.is_equal).then_inc(dve_step, k.inc(dve_step))
                    dve.wait_ge(*k.own())
                    for h in range(PH):
                        v.tensor_tensor(work[:, h * PK:(h + 1) * PK, :], work[:, h * PK:(h + 1) * PK, :],
                                             tf[:, h, s, :].unsqueeze(1).to_broadcast([P, PK, PK]), ALU.mult).then_inc(dve_step, k.inc(dve_step))
                    dve.wait_ge(*k.own())
                    v.tensor_reduce(dst.rearrange("p h j -> p (h j)"), work, AX, ALU.add).then_inc(dve_step, k.inc(dve_step))
                    dve.wait_ge(*k.own())
                dve.wait_ge(exp_ready, k.next(exp_ready))
                v.tensor_reduce(gsum[:, 0, 0:8], gg, AX, ALU.add).then_inc(dve_step, k.inc(dve_step))
                dve.wait_ge(*k.own())
                v.reciprocal(gsum[:, 0, 8:16], gsum[:, 0, 0:8]).then_inc(dve_step, k.inc(dve_step))
                dve.wait_ge(*k.own())
                v.tensor_tensor(gg, gg, gsum[:, 0, 8:16].unsqueeze(2).to_broadcast([P, PH, PK]), ALU.mult).then_inc(kt_ready, k.inc(kt_ready))

            for tt in range(TX):
                choose(tt)
                if tt >= 2:
                    dve.wait_ge(filled, k.filling(filled, ("g", tt - 2, 31)))
                b = bank_of(("kt", tt))
                v.tensor_copy(KT[:, tt % 2, :, :].rearrange("p a b -> p (a b)"), b[:, 0:3 * P]).then_inc(dve_read, k.inc(dve_read))
                dve.wait_ge(*k.own())
                for q in range(P // 4):
                    n = tt * (P // 4) + q
                    if n >= 2:
                        dve.wait_ge(filled, k.filling(filled, ("g", (n - 2) // 32, (n - 2) % 32)))
                    for t in range(4):
                        c = 4 * q + t
                        v.tensor_scalar(hotA[:, n % 2, t, :], consts["iota128"][:, :],
                                               KT[:, tt % 2, 0, c:c + 1], KT[:, tt % 2, 2, c:c + 1],
                                               ALU.is_equal, ALU.mult).then_inc(hot_a, k.inc(hot_a))
            dve.wait_ge(act_read, k.reading(act_read, ("g", TX - 1, 31)))
            for b in range(2):
                dve.wait_ge(g_stored[b], k.at(g_stored[b], 16 * (NTB // 2)))
            v.memset(ACC.rearrange("p a b -> p (a b)"), 0.0).then_inc(dve_step, k.inc(dve_step))
            dve.wait_ge(*k.own())

            def gate_group(g, n_loaded):
                dve.wait_ge(g_loaded[g % 2], k.at(g_loaded[g % 2], n_loaded))
                for j in range(GROUP):
                    dve.wait_ge(act_read, k.reading(act_read, ("U", g, j)))
                    at_ = aT[:, g % 2, j, :].rearrange("p (n t) -> p n t", n=NTB)
                    v.tensor_tensor(at_, at_, Gt[g % 2][:, :, j, :], ALU.mult).then_inc(a_ready, k.inc(a_ready))

            def add_up(g):
                for dd in range(KD):
                    b = bank_of(("V", g, dd))
                    if dd == 0:
                        dve.wait_ge(*k.own())
                    v.tensor_tensor(ACC[:, dd, :], b[:, :], ACC[:, dd, :], ALU.add).then_inc(dve_read, k.inc(dve_read))
            gate_group(0, 16)
            gate_group(1, 16)
            add_up(0)
            for i in k.loop(15, {filled: 24, act_read: 2 * GROUP, dve_read: 2 * KD, a_ready: 2 * GROUP,
                                    g_loaded[0]: 16, g_loaded[1]: 16}):
                gate_group(2, 32)
                add_up(1)
                gate_group(3, 32)
                add_up(2)
            add_up(GROUPS - 1)
            dve.wait_ge(*k.own())
            for f in range(8):
                v.scalar_tensor_tensor(XT[:, f, 0:T], ACC[:, f, :], mod[:, 40 + f, 0:1], XT[:, f, 0:T],
                                              ALU.mult, ALU.add).then_inc(sem := (res_ready if f == 7 else dve_step), k.inc(sem))
            dve.wait_ge(*k.own())
            dve.wait_ge(act_read, k.reading(act_read, ("final", "x")))
            v.reciprocal(rt[:, 0:T], rt[:, 0:T]).then_inc(dve_step, k.inc(dve_step))
            dve.wait_ge(*k.own())
            for f in range(8):
                v.scalar_tensor_tensor(XT[:, f, 0:T], XT[:, f, 0:T], V("final", f), rt[:, 0:T],
                                              ALU.mult, ALU.mult).then_inc(sem := (res_ready if f == 7 else dve_step), k.inc(sem))
            dve.wait_ge(*k.own())

            dve.wait_ge(tab2_loaded, k.at(tab2_loaded, 16))
            dve.wait_ge(ctx_loaded, k.at(ctx_loaded, 16))
            for l in range(LAYERS):
                upd = l < LAYERS - 1
                xc = ("x", "c") if upd else ("x",)
                w = A if upd else T
                normed([("pre", l, "x"), ("pre", l, "c")], A)
                for f in range(5):
                    dst = qA[:, f, :] if f < 4 else kA[:, 0, :]
                    dve.wait_ge(act_read, k.reading(act_read, ("qa", l, f, "x")))
                    v.tensor_tensor(dst[:, 0:T], R4[:, f % 3, :], cosA, ALU.mult).then_inc(dve_step, k.inc(dve_step))
                    v.tensor_tensor(SGA[:, f % 2, 0:T], bank_of(("qap", l, f))[:, :], sinA, ALU.mult).then_inc(dve_read, k.inc(dve_read))
                    dve.wait_ge(*k.own())
                    if f == 4:
                        dve.wait_ge(act_read, k.reading(act_read, ("va", l, "c")))
                    v.tensor_tensor(dst[:, 0:T], dst[:, 0:T], SGA[:, f % 2, 0:T], ALU.add).then_inc(sem := (qk_ready if f == 4 else dve_step), k.inc(sem))

                def project(h):
                    dve.wait_ge(act_read, k.reading(act_read, ("hq", l, h, "x")))
                    if h >= 2:
                        us = units("B", l)
                        dve.wait_ge(filled, k.filling(filled, ("S", "B", l, max(n for n, u in enumerate(us) if u[0] == h - 2), 1)))
                    t_ = rt if h % 2 else rk
                    v.tensor_tensor(QH[0:QKB, h % 2, 0:T], R4[0:QKB, h % 3, :], cosB[0:QKB, :], ALU.mult).then_inc(dve_step, k.inc(dve_step))
                    v.tensor_tensor(t_[0:QKB, 0:T], bank_of(("hqp", l, h))[0:QKB, :], sinB[0:QKB, :], ALU.mult).then_inc(dve_read, k.inc(dve_read))
                    dve.wait_ge(*k.own())
                    dve.wait_ge(kr_ready, k.next(kr_ready))
                    v.tensor_tensor(QH[0:QKB, h % 2, 0:T], QH[0:QKB, h % 2, 0:T], t_[0:QKB, 0:T], ALU.add).then_inc(qk_ready, k.inc(qk_ready))

                def attend(kind):
                    us = units(kind, l)
                    n = len(us)
                    scale = HDA ** -0.5 if kind == "A" else QKB ** -0.5
                    for s in range(n + 2):
                        if s < n and kind == "B" and us[s][1] == 0:
                            if us[s][0] == 0:
                                project(0)
                            if us[s][0] + 1 < HB:
                                project(us[s][0] + 1)
                        if s < n:
                            h, qb, lo, hi = us[s]
                            nl = (hi - lo) * P
                            W = nl + C
                            m = s % 4
                            row = Srow[:, s % 3, :]
                            if s >= 3:
                                dve.wait_ge(filled, k.filling(filled, ("T", kind, l, s - 3, 1 if us[s - 3][3] - us[s - 3][2] > 2 else 0)))
                            if nl:
                                b = bank_of(("S", kind, l, s, 0))
                                if kind == "A":
                                    m0 = (lo - qb + 1) * P
                                    v.scalar_tensor_tensor(row[:, 0:nl], b[:, 0:nl], scale, band[:, m0:m0 + nl],
                                                                ALU.mult, ALU.add).then_inc(dve_read, k.inc(dve_read))
                                else:
                                    v.tensor_scalar(row[:, 0:nl], b[:, 0:nl], scale, None, ALU.mult).then_inc(dve_read, k.inc(dve_read))
                            b = bank_of(("S", kind, l, s, 1))
                            v.tensor_scalar(row[:, nl:W], b[:, 0:C], scale, None, ALU.mult).then_inc(dve_read, k.inc(dve_read))
                            dve.wait_ge(*k.own())
                            v.reduce_max(mx[:, m:m + 1], row[:, 0:W], AX).then_inc(dve_step, k.inc(dve_step))
                            dve.wait_ge(*k.own())
                            if kind == "A":
                                v.tensor_scalar(nm[:, m:m + 1], mx[:, m:m + 1], V("sink", l * 8 + h), -1.0,
                                                       ALU.max, ALU.mult).then_inc(row_ready, k.inc(row_ready))
                            else:
                                v.tensor_scalar(nm[:, m:m + 1], mx[:, m:m + 1], -1.0, None, ALU.mult).then_inc(row_ready, k.inc(row_ready))
                        if s >= 2:
                            u = s - 2
                            h, qb, lo, hi = us[u]
                            m = u % 4
                            dve.wait_ge(p_ready, k.next(p_ready))
                            if kind == "A":
                                v.tensor_tensor(sm[:, m:m + 1], sm[:, m:m + 1], es[:, m:m + 1], ALU.add).then_inc(dve_step, k.inc(dve_step))
                                dve.wait_ge(*k.own())
                            v.reciprocal(ri[:, m:m + 1], sm[:, m:m + 1]).then_inc(dve_step, k.inc(dve_step))
                            dve.wait_ge(*k.own())
                            b = bank_of(("Y", kind, l, u))
                            v.tensor_scalar(Y4[:, qb, h * 64:(h + 1) * 64], b[:, 0:64], ri[:, m:m + 1], None,
                                                 ALU.mult).then_inc(dve_read, k.inc(dve_read))

                def merge(b):
                    for f in range(8):
                        for c in xc:
                            n_ = T if c == "x" else C
                            dve.wait_ge(act_read, k.reading(act_read, ("gate", b, l, f, c)))
                            s_ = SG[b][:, f % 2, xcols(c)]
                            p_ = bank_of(("br", b, l, f, c))[:, 0:n_]
                            m_ = M4[:, f, xcols(c)]
                            if b == 0:
                                v.tensor_tensor(m_, p_, s_, ALU.mult).then_inc(dve_read, k.inc(dve_read))
                            else:
                                t_ = rt[:, xcols(c)] if f % 2 else rk[:, xcols(c)]
                                v.tensor_tensor(t_, p_, s_, ALU.mult).then_inc(dve_read, k.inc(dve_read))
                                dve.wait_ge(*k.own())
                                last = b == 2 and c == xc[-1]
                                v.tensor_tensor(m_, m_, t_, ALU.add).then_inc(sem := (gated if last else dve_step), k.inc(sem))

                def branch(b):
                    for f in range(4):
                        for c in xc:
                            n_ = T if c == "x" else C
                            dve.wait_ge(act_read, k.reading(act_read, (("z", b, l), f, c)))
                            v.tensor_tensor(YT[b][:, f, xcols(c)], bank_of(("yt", b, l, f, c))[:, 0:n_],
                                                 YT[b][:, f, xcols(c)], ALU.mult).then_inc(dve_read, k.inc(dve_read))
                    merge(b)

                attend("A")
                branch(0)
                dve.wait_ge(act_read, k.reading(act_read, ("krb", l, "c")))
                v.tensor_tensor(KR[0:QKB, 0, 0:T], R4[0:QKB, 0, :], cosB[0:QKB, :], ALU.mult).then_inc(dve_step, k.inc(dve_step))
                b = bank_of(("krbp", l))
                v.tensor_tensor(QH[0:QKB, 0, 0:T], b[0:QKB, :], sinB[0:QKB, :], ALU.mult).then_inc(dve_step, k.inc(dve_step))
                dve.wait_ge(*k.own())
                v.tensor_tensor(KR[0:QKB, 0, 0:T], KR[0:QKB, 0, 0:T], QH[0:QKB, 0, 0:T], ALU.add).then_inc(dve_read, k.inc(dve_read))
                for c in xc:
                    dve.wait_ge(act_read, k.reading(act_read, ("qn", l, c)))
                v.reciprocal(rt[:, 0:w], rt[:, 0:w]).then_inc(dve_step, k.inc(dve_step))
                for c in ("x", "c"):
                    dve.wait_ge(act_read, k.reading(act_read, ("kvn", l, c)))
                v.reciprocal(rk[:, :], rk[:, :]).then_inc(dve_step, k.inc(dve_step))
                dve.wait_ge(*k.own())
                for j in range(QL + KVL):
                    r_, w_, g_ = (rt, w, V(f"qa{l}", j)) if j < QL else (rk, A, V(f"kva{l}", j - QL))
                    v.scalar_tensor_tensor(LAT[:, j, 0:w_], LAT[:, j, 0:w_], g_, r_[:, 0:w_],
                                                  ALU.mult, ALU.mult).then_inc(lat_ready, k.inc(lat_ready))
                attend("B")
                branch(1)
                dve.wait_ge(filled, k.filling(filled, ("br", 1, l, 7, xc[-1])))
                for f in range(4):
                    z, y = ZP[:, f % 2, :], yTC[:, f, :]
                    if f < 2:
                        v.memset(z, 0.0).then_inc(dve_step, k.inc(dve_step))
                        dve.wait_ge(*k.own())
                    spans = [("x", 1, T)] + ([("c", T + 3, C)] if upd else [])
                    for c, z0, n_ in spans:
                        dve.wait_ge(act_read, k.reading(act_read, ("cc", l, f, c)))
                        v.tensor_tensor(z[:, z0:z0 + n_], bank_of(("uc", l, f, c))[:, 0:n_],
                                             C1[:, f % 2, xcols(c)], ALU.mult).then_inc(dve_read, k.inc(dve_read))
                    dve.wait_ge(*k.own())
                    for tap in range(3):
                        wcol = V(f"conv{l}", tap * 4 + f)
                        for c, z0, n_ in spans:
                            src = z[:, z0 - 1 + tap:z0 - 1 + tap + n_]
                            if tap == 0:
                                v.tensor_scalar(y[:, xcols(c)], src, wcol, None, ALU.mult).then_inc(dve_step, k.inc(dve_step))
                            else:
                                v.scalar_tensor_tensor(y[:, xcols(c)], src, wcol, y[:, xcols(c)], ALU.mult, ALU.add).then_inc(dve_step, k.inc(dve_step))
                        dve.wait_ge(*k.own())
                    for c, _, n_ in spans:
                        v.tensor_tensor(y[:, xcols(c)], y[:, xcols(c)], bank_of(("bc", l, f, c))[:, 0:n_], ALU.mult).then_inc(dve_read, k.inc(dve_read))
                    dve.wait_ge(*k.own())
                    for c, _, n_ in spans:
                        dve.wait_ge(act_read, k.reading(act_read, ("zc", l, f, c)))
                        last = c == xc[-1]
                        v.tensor_tensor(y[:, xcols(c)], y[:, xcols(c)], C2[:, f % 2, xcols(c)], ALU.mult).then_inc(sem := (c_ready if last else dve_step), k.inc(sem))
                merge(2)
                for c in xc:
                    dve.wait_ge(act_read, k.reading(act_read, ("post", l, c)))
                v.reciprocal(rt[:, 0:w], rt[:, 0:w]).then_inc(dve_step, k.inc(dve_step))
                dve.wait_ge(*k.own())
                for f in range(8):
                    for n_, c in enumerate(xc):
                        v.scalar_tensor_tensor(HT[:, f, xcols(c)], HT[:, f, xcols(c)], post[:, l, n_, f:f + 1],
                                                    rt[:, xcols(c)], ALU.mult, ALU.mult).then_inc(dve_step, k.inc(dve_step))
                dve.wait_ge(*k.own())
                for f in range(8):
                    v.tensor_tensor(XT[:, f, 0:w], XT[:, f, 0:w], HT[:, f, 0:w], ALU.add).then_inc(sem := (res_ready if f == 7 else dve_step), k.inc(sem))
                dve.wait_ge(*k.own())


def tiles_of(w):
    k, n = w.shape
    return w.reshape(k // P, P, n).transpose(1, 0, 2).reshape(P, k // P * n)


def lay_chunk(what, a):
    kind, rest = what[0], what[1:]
    if kind == "mod":
        f = rest[0]
        w = a["w_ada"][0] if f < 48 else a["w_mod_2"][(f - 48) // 24]
        f = f if f < 48 else (f - 48) % 24
        return tiles_of(w[:, f * P:(f + 1) * P])
    if kind in ("w_in", "w_ret_out", "w_sgu_out", "w_out", "peer_w_q"):
        at = rest[0] + rest[1] * P
        return tiles_of(a[kind][0][:, at:at + P])
    if kind == "in2":
        at = rest[1] + (rest[2] * P if len(rest) > 2 else 0)
        return tiles_of(a["w_in_2"][rest[0]][:, at:at + P])
    if kind == "qa":
        w, f = a["w_in_2"][rest[0]], rest[1]
        if f == 4:
            return tiles_of(w[:, IN_AT["ka"]:IN_AT["ka"] + P])
        return tiles_of(np.concatenate([w[:, h * HDA:(h + 1) * HDA] for h in (f, f + 4)], axis=1))
    if kind == "U":
        return tiles_of(a["peer_u"][0][rest[0] * P:(rest[0] + 1) * P].T)
    if kind == "V":
        return a["peer_v"][0][rest[0] * P:(rest[0] + 1) * P]
    if kind == "br":
        l, b, f = rest
        return tiles_of(a["w_branch_2"][l][b][:, f * 256:(f + 1) * 256])
    if kind == "w_o":
        return tiles_of(a["w_o_2"][rest[0]][:, rest[1] * P:(rest[1] + 1) * P])
    if kind == "krb":
        out = np.zeros((P, KD, P), np.float32)
        w = a["w_in_2"][rest[0]][:, IN_AT["krb"]:IN_AT["krb"] + ROPE]
        out[:, :, NOPE:QKB] = w.reshape(KD, P, ROPE).transpose(1, 0, 2)
        return out.reshape(P, KD * P)
    if kind == "vb":
        w = a["w_kvb_2"][rest[0]].reshape(KVL * P, HB, NOPE + VB)[:, :, NOPE:]
        return tiles_of(w.reshape(KVL * P, HB * VB))
    if kind == "hb":
        l, h = rest
        out = np.zeros((P, KD * P), np.float32)
        out[:, 0:QL * QKB] = tiles_of(a["w_qb_2"][l][:, h * QKB:(h + 1) * QKB])
        w = a["w_kvb_2"][l][:, h * (NOPE + VB):h * (NOPE + VB) + NOPE]
        out[:, QL * QKB:QL * QKB + KVL * NOPE] = tiles_of(w)
        return out
    raise ValueError(what)


def columns(v):
    return v.reshape(-1, P).T


def swap(n, half, at=0):
    m = np.zeros((P, n), np.float32)
    for b in range(at, n, 2 * half):
        for i in range(half):
            m[b + half + i, b + i] = -1.0
            m[b + i, b + half + i] = 1.0
    return m


def shape_constants():
    f = np.float32
    consts = np.concatenate([np.eye(P, dtype=f), swap(P, 64), swap(P, 32), swap(QKB, 16, NOPE),
                             np.tile(np.arange(P, dtype=f), (P, 1)), np.tile(np.arange(PK, dtype=f), (P, 1))], axis=1)
    pos = np.arange(T, dtype=f)
    inv = (f(10000.0) ** (-np.arange(64, dtype=f) * f(2.0) / f(128))).astype(f)
    ang = (pos[:, None] * inv[None, :]).astype(f)
    cos, sin = np.cos(ang).astype(f).T, np.sin(ang).astype(f).T
    gamma = 1.0 - 2.0 ** (-5.0 - np.arange(RET_H, dtype=np.float64))
    diff = np.arange(T)[None, :] - np.arange(P)[:, None]
    decay = [np.where(diff >= 0, g ** np.maximum(diff, 0), 0.0).astype(f) for g in gamma]
    tab1 = np.concatenate([np.tile(cos, (2, 1)), np.tile(sin, (2, 1))] + decay, axis=1)

    def axial(rot):
        row, c = np.repeat(np.arange(T // 64, dtype=f), 64), np.tile(np.arange(64, dtype=f), T // 64)
        ax = rot // 2
        iv = (f(10000.0) ** (-np.arange(0, ax, 2, dtype=f) / f(ax))).astype(f)
        an = np.concatenate([row[:, None] * iv, c[:, None] * iv], axis=-1).astype(f)
        return np.cos(an).astype(f).T, np.sin(an).astype(f).T
    ca, sa = axial(HDA)
    cb, sb_ = axial(ROPE)
    one, zero = np.ones((NOPE, T), f), np.zeros((NOPE, T), f)
    pad = np.zeros((P - QKB, T), f)
    i, j = np.arange(P)[:, None], np.arange(3 * P)[None, :]
    band = np.where(np.abs(j - (i + P)) <= P, 0.0, MASKED).astype(f)
    tab2 = np.concatenate([np.tile(ca, (4, 1)), np.tile(sa, (4, 1)), np.concatenate([one, cb, cb, pad]),
                           np.concatenate([zero, sb_, sb_, pad]), band], axis=1)
    return consts, tab1, tab2


def kernel(**inputs):
    import concourse.bacc as bacc
    from concourse.bass_utils import run_bass_kernel_spmd

    a = {n: np.asarray(v) for n, v in inputs.items()}
    plan = make_plan()
    weights = np.empty((len(plan.chunks), P, KD * P), np.float32)
    for n, what in enumerate(plan.chunks):
        weights[n] = lay_chunk(what, a)
    c3 = np.stack([columns(a["c"][0]), columns(a["c_2"][0]), columns(a["c_ctx_2"])], axis=2).reshape(P, 24)
    parts = [c3, columns(a["b_ada"][0]), columns(a["b_mod_2"][0]), columns(a["b_mod_2"][1]),
             columns(a["norm1_g"][0]), columns(a["ret_gn_g"][0]), columns(a["norm2_g"][0]), columns(a["final_g"]),
             np.tile(a["sink_2"].reshape(1, 16), (P, 1))]
    for l in range(LAYERS):
        parts += [columns(a["g_pre_2"][l]), columns(a["g_post_2"][l]), columns(a["g_qa_2"][l]),
                  columns(a["g_kva_2"][l]), columns(a["conv_w_2"][l].reshape(-1))]
    consts, tab1, tab2 = shape_constants()

    def spread(v):
        return np.tile(v.reshape(1, -1), (P, 1))
    arrays = {
        "weights": weights, "vec": np.concatenate(parts, axis=1), "consts": consts, "tab1": tab1, "tab2": tab2,
        "x": tiles_of(a["x"][0].T).reshape(P, KD, T), "ctx": tiles_of(a["ctx_2"][0].T).reshape(P, KD, C),
        "bs": spread(a["sgu_b"][0]), "ws": a["sgu_w"][0].transpose(2, 0, 1).reshape(P, 4 * P),
        "lng": spread(a["sgu_ln_g"][0]), "lnb": spread(a["sgu_ln_b"][0]),
        "sub": a["peer_sub_keys"][0].reshape(16, NK, P).transpose(2, 0, 1).reshape(P, 16 * NK),
    }
    nc = bacc.Bacc("TRN2", target_bir_lowering=False, num_devices=1)
    f32 = mybir.dt.float32
    arrays = {n: np.ascontiguousarray(v) for n, v in arrays.items()}
    d = {n: nc.dram_tensor(f"in_{n}", v.shape, f32, kind="ExternalInput").ap() for n, v in arrays.items()}
    out = nc.dram_tensor("out_features", (P, KD, T), f32, kind="ExternalOutput").ap()
    build(nc, plan, d, out)
    got = run_bass_kernel_spmd(nc, [{f"in_{n}": v for n, v in arrays.items()}], core_ids=[0])
    y = got.results[0]["out_features"]
    return np.ascontiguousarray(y.transpose(2, 1, 0).reshape(1, T, D))
```

```python
import numpy as np
import concourse.bass as bass
from concourse import mybir
from contextlib import ExitStack

P = 128
D = 1024
T = 512
C = 256
A = T + C
KD = D // P
TX, TA = T // P, A // P
EPS = 1e-6
RET_H, RET_DK, RET_DV = 4, 128, 256
PH, PK, NK = 8, 16, 128
NEG = -3.0e38
MASKED = -1e30
LAYERS = 2
HA, HDA, HB, NOPE, ROPE, VB = 8, 64, 8, 64, 32, 64
QKB = NOPE + ROPE
QL, KVL = 3, 2
IN_SIZES = (512, 128, 128, 512, 384, 256, 32, 512, 512, 512, 512, 512, 1024, 1024, 1024)
IN_NAMES = ("qa", "ka", "va", "za", "qlb", "kvlb", "krb", "zb", "bc", "cc", "uc", "zc", "ga", "gb", "gc")
IN_AT = dict(zip(IN_NAMES, np.concatenate([[0], np.cumsum(IN_SIZES)[:-1]]).tolist()))
GROUP = 2
GROUPS = NK // GROUP
GPT = 2
RING = 8
SLOTS = 4
LOOK = 2
MODS = (16, 24, 40, 48, 72, 96)
TILES = 24
HOTS = 4
TB = 32
NTB = T // TB

VEC = {}
_at = 0
for _name, _n in [("c3", 24), ("bias", 96), ("norm1", 8), ("retg", 8), ("norm2", 8), ("final", 8),
                  ("sink", 16), ("pre0", 8), ("post0", 8), ("qa0", 3), ("kva0", 2), ("conv0", 12),
                  ("pre1", 8), ("post1", 8), ("qa1", 3), ("kva1", 2), ("conv1", 12)]:
    VEC[_name] = _at
    _at += _n
NVEC = _at

CONSTS = [("ident", 128), ("perm128", 128), ("permA", 128), ("permB", 96), ("iota128", 128)]
TAB1 = [("cosR", T), ("sinR", T), ("decay", RET_H * T)]
TAB2 = [("cosA", T), ("sinA", T), ("cosB", T), ("sinB", T), ("band", 3 * P)]


class Job:
    pass


class Plan:

    def __init__(self):
        self.jobs, self.by_key, self.ranks = [], {}, {"A": 0, "V": 0}
        self.chunks, self.free, self.chunk_at = [], [], {}
        self.splits, self.split_at, self.split_of, self.limit = [], {}, {}, np.inf

    def chunk(self, key, what, split=True):
        n = len(self.chunks)
        self.chunk_at[key] = n
        self.chunks.append(what)
        self.free.append(None)
        if split:
            self.split_at[key] = self.split_of[n] = len(self.splits)
            self.splits.append(n)

    def job(self, key, owner, frees=()):
        j = Job()
        j.key, j.owner, j.fill, j.rank = key, owner, len(self.jobs), self.ranks[owner]
        j.bank = j.fill % RING
        j.before = self.jobs[j.fill - RING] if j.fill >= RING else None
        j.split = min(len(self.splits) - 1 + LOOK, self.limit)
        self.ranks[owner] += 1
        self.jobs.append(j)
        assert key not in self.by_key
        self.by_key[key] = j
        for c in frees:
            self.free[self.chunk_at[c]] = j.fill + 1


def units(kind, l):
    out = []
    for h in range(HA):
        for qb in range(TX):
            lo, hi = (max(qb - 1, 0), min(qb + 2, TX)) if kind == "A" else (0, TX)
            out.append((h, qb, lo, hi))
        if l == 0:
            out += [(h, TX + c, 0, 0) for c in range(C // P)]
    return out


def mod_with(tt, q):
    n = tt * (P // 4) + q
    return MODS[4] + n // 5 if n % 5 == 0 and n // 5 <= MODS[5] - MODS[4] else None


def make_plan():
    p = Plan()

    def lin(key, what, owner, n, cols=("x",)):
        for f in range(n):
            p.chunk((key, f), (*what, f))
            for c in cols:
                p.job((key, f, c), owner, [(key, f)] if c == cols[-1] else [])

    def rows(key, what, owner):
        for pair in range(4):
            for s in range(2):
                p.chunk((key, 2 * pair + s), (*what, 2 * pair + s))
            for t in range(TX):
                p.job((key, pair, t), owner, [(key, 2 * pair + s) for s in range(2)] if t == TX - 1 else [])

    def modulate(f, lo, hi):
        if f < hi:
            p.chunk(("mod", f), ("mod", f), False)
            p.job(("mod", f), "A", [("mod", f)])
        if f > lo:
            p.job(("modt", f - 1), "V")

    p.limit = -1
    for f in range(MODS[0] + 1):
        modulate(f, 0, MODS[0])
    p.limit = np.inf
    p.job(("norm1", "x"), "A")
    for f in range(9):
        if f < 8:
            p.chunk(("qk", f), ("w_in", 0, f))
            p.job(("qk", f), "A", [("qk", f)])
        if f:
            p.job(("qkp", f - 1), "V")
        modulate(MODS[0] + f, MODS[0], MODS[1])
    rows("v", ("w_in", 1024), "A")
    for h in range(RET_H):
        for jt in range(TX):
            p.job(("s", h, jt), "V")
        if h:
            for e in range(2):
                p.job(("y", h - 1, e), "A")
    for e in range(2):
        p.job(("y", RET_H - 1, e), "A")
    rows("sv", ("w_in", 4096), "A")
    for h in range(RET_H):
        p.job(("mean", h), "V")
    for h in range(RET_H):
        p.job(("var", h), "A")
    for name, at, m0 in (("g_ret", 2048, 0), ("u", 3072, 8)):
        for f in range(8):
            p.chunk((name, f), ("w_in", at, f))
            p.job((name, f, "x"), "A", [(name, f)])
            modulate(MODS[1] + m0 + f, MODS[1], MODS[2])
    modulate(MODS[2], MODS[1], MODS[2])
    for f in range(8):
        p.job(("mix", f), "V")
    for gate, at, name in (("gate_a", 5120, "ret_out"), ("gate_b", 6144, "sgu_out")):
        for f in range(9):
            if f < 8:
                p.chunk((gate, f), ("w_in", at, f))
                p.job((gate, f, "x"), "A", [(gate, f)])
            if f:
                p.chunk((name, f - 1), ("w_" + name, 0, f - 1))
                p.job((name, f - 1, "x"), "V", [(name, f - 1)])
    lin("w_out", ("w_out", 0), "V", 8)
    p.job(("norm2", "x"), "A")
    p.limit = len(p.splits) + 15
    for f in range(17):
        if f < 16:
            p.chunk(("pq", f), ("peer_w_q", 0, f))
            p.job(("pq", f), "A", [("pq", f)])
        if f:
            p.job(("sc", f - 1), "A")
        if f < 9:
            modulate(MODS[2] + f, MODS[2], MODS[3])
    for f in range(MODS[3], MODS[4] + 1):
        modulate(f, MODS[3], MODS[4])
    for tt in range(TX):
        p.job(("kt", tt), "V")
        for q in range(P // 4):
            p.job(("g", tt, q), "A")
            if mod_with(tt, q):
                modulate(mod_with(tt, q), MODS[4], MODS[5])
    p.limit = np.inf
    for g in range(GROUPS + 1):
        if g < GROUPS:
            for j in range(GROUP):
                p.chunk(("U", g, j), ("U", g * GROUP + j))
                p.job(("U", g, j), "A", [("U", g, j)])
        if g:
            for j in range(GROUP):
                p.chunk(("V", g - 1, j), ("V", (g - 1) * GROUP + j))
            for d in range(KD):
                p.job(("V", g - 1, d), "V", [("V", g - 1, j) for j in range(GROUP)] if d == KD - 1 else [])
    p.job(("final", "x"), "A")
    for l in range(LAYERS):
        upd = l < LAYERS - 1
        xc = ("x", "c") if upd else ("x",)
        p.job(("pre", l, "x"), "A")
        p.job(("pre", l, "c"), "A")

        def queries_a():
            for f in range(6):
                if f < 5:
                    p.chunk(("qa", l, f), ("qa", l, f))
                    both = upd or f == 4
                    p.job(("qa", l, f, "x"), "A", [] if both else [("qa", l, f)])
                    if both:
                        p.job(("qa", l, f, "c"), "A", [("qa", l, f)])
                if f:
                    p.job(("qap", l, f - 1), "V")
            p.chunk(("va", l), ("in2", l, IN_AT["va"]))
            p.job(("va", l, "x"), "A")
            p.job(("va", l, "c"), "A", [("va", l)])
            for c in ("x", "c"):
                p.job(("vat", l, c), "A")

        def attend(kind):
            us = units(kind, l)
            n = len(us)
            for s in range(n + 3):
                if s < n:
                    if kind == "B" and us[s][1] == 0:
                        heads(us[s][0])
                    if us[s][3] > us[s][2]:
                        p.job(("S", kind, l, s, 0), "V")
                    p.job(("S", kind, l, s, 1), "V")
                if 2 <= s <= n + 1:
                    _, _, lo, hi = us[s - 2]
                    p.job(("T", kind, l, s - 2, 0), "A")
                    if hi - lo + 2 > 4:
                        p.job(("T", kind, l, s - 2, 1), "A")
                if s >= 3:
                    p.job(("Y", kind, l, s - 3), "V")

        def heads(h):
            if h == 0:
                project(0)
            if h + 1 < HB:
                project(h + 1)
            else:
                p.limit = np.inf

        def project(h):
            p.chunk(("hb", l, h), ("hb", l, h), False)
            p.job(("hq", l, h, "x"), "A")
            if upd:
                p.job(("hq", l, h, "c"), "A")
            p.job(("hk", l, h, "x"), "A")
            p.job(("hk", l, h, "c"), "A", [("hb", l, h)])
            p.job(("hqp", l, h), "V")

        def branch(b):
            lin(("z", b, l), ("za", l) if b == 0 else ("in2", l, IN_AT["zb"]), "A", 4, xc)
            if b < 2:
                for f in range(4):
                    for c in xc:
                        p.job(("yt", b, l, f, c), "V")
            merge(b)

        def merge(b):
            for f in range(8):
                p.chunk(("gate", b, l, f), ("in2", l, IN_AT["ga"] + b * D, f))
                for c in xc:
                    p.job(("gate", b, l, f, c), "A", [("gate", b, l, f)] if c == xc[-1] else [])
                if f % 2 == 0:
                    p.chunk(("br", b, l, f // 2), ("br", l, b, f // 2))
                for c in xc:
                    last = f % 2 == 1 and c == xc[-1]
                    p.job(("br", b, l, f, c), "V", [("br", b, l, f // 2)] if last else [])

        def queries_b():
            p.limit = len(p.splits) + QL + KVL
            lin(("lat", l), ("in2", l, IN_AT["qlb"]), "A", 3, xc)
            lin(("latkv", l), ("in2", l, IN_AT["kvlb"]), "A", 2, ("x", "c"))
            p.chunk(("krb", l), ("krb", l))
            p.job(("krb", l, "x"), "A")
            p.job(("krb", l, "c"), "A", [("krb", l)])
            p.job(("krbp", l), "V")
            for c in xc:
                p.job(("qn", l, c), "A")
            for c in ("x", "c"):
                p.job(("kvn", l, c), "A")
            p.chunk(("vb", l), ("vb", l), False)
            for t in range(TA):
                p.job(("vb", l, t), "A", [("vb", l)] if t == TA - 1 else [])

        queries_b()
        attend("B")
        branch(1)
        queries_a()
        attend("A")
        branch(0)
        for f in range(4):
            for name, owner in (("cc", "A"), ("uc", "V"), ("bc", "V"), ("zc", "A")):
                p.chunk((name, l, f), ("in2", l, IN_AT[name], f))
                for c in xc:
                    p.job((name, l, f, c), owner, [(name, l, f)] if c == xc[-1] else [])
        merge(2)
        lin(("wo", l), ("w_o", l), "A", 8, xc)
        for c in xc:
            p.job(("post", l, c), "A")
    return p


class Counts:

    def __init__(self, eng, plan):
        self.eng, self.plan = eng, plan
        self.made, self.taken, self.last = {}, {}, None
        self.turn, self.moves = None, {}

    def at(self, sem, value):
        assert value > 0
        return value if self.turn is None else self.turn * self.moves.get(sem.name, 0) + value

    def inc(self, sem):
        self.made[sem.name] = self.made.get(sem.name, 0) + 1
        self.last = sem
        return 1

    def own(self):
        return self.last, self.at(self.last, self.made[self.last.name])

    def next(self, sem, n=1):
        self.taken[sem.name] = self.taken.get(sem.name, 0) + n
        return self.at(sem, self.taken[sem.name])

    def filling(self, filled, key):
        return self.at(filled, self.plan.by_key[key].fill + 1)

    def reading(self, sem, key):
        return self.at(sem, self.plan.by_key[key].rank + 1)

    def loaded(self, w_loaded, n):
        sem = w_loaded[n % SLOTS]
        return sem, self.at(sem, 16 * (n // SLOTS + 1))

    def emptied(self, filled, n):
        return self.at(filled, self.plan.free[self.plan.splits[n - SLOTS]])

    def loop(self, turns, moves):
        made, taken = dict(self.made), dict(self.taken)
        self.moves = {sem.name: n for sem, n in moves.items()}
        with self.eng.Fori(0, turns) as i:
            self.turn = i
            yield i
        self.turn = None
        for now, before in ((self.made, made), (self.taken, taken)):
            for name in now:
                step = now[name] - before.get(name, 0)
                assert step == 0 or step == self.moves.get(name, 0), (name, step)
                now[name] = before.get(name, 0) + turns * step


def build(nc, plan, d, out):
    f32, u32, i32 = mybir.dt.float32, mybir.dt.uint32, mybir.dt.int32
    ALU, ACT, AX = mybir.AluOpType, mybir.ActivationFunctionType, mybir.AxisListType.X
    f32r = mybir.dt.float32r
    x_dram = nc.dram_tensor("x_kept", [P, KD, A], f32, kind="Internal").ap()
    gates_dram = nc.dram_tensor("gates_by_expert", [NTB, P, NK, TB], f32, kind="Internal").ap()

    ctx = ExitStack()
    with ctx:
        def sb(name, shape, dt=f32):
            return ctx.enter_context(nc.sbuf_tensor(name, shape, dt))

        vec = sb("vec", [P, NVEC])
        consts = {n: sb(n, [P, w]) for n, w in CONSTS}
        ones = sb("ones", [P, P])
        epsc = sb("epsc", [P, 1])
        cs = sb("cs", [P, KD, 3])
        mrow = sb("mrow", [P, 2, P])
        mod = sb("mod", [P, 96, 3])
        scl1 = sb("scl1", [P, KD])
        scl2 = sb("scl2", [P, KD])
        pre = sb("pre", [P, LAYERS, 2, KD])
        post = sb("post", [P, LAYERS, 2, KD])
        rt = sb("rt", [P, A])
        rk = sb("rk", [P, A])
        tab = sb("tab", [P, 4096])
        mx = sb("mx", [P, 8])
        nm = sb("nm", [P, 8])
        es = sb("es", [P, 8])
        sm = sb("sm", [P, 8])
        inv = sb("inv", [P, TA, 8])
        stats = sb("stats", [P, TX, 2, 6])
        mv = sb("mv", [P, TX, 2])
        rs = sb("rs", [P, TX])
        POOL = 45568
        pool0 = -(-nc.sbuf_base // 32) * 32
        sb("pool", [P, POOL + 8])

        def place(name, at, *dims, dt=f32):
            assert at + int(np.prod(dims)) <= POOL, name
            return nc.alloc_sbuf_tensor_at(name, [P, *dims], dt, offset=pool0 + 4 * at)

        WR = place("WR", 0, SLOTS, KD, P)
        WH, WL = place("WH", 4096, SLOTS, KD, P, dt=f32r), place("WL", 8192, SLOTS, KD, P, dt=f32r)
        X0 = 12288
        bank = [ctx.enter_context(nc.psum_tensor(f"bank{b}", [P, 512], f32)) for b in range(RING)]

        def sem(name):
            return ctx.enter_context(nc.semaphore(name))

        filled = sem("filled")
        act_read, dve_read = sem("act_read"), sem("dve_read")
        act_step, dve_step = sem("act_step"), sem("dve_step")
        w_loaded = [sem(f"w_loaded{s}") for s in range(SLOTS)]
        w_hi, w_split = sem("w_hi"), sem("w_split")
        g_loaded = [sem(f"g_loaded{b}") for b in range(2)]
        g_stored = [sem(f"g_stored{b}") for b in range(2)]
        x_loaded, ctx_loaded = sem("x_loaded"), sem("ctx_loaded")
        small_loaded, tab_loaded, tab2_loaded = sem("small_loaded"), sem("tab_loaded"), sem("tab2_loaded")
        sgu_loaded, sub_loaded, out_done = sem("sgu_loaded"), sem("sub_loaded"), sem("out_done")
        cs_ready = sem("cs_ready")
        mod_ready = sem("mod_ready")
        sq_ready = sem("sq_ready")
        xr_ready = sem("xr_ready")
        h_ready = sem("h_ready")
        keys_ready = sem("keys_ready")
        ws_ready = sem("ws_ready")
        ln_row, r_done = sem("ln_row"), sem("r_done")
        vn_ready = sem("vn_ready")
        ysq_ready = sem("ysq_ready")
        g_used = sem("g_used")
        ug_ready = sem("ug_ready")
        gated = sem("gated")
        soft_in, exp_ready = sem("soft_in"), sem("exp_ready")
        kt_ready = sem("kt_ready")
        hot_a, hot_b = sem("hot_a"), sem("hot_b")
        a_ready = sem("a_ready")
        t_full, t_hi, t_split = sem("t_full"), sem("t_hi"), sem("t_split")
        x_kept, x_back = sem("x_kept"), sem("x_back")
        res_ready = sem("res_ready")
        inv_ready = sem("inv_ready")
        qk_ready = sem("qk_ready")
        kr_ready = sem("kr_ready")
        row_ready, p_ready = sem("row_ready"), sem("p_ready")
        lat_ready = sem("lat_ready")
        c_ready = sem("c_ready")
        block = ctx.enter_context(nc.Block())

        def V(name, k=0, n=1):
            return vec[:, VEC[name] + k:VEC[name] + k + n]

        def col(t, tt):
            return t[:, tt * P:(tt + 1) * P]

        XT = place("XT", X0, KD, T)
        Hh, Hl = place("Hh", X0 + 4096, KD, T, dt=f32r), place("Hl", X0 + 8192, KD, T, dt=f32r)
        F0 = X0 + 12288
        qT, kT = place("qT", F0, 4, T), place("kT", F0 + 2048, 4, T)
        Vr, ST = place("Vr", F0 + 4096, TX, D), place("ST", F0 + 8192, 2, TX, T)
        yT1 = place("yT1", F0 + 12288, 8, T)
        R1, G1 = place("R1", F0 + 16384, 3, T), place("G1", F0 + 17920, 2, T)
        lng, lnb = place("lng", F0 + 18944, D), place("lnb", F0 + 19968, D)
        SV = place("SV", F0, TX, D)
        XW = place("XW", F0 + 4096, KD, T)
        uT = place("uT", F0 + 4096, 8, T)
        M1 = place("M1", F0, 8, T)
        yh, yl = place("yh", F0 + 8192, 8, T, dt=f32r), place("yl", F0 + 12288, 8, T, dt=f32r)
        uh, ul = place("uh", F0 + 8192, 8, T, dt=f32r), place("ul", F0 + 4096, 8, T, dt=f32r)
        Mh, Ml = place("Mh", F0 + 12288, 8, T, dt=f32r), place("Ml", F0, 8, T, dt=f32r)
        cosR, sinR = tab[:, 0:T], tab[:, T:2 * T]
        decay = tab[:, 2 * T:6 * T].rearrange("p (h t) -> p h t", h=RET_H)
        bs = tab[:, 3072:3584]
        ws = tab[:, 3584:4096].rearrange("p (g t) -> p g t", g=4)

        S2 = place("S2", F0, TX, 16, P)
        hotA, hotB = place("hotA", F0 + 8192, HOTS, 4, P), place("hotB", F0 + 16928, HOTS, 4, P)
        Q2 = place("Q2", F0 + 8192, 2, T)
        Rw = place("Rw", F0 + 10240, 16, P)
        cand = place("cand", F0 + 12288, PH, PK * PK)
        f1 = F0 + 14336
        top, topi, topf = (place(n_, f1 + 256 * i_, 16, PK)[:, :, :] for i_, n_ in enumerate(("top", "topi", "topf")))
        cv, ca, cb, kk1, kk2, gg, cpos, cpa = (
            place(n_, f1 + 768 + 128 * i_, PH, PK)[:, :, :]
            for i_, n_ in enumerate(("cv", "ca", "cb", "kk1", "kk2", "gg", "cpos", "cpa")))
        gsum, KT = place("gsum", f1 + 1792, 1, 16), place("KT", f1 + 1824, 2, 3, P)
        Gs = place("Gs", 4096, 2, NK, TB)
        sub = tab[:, 0:2048].rearrange("p (s n) -> p s n", s=16)

        ge = place("ge", F0, 2, GROUP, T)
        ah, al = place("ah", F0 + 2048, 2, GROUP, T, dt=f32r), place("al", F0 + 4096, 2, GROUP, T, dt=f32r)
        Gt = [place(f"Gt{b}", F0 + 6144 + 2048 * b, NTB, GPT * GROUP, TB)[:, :, :, :] for b in range(2)]
        ACC = place("ACC", F0 + 10240, KD, T)[:, :, :]
        XF = place("XF", F0, KD, T)

        H2h, H2l = place("H2h", X0, KD, A, dt=f32r), place("H2l", X0 + 6144, KD, A, dt=f32r)
        B0 = X0 + 12288
        X2 = place("X2", B0 + 14336, KD, A)
        X2W = place("X2W", B0, KD, A)
        R4 = place("R4", B0, 3, T)
        LAT, KR = place("LAT", B0 + 1536, QL + KVL, A), place("KR", B0 + 5376, 1, A)
        SrowB, PTB = place("SrowB", B0 + 6144, 3, A), place("PTB", B0 + 8448, 2, TA, P)
        QH, KH = place("QH", B0 + 9984, 2, A), place("KH", B0 + 11520, 2, A)
        vB = place("vB", B0 + 13056, TA, 512)
        YT = place("YT", B0 + 16128, 4, A)
        qA, kA = place("qA", B0 + 1536, 4, A), place("kA", B0 + 4608, 1, A)
        SrowA, PTA = place("SrowA", B0 + 5376, 3, A), place("PTA", B0 + 7680, 2, TA, P)
        M4 = place("M4", B0 + 9216, KD, A)
        vA = place("vA", B0 + 15360, TA, P)
        vT = place("vT", B0 + 7680, 1, A)
        yT = place("yT", B0, 4, A)
        y2h, y2l = place("y2h", B0 + 3072, 4, A, dt=f32r), place("y2l", B0 + 6144, 4, A, dt=f32r)
        SG = place("SG", B0 + 19200, 2, A)
        C1, ZP = place("C1", B0 + 15360, 2, A), place("ZP", B0 + 16896, 2, A + 4)
        C2 = tab[:, 2560:4096].rearrange("p (a b) -> p a b", a=2)
        OF = place("OF", B0, KD, A)
        OS = place("OS", B0 + 6144, KD, A)
        cosA, sinA, cosB, sinB = (tab[:, k * T:(k + 1) * T] for k in range(4))
        band = tab[:, 4 * T:4 * T + 3 * P]
        Srow = {n_: [t_[:, r, :] for r in range(3)] + [tab[:, 2560:2560 + A]]
                for n_, t_ in (("A", SrowA), ("B", SrowB))}
        PT = {"A": PTA, "B": PTB}

        def lat_sq(j):
            return SrowB[:, j, :] if j < 3 else PTB[:, :, :, :].rearrange("p a b c -> p a (b c)")[:, j - 3, :]

        def place_of(kind, h):
            return (h % 4, h // 4) if kind == "A" else (h // 2, h % 2)

        def xcols(c):
            return slice(0, T) if c == "x" else slice(T, A)

        @block.sync
        def _(sp):
            k = Counts(sp, plan)

            def load(n, src):
                if n >= SLOTS:
                    if n - SLOTS in plan.split_of:
                        sp.wait_ge(w_split, k.at(w_split, plan.split_of[n - SLOTS] + 1))
                    else:
                        sp.wait_ge(filled, k.at(filled, plan.free[n - SLOTS]))
                sp.dma_start(WR[:, n % SLOTS, :, :].rearrange("p a b -> p (a b)"), src)\
                    .then_inc(w_loaded[n % SLOTS], 16)

            def load_gates(t, i=None):
                if t >= 2 or i is not None:
                    sp.wait_ge(a_ready, k.at(a_ready, GPT * GROUP * (t - 1)))
                row = t * GPT * GROUP if i is None else i * (2 * GPT * GROUP) + t * GPT * GROUP
                sp.dma_start(Gt[t % 2].rearrange("p n k t -> p n (k t)"),
                             gates_dram[:, :, bass.ds(row, GPT * GROUP), :].rearrange("n p k t -> p n (k t)"))\
                    .then_inc(g_loaded[t % 2], 16)

            W = d["weights"]
            first_u = plan.chunk_at[("U", 0, 0)]
            for n in range(first_u + 4):
                load(n, W[n, :, :])
            for b in range(2):
                sp.wait_ge(g_stored[b], k.at(g_stored[b], 16 * (NTB // 2)))
            load_gates(0)
            load_gates(1)
            g2 = first_u + 6
            for n in range(first_u + 4, g2):
                load(n, W[n, :, :])
            for i in k.loop(15, {w_split: 16, a_ready: 4 * GROUP}):
                for c in range(16):
                    load(g2 + c, W[i * 16 + (g2 + c), :, :])
                    if c in (3, 11):
                        load_gates(2 + c // 8, i)
            for n in range(g2 + 15 * 16, len(plan.chunks)):
                load(n, W[n, :, :])

        @block.gpsimd
        def _(pool):
            k = Counts(pool, plan)
            pool.wait_ge(sgu_loaded, 64)
            nc.gpsimd.affine_select(out=ws, in_=ws, pattern=[[0, 4], [1, P]], compare_op=ALU.is_ge,
                                           fill=0.0, base=0, channel_multiplier=-1).then_inc(ws_ready, k.inc(ws_ready))
            for tt in range(TX):
                pool.wait_ge(dve_read, k.reading(dve_read, ("kt", tt)))
                for q in range(P // 4):
                    n = tt * (P // 4) + q
                    if n >= HOTS:
                        pool.wait_ge(filled, k.filling(filled, ("g", (n - HOTS) // 32, (n - HOTS) % 32)))
                    for t in range(4):
                        c = 4 * q + t
                        nc.gpsimd.tensor_scalar(hotB[:, n % HOTS, t, :], consts["iota128"][:, :],
                                                       KT[:, tt % 2, 1, c:c + 1], None, ALU.is_equal).then_inc(hot_b, k.inc(hot_b))

        @block.tensor
        def _(pe):
            k = Counts(pe, plan)

            def whole(key):
                n = plan.chunk_at[key]
                pe.wait_ge(*k.loaded(w_loaded, n))
                return WR[:, n % SLOTS, :, :].rearrange("p a b -> p (a b)")

            def halves(key):
                n = plan.split_at[key]
                pe.wait_ge(w_split, k.at(w_split, n + 1))
                return WH[:, n % SLOTS, :, :], WL[:, n % SLOTS, :, :]

            def three(a, b):
                return [(a[0], b[0]), (a[1], b[0]), (a[0], b[1])]

            def fill(key, calls):
                before = plan.by_key[key].before
                if before:
                    free = act_read if before.owner == "A" else dve_read
                    pe.wait_ge(free, k.reading(free, before.key))
                b = bank[plan.by_key[key].bank]
                for c in calls(b):
                    last = c
                last.then_inc(filled, 1)

            def product(key, out_cols, pairs, rows=P, tiles=None, per=1):
                def calls(b):
                    for n, (a, r) in enumerate(pairs):
                        if tiles is not None and n % per == 0:
                            pe.wait_ge(tiles, k.next(tiles))
                        yield nc.tensor.matmul(b[0:rows, out_cols], a, r, start=n == 0, stop=n == len(pairs) - 1)
                fill(key, calls)

            def linear(key, chunk, src, cols, rows=P, tiles=None):
                wh, wl = halves(chunk)
                pairs = []
                for j in range(KD):
                    pairs += three((wh[:, j, 0:rows], wl[:, j, 0:rows]), [h[:, j, cols] for h in src])
                product(key, slice(0, cols.stop - cols.start), pairs, rows, tiles, 3)

            H1, H2 = (Hh, Hl), (H2h, H2l)

            def token_rows(key):
                for pair in range(4):
                    for s in range(2):
                        halves((key, 2 * pair + s))
                    s0 = plan.split_at[(key, 2 * pair)] % SLOTS
                    assert s0 % 2 == 0
                    for t in range(TX):
                        pairs = []
                        for j in range(KD):
                            pairs += three([col(h[:, j, :], t) for h in H1], [w[:, s0:s0 + 2, j, :] for w in (WH, WL)])
                        product((key, pair, t), slice(0, 256), pairs)

            def sum_squares(keys_cols, src, n):
                for i, (key, cols) in enumerate(keys_cols):
                    w = cols.stop - cols.start
                    product(key, slice(0, w), [(ones[:, :], src(j)[:, cols] if callable(src) else src[:, j, cols])
                                               for j in range(n)], tiles=None if i else sq_ready)

            pe.wait_ge(cs_ready, k.next(cs_ready))

            def modulate(f, lo, hi):
                if f < hi:
                    w = whole(("mod", f)).rearrange("p (k n) -> p k n", k=KD)
                    product(("mod", f), slice(0, P), [(cs[:, j, :], w[:, j, :]) for j in range(KD)], 3)
                if f > lo:
                    pe.wait_ge(act_read, k.reading(act_read, ("mod", f - 1)))
                    fill(("modt", f - 1), lambda b: [nc.tensor.transpose(b[:, 0:3], mrow[0:3, (f - 1) % 2, :],
                                                                         consts["ident"][0:3, 0:3])])

            for f in range(MODS[0] + 1):
                modulate(f, 0, MODS[0])

            sum_squares([(("norm1", "x"), slice(0, T))], XW, KD)
            for f in range(9):
                if f < 8:
                    linear(("qk", f), ("qk", f), H1, slice(0, T), tiles=None if f else h_ready)
                if f:
                    pe.wait_ge(act_read, k.reading(act_read, ("qk", f - 1)))
                    product(("qkp", f - 1), slice(0, T), [(consts["perm128"][:, :], R1[:, (f - 1) % 3, :])])
                modulate(MODS[0] + f, MODS[0], MODS[1])
            token_rows("v")

            def ret_values(h):
                pe.wait_ge(dve_read, k.reading(dve_read, ("s", h, TX - 1)))
                for e in range(2):
                    def calls(b, h=h, e=e):
                        for jt in range(TX):
                            yield nc.tensor.matmul(
                                b[:, jt * P:T], Vr[:, jt, h * RET_DV + e * P:h * RET_DV + (e + 1) * P],
                                ST[:, h % 2, jt, jt * P:T], start=jt == 0, stop=jt == TX - 1)
                    fill(("y", h, e), calls)
            pe.wait_ge(act_read, k.reading(act_read, ("v", 3, TX - 1)))
            pe.wait_ge(keys_ready, k.next(keys_ready))
            for h in range(RET_H):
                for jt in range(TX):
                    product(("s", h, jt), slice(0, T - jt * P), [(col(kT[:, h, :], jt), qT[:, h, jt * P:T])])
                if h:
                    ret_values(h - 1)
            ret_values(RET_H - 1)
            token_rows("sv")
            pe.wait_ge(act_read, k.reading(act_read, ("y", RET_H - 1, 1)))
            for h in range(RET_H):
                product(("mean", h), slice(0, T), [(ones[:, :], yT1[:, 2 * h + e, :]) for e in range(2)])
            for h in range(RET_H):
                pe.wait_ge(ysq_ready, k.next(ysq_ready, 2))
                product(("var", h), slice(0, T), [(ones[:, :], XW[:, 2 * h + e, :]) for e in range(2)])
            for name, m0 in (("g_ret", 0), ("u", 8)):
                for f in range(8):
                    linear((name, f, "x"), (name, f), H1, slice(0, T))
                    modulate(MODS[1] + m0 + f, MODS[1], MODS[2])
            modulate(MODS[2], MODS[1], MODS[2])
            pe.wait_ge(ws_ready, k.next(ws_ready))
            pe.wait_ge(vn_ready, k.next(vn_ready, TX))
            for f in range(8):
                def calls(b, f=f):
                    for n in range(TX):
                        yield nc.tensor.matmul(col(b, n), SV[:, n, f * P:(f + 1) * P], ws[:, f // 2, :],
                                               start=True, stop=True)
                fill(("mix", f), calls)
            for gate, name, src in (("gate_a", "ret_out", (yh, yl)), ("gate_b", "sgu_out", (uh, ul))):
                for f in range(9):
                    if f < 8:
                        linear((gate, f, "x"), (gate, f), H1, slice(0, T))
                    if f:
                        linear((name, f - 1, "x"), (name, f - 1), src, slice(0, T), tiles=None if f > 1 else t_split)
            for f in range(8):
                linear(("w_out", f, "x"), ("w_out", f), (Mh, Ml), slice(0, T), tiles=None if f else t_split)

            sum_squares([(("norm2", "x"), slice(0, T))], XW, KD)
            pe.wait_ge(sub_loaded, k.at(sub_loaded, 16))
            for f in range(17):
                if f < 16:
                    linear(("pq", f), ("pq", f), H1, slice(0, T), tiles=None if f else h_ready)
                if f:
                    pe.wait_ge(act_read, k.reading(act_read, ("pq", f - 1)))

                    def calls(b, f=f - 1):
                        for t in range(TX):
                            yield nc.tensor.matmul(col(b, t), col(Q2[:, f % 2, :], t), sub[:, f, :],
                                                   start=True, stop=True)
                    fill(("sc", f - 1), calls)
                if f < 9:
                    modulate(MODS[2] + f, MODS[2], MODS[3])
            for f in range(MODS[3], MODS[4] + 1):
                modulate(f, MODS[3], MODS[4])
            for tt in range(TX):
                pe.wait_ge(kt_ready, k.next(kt_ready))

                def calls(b):
                    for n, src in enumerate((kk1, kk2, gg)):
                        yield nc.tensor.transpose(col(b, n), src.rearrange("p a b -> p (a b)"), consts["ident"][:, :])
                fill(("kt", tt), calls)
                for q in range(P // 4):
                    pe.wait_ge(hot_a, k.next(hot_a, 4))
                    pe.wait_ge(hot_b, k.next(hot_b, 4))
                    n = tt * (P // 4) + q

                    def calls(b, n=n):
                        for t in range(4):
                            yield nc.tensor.matmul(col(b, t), hotB[:, n % HOTS, t, :], hotA[:, n % HOTS, t, :],
                                                   start=True, stop=True)
                    fill(("g", tt, q), calls)
                    if mod_with(tt, q):
                        modulate(mod_with(tt, q), MODS[4], MODS[5])

            def up(g):
                for j in range(GROUP):
                    linear(("U", g, j), ("U", g, j), H1, slice(0, T))

            def down(g):
                w = [halves(("V", g, j)) for j in range(GROUP)]
                pe.wait_ge(t_split, k.next(t_split, GROUP))
                for dd in range(KD):
                    pairs = []
                    for j, (wh, wl) in enumerate(w):
                        pairs += three((wh[:, dd, :], wl[:, dd, :]), (ah[:, g % 2, j, :], al[:, g % 2, j, :]))
                    product(("V", g, dd), slice(0, T), pairs)
            up(0)
            up(1)
            down(0)
            for i in k.loop(15, {act_read: 4 * GROUP, dve_read: 4 * KD, w_split: 16, t_split: 4 * GROUP}):
                for g in range(2, 6):
                    up(g)
                    down(g - 1)
            for g in range(GROUPS - 2, GROUPS):
                up(g)
                down(g - 1)
            down(GROUPS - 1)
            sum_squares([(("final", "x"), slice(0, T))], XF, KD)

            for l in range(LAYERS):
                upd = l < LAYERS - 1
                xc = ("x", "c") if upd else ("x",)
                sum_squares([(("pre", l, c), xcols(c)) for c in ("x", "c")], X2W, KD)

                def queries_a():
                    for f in range(6):
                        if f < 5:
                            linear(("qa", l, f, "x"), ("qa", l, f), H2, xcols("x"))
                            if upd or f == 4:
                                linear(("qa", l, f, "c"), ("qa", l, f), H2, xcols("c"))
                        if f:
                            pe.wait_ge(act_read, k.reading(act_read, ("qa", l, f - 1, "x")))
                            product(("qap", l, f - 1), slice(0, T), [(consts["permA"][:, :], R4[:, (f - 1) % 3, :])])
                    for c in ("x", "c"):
                        linear(("va", l, c), ("va", l), H2, xcols(c))
                    pe.wait_ge(act_read, k.reading(act_read, ("va", l, "c")))
                    for c, tiles in (("x", range(0, TX)), ("c", range(TX, TA))):
                        def calls(b, tiles=tiles):
                            for n, t in enumerate(tiles):
                                yield nc.tensor.transpose(col(b, n), col(vT[:, 0, :], t), consts["ident"][:, :])
                        fill(("vat", l, c), calls)

                def project(h):
                    w = whole(("hb", l, h))
                    wq = w[:, 0:QL * QKB].rearrange("p (k n) -> p k n", k=QL)
                    wk = w[:, QL * QKB:QL * QKB + KVL * NOPE].rearrange("p (k n) -> p k n", k=KVL)
                    for c in xc:
                        product(("hq", l, h, c), slice(0, T if c == "x" else C),
                                [(wq[:, j, :], LAT[:, j, xcols(c)]) for j in range(QL)], QKB)
                    for c in ("x", "c"):
                        product(("hk", l, h, c), slice(0, T if c == "x" else C),
                                [(wk[:, j, :], LAT[:, QL + j, xcols(c)]) for j in range(KVL)], NOPE)
                    pe.wait_ge(act_read, k.reading(act_read, ("hq", l, h, "x")))
                    product(("hqp", l, h), slice(0, T),
                            [(consts["permB"][0:QKB, 0:QKB], R4[0:QKB, h % 3, :])], QKB)

                def attend(kind):
                    us = units(kind, l)
                    n = len(us)
                    for s in range(n + 3):
                        if s < n:
                            h, qb, lo, hi = us[s]
                            if kind == "A":
                                if s == 0:
                                    pe.wait_ge(qk_ready, k.next(qk_ready))
                                p0 = HDA * (h // 4)
                                q, kk = col(qA[p0:p0 + HDA, h % 4, :], qb), kA[p0:p0 + HDA, 0, :]
                            else:
                                if qb == 0:
                                    if h == 0:
                                        project(0)
                                    if h + 1 < HB:
                                        project(h + 1)
                                    pe.wait_ge(qk_ready, k.next(qk_ready))
                                q, kk = col(QH[0:QKB, h % 2, :], qb), KH[0:QKB, h % 2, :]
                            if hi > lo:
                                product(("S", kind, l, s, 0), slice(0, (hi - lo) * P), [(q, kk[:, lo * P:hi * P])])
                            product(("S", kind, l, s, 1), slice(0, C), [(q, kk[:, T:A])])
                        if 2 <= s <= n + 1:
                            u = s - 2
                            _, _, lo, hi = us[u]
                            tiles = hi - lo + 2
                            pe.wait_ge(p_ready, k.next(p_ready))
                            for part in range(2):
                                t0, t1 = 4 * part, min(tiles, 4 * part + 4)
                                if t1 > t0:
                                    def calls(b, t0=t0, t1=t1, u=u):
                                        for t in range(t0, t1):
                                            yield nc.tensor.transpose(col(b, t - t0), col(Srow[kind][u % 4], t),
                                                                      consts["ident"][:, :])
                                    fill(("T", kind, l, u, part), calls)
                        if s >= 3:
                            u = s - 3
                            h, qb, lo, hi = us[u]
                            tiles = list(range(lo, hi)) + [TX, TX + 1]
                            pe.wait_ge(act_read, k.reading(act_read, ("T", kind, l, u, 1 if len(tiles) > 4 else 0)))
                            f = place_of(kind, h)[0]
                            product(("Y", kind, l, u), slice(0, P),
                                    [(vA[:, t, :] if kind == "A" else col(vB[:, t, :], f), PT[kind][:, u % 2, n_, :])
                                     for n_, t in enumerate(tiles)])

                def branch(b):
                    for f in range(4):
                        for c in xc:
                            linear((("z", b, l), f, c), (("z", b, l), f), H2, xcols(c))
                    for f in range(4):
                        pe.wait_ge(inv_ready, k.next(inv_ready))
                        for c in xc:
                            def calls(bk, c=c, f=f):
                                for n_, t in enumerate(range(0, TX) if c == "x" else range(TX, TA)):
                                    yield nc.tensor.transpose(col(bk, n_), col(SG[:, f % 2, :], t),
                                                              consts["ident"][:, :])
                            fill(("yt", b, l, f, c), calls)
                    merge(b)

                def merge(b):
                    for f in range(8):
                        for c in xc:
                            linear(("gate", b, l, f, c), ("gate", b, l, f), H2, xcols(c))
                        if f == 0:
                            pe.wait_ge(t_split, k.next(t_split, 4))
                        wh, wl = (w.rearrange("p a b -> p (a b)").rearrange("p (k n) -> p k n", k=4)
                                  for w in halves(("br", b, l, f // 2)))
                        f0 = (f % 2) * P
                        for c in xc:
                            pairs = []
                            for j in range(4):
                                pairs += three((wh[:, j, f0:f0 + P], wl[:, j, f0:f0 + P]),
                                               (y2h[:, j, xcols(c)], y2l[:, j, xcols(c)]))
                            product(("br", b, l, f, c), slice(0, T if c == "x" else C), pairs)

                for f in range(QL):
                    for c in xc:
                        linear((("lat", l), f, c), (("lat", l), f), H2, xcols(c),
                               tiles=h_ready if f == 0 and c == "x" else None)
                for f in range(KVL):
                    for c in ("x", "c"):
                        linear((("latkv", l), f, c), (("latkv", l), f), H2, xcols(c))
                for c in ("x", "c"):
                    linear(("krb", l, c), ("krb", l), H2, xcols(c), QKB)
                pe.wait_ge(act_read, k.reading(act_read, ("krb", l, "x")))
                product(("krbp", l), slice(0, T), [(consts["permB"][0:QKB, 0:QKB], R4[0:QKB, 0, :])], QKB)
                sum_squares([(("qn", l, c), xcols(c)) for c in xc], lambda j: lat_sq(j), QL)
                sum_squares([(("kvn", l, c), xcols(c)) for c in ("x", "c")], lambda j: lat_sq(QL + j), KVL)
                pe.wait_ge(lat_ready, k.next(lat_ready, QL + KVL))
                wv = whole(("vb", l)).rearrange("p (k n) -> p k n", k=KVL)
                for t in range(TA):
                    product(("vb", l, t), slice(0, 512),
                            [(col(LAT[:, QL + j, :], t), wv[:, j, :]) for j in range(KVL)])
                attend("B")
                branch(1)
                queries_a()
                attend("A")
                branch(0)
                for f in range(4):
                    for name in ("cc", "uc", "bc", "zc"):
                        for c in xc:
                            linear((name, l, f, c), (name, l, f), H2, xcols(c))
                merge(2)
                for f in range(8):
                    for c in xc:
                        linear((("wo", l), f, c), (("wo", l), f), H2, xcols(c),
                               tiles=t_split if f == 0 and c == "x" else None)
                sum_squares([(("post", l, c), xcols(c)) for c in xc], OS, KD)

        @block.scalar
        def _(act):
            k = Counts(act, plan)
            dma = act.dma_start
            dma(vec[:, :], d["vec"][:, :]).then_inc(small_loaded, 16)
            dma(XT[:, :, :], d["x"][:, :, :]).then_inc(x_loaded, 16)
            at = 0
            for name, w in CONSTS:
                dma(consts[name][:, :], d["consts"][:, at:at + w]).then_inc(small_loaded, 16)
                at += w
            dma(tab[:, 0:3072], d["tab1"][:, :]).then_inc(tab_loaded, 16)
            for dst, src in ((bs, "bs"), (ws.rearrange("p g t -> p (g t)"), "ws"), (lng[:, :], "lng"), (lnb[:, :], "lnb")):
                dma(dst, d[src][:, :]).then_inc(sgu_loaded, 16)
            act.wait_ge(small_loaded, k.at(small_loaded, 16 * (1 + len(CONSTS))))
            act.activation(cs[:, :, :].rearrange("p a b -> p (a b)"), V("c3", 0, 24), ACT.Silu)\
                .then_inc(cs_ready, k.inc(cs_ready))

            def high(n):
                c = plan.splits[n]
                act.wait_ge(*k.loaded(w_loaded, c))
                if n >= SLOTS:
                    act.wait_ge(filled, k.emptied(filled, n))
                act.activation(WH[:, n % SLOTS, :, :].rearrange("p a b -> p (a b)"),
                               WR[:, c % SLOTS, :, :].rearrange("p a b -> p (a b)"), ACT.Copy)\
                    .then_inc(w_hi, k.inc(w_hi))

            split = [0]

            def ahead(key):
                while split[0] <= min(plan.by_key[key].split, len(plan.splits) - 1):
                    high(split[0])
                    split[0] += 1

            def filled_at(key):
                ahead(key)
                return k.filling(filled, key)

            def dve_at(key):
                ahead(key)
                return k.reading(dve_read, key)

            def out_of(key, dst, src_cols, func=ACT.Copy, rows=P, **kw):
                act.wait_ge(filled, filled_at(key) if k.turn is None else k.filling(filled, key))
                j = plan.by_key[key]
                assert j.owner == "A" and k.made.get(act_read.name, 0) == j.rank or k.turn is not None, key
                src = src_cols(bank[j.bank]) if callable(src_cols) else bank[j.bank][0:rows, src_cols]
                act.activation(dst, src, func, **kw).then_inc(act_read, k.inc(act_read))

            def square(src, dst, j, w):
                act.activation(dst[:, j, 0:w], src[:, j, 0:w], ACT.Square).then_inc(sq_ready, k.inc(sq_ready))

            def root(key, dst, cols, n):
                out_of(key, dst, cols, ACT.Sqrt, scale=1.0 / n, bias=epsc[:, 0:1])

            def shift(x, hi, scale, bias, cols, w):
                for j in range(KD):
                    act.wait_ge(xr_ready, k.next(xr_ready))
                    for c in cols:
                        act.activation(x[:, j, xcols(c)], x[:, j, xcols(c)], ACT.Identity,
                                       scale=scale(c, j), bias=bias(c, j)).then_inc(act_step, k.inc(act_step))
                    act.wait_ge(*k.own())
                    act.activation(hi[:, j, 0:w], x[:, j, 0:w], ACT.Copy).then_inc(t_hi, k.inc(t_hi))

            def high_tile(dst, src):
                act.activation(dst, src, ACT.Copy).then_inc(t_hi, k.inc(t_hi))

            def modulate(f, lo, hi):
                if f < hi:
                    if f >= lo + 2:
                        act.wait_ge(filled, filled_at(("modt", f - 2)))
                    elif lo:
                        act.wait_ge(filled, filled_at(("modt", lo - 1)))
                    out_of(("mod", f), mrow[0:3, f % 2, :], slice(0, P), rows=3)

            act.wait_ge(x_loaded, k.at(x_loaded, 16))
            for j in range(KD):
                square(XT, XW, j, T)
            for f in range(MODS[0] + 1):
                modulate(f, 0, MODS[0])
            act.wait_ge(mod_ready, k.next(mod_ready))
            root(("norm1", "x"), rt[:, 0:T], slice(0, T), D)
            shift(XW, Hh, lambda c, j: scl1[:, j:j + 1], lambda c, j: mod[:, j, 0:1], ("x",), T)
            for f in range(8):
                if f >= 3:
                    act.wait_ge(dve_read, dve_at(("qkp", f - 3)))
                out_of(("qk", f), R1[:, f % 3, :], slice(0, T), scale=1.0 if f < 4 else RET_DK ** -0.5)
                modulate(MODS[0] + f, MODS[0], MODS[1])
            for pair in range(4):
                for t in range(TX):
                    out_of(("v", pair, t), Vr[:, t, pair * 256:(pair + 1) * 256], slice(0, 256))
            for h in range(RET_H):
                for e in range(2):
                    out_of(("y", h, e), yT1[:, 2 * h + e, :], slice(0, T))
            for pair in range(4):
                for t in range(TX):
                    out_of(("sv", pair, t), SV[:, t, pair * 256:(pair + 1) * 256], slice(0, 256), ACT.Gelu)
            act.wait_ge(ln_row, k.next(ln_row))
            act.activation(rs[:, :], mv[:, :, 1], ACT.Sqrt, bias=epsc[:, 0:1]).then_inc(r_done, k.inc(r_done))
            for h in range(RET_H):
                for e in range(2):
                    act.wait_ge(dve_read, dve_at(("mean", h)))
                    act.activation(XW[:, 2 * h + e, :], yT1[:, 2 * h + e, :], ACT.Square)\
                        .then_inc(ysq_ready, k.inc(ysq_ready))
            for h in range(RET_H):
                out_of(("var", h), ST[:, 0, h, :], slice(0, T), ACT.Sqrt, scale=1.0 / RET_DV, bias=epsc[:, 0:1])
            for f in range(8):
                if f >= 2:
                    act.wait_ge(g_used, k.next(g_used))
                out_of(("g_ret", f, "x"), G1[:, f % 2, :], slice(0, T), ACT.Silu)
                modulate(MODS[1] + f, MODS[1], MODS[2])
            for f in range(8):
                out_of(("u", f, "x"), uT[:, f, :], slice(0, T), ACT.Gelu)
                modulate(MODS[1] + 8 + f, MODS[1], MODS[2])
            act.wait_ge(g_used, k.at(g_used, 8))
            ahead(("mix", 7))
            act.wait_ge(ug_ready, k.next(ug_ready, 8))
            for f in range(8):
                high_tile(yh[:, f, :], yT1[:, f, :])
            for f in range(8):
                if f >= 2:
                    act.wait_ge(dve_read, dve_at(("ret_out", f - 2, "x")))
                out_of(("gate_a", f, "x"), G1[:, f % 2, :], slice(0, T), ACT.Sigmoid)
            act.wait_ge(filled, filled_at(("ret_out", 7, "x")))
            for f in range(8):
                high_tile(uh[:, f, :], uT[:, f, :])
            for f in range(10):
                if f < 8:
                    act.wait_ge(dve_read, dve_at((("sgu_out", f - 2) if f >= 2 else ("ret_out", f + 6)) + ("x",)))
                    out_of(("gate_b", f, "x"), G1[:, f % 2, :], slice(0, T), ACT.Sigmoid)
                if f >= 2:
                    ahead(("sgu_out", f - 2, "x"))
                    act.wait_ge(gated, k.next(gated))
                    high_tile(Mh[:, f - 2, :], M1[:, f - 2, :])
            for f in range(8):
                act.wait_ge(dve_read, dve_at(("w_out", f, "x")))
                square(XT, XW, f, T)
            root(("norm2", "x"), rt[:, 0:T], slice(0, T), D)
            dma(tab[:, 0:2048], d["sub"][:, :]).then_inc(sub_loaded, 16)
            act.wait_ge(mod_ready, k.next(mod_ready))
            shift(XW, Hh, lambda c, j: scl2[:, j:j + 1], lambda c, j: mod[:, 24 + j, 0:1], ("x",), T)
            for f in range(17):
                if f < 16:
                    if f >= 2:
                        act.wait_ge(filled, filled_at(("sc", f - 2)))
                    out_of(("pq", f), Q2[:, f % 2, :], slice(0, T))
                if f:
                    out_of(("sc", f - 1), S2[:, :, f - 1, :], lambda b: b[:, :].rearrange("p (t n) -> p t n", t=TX))
                if f < 9:
                    modulate(MODS[2] + f, MODS[2], MODS[3])
            dma(tab[:, 0:4 * T + 3 * P], d["tab2"][:, :]).then_inc(tab2_loaded, 16)
            for f in range(MODS[3], MODS[4] + 1):
                modulate(f, MODS[3], MODS[4])

            def softmax(tt):
                act.wait_ge(soft_in, k.next(soft_in))
                act.activation(gg, gg, ACT.Exp).then_inc(exp_ready, k.inc(exp_ready))
            softmax(0)
            for tt in range(TX):
                for q in range(P // 4):
                    n = tt * (P // 4) + q
                    tb, sl = n // 8, (n // 8) % 2
                    if n % 8 == 0 and tb >= 2:
                        act.wait_ge(g_stored[sl], k.at(g_stored[sl], 16 * (tb // 2)))
                    out_of(("g", tt, q), Gs[:, sl, :, (n % 8) * 4:(n % 8) * 4 + 4].rearrange("p k t -> p t k"),
                           lambda b: b[:, :].rearrange("p (t n) -> p t n", t=4))
                    if n % 8 == 7:
                        act.wait_ge(*k.own())
                        dma(gates_dram[tb, :, :, :].rearrange("p k t -> p (k t)"),
                            Gs[:, sl, :, :].rearrange("p k t -> p (k t)")).then_inc(g_stored[sl], 16)
                    if mod_with(tt, q):
                        modulate(mod_with(tt, q), MODS[4], MODS[5])
                    if q == 27 and tt + 1 < TX:
                        softmax(tt + 1)
            dma(X2[:, :, T:A], d["ctx"][:, :, :]).then_inc(ctx_loaded, 16)
            for b in range(2):
                act.wait_ge(g_stored[b], k.at(g_stored[b], 16 * (NTB // 2)))
            S = plan.split_at
            for j in range(GROUP):
                high(S["U", 0, j])

            def group(g):
                for j in range(GROUP):
                    if g:
                        high(S["V", g - 1, j])
                    if g >= 2:
                        act.wait_ge(t_split, k.at(t_split, TILES + GROUP * (g - 1)))
                    out_of(("U", g, j), ge[:, g % 2, j, :], slice(0, T), ACT.Gelu)
                if g + 1 < GROUPS:
                    for j in range(GROUP):
                        high(S["U", g + 1, j])
                for j in range(GROUP):
                    act.wait_ge(a_ready, k.at(a_ready, GROUP * g + j + 1))
                    if g >= 2:
                        act.wait_ge(filled, k.filling(filled, ("V", g - 2, KD - 1)))
                    high_tile(ah[:, g % 2, j, :], ge[:, g % 2, j, :])
            split[0] = len(plan.splits)
            group(0)
            group(1)
            per_group = {w_loaded[s]: 64 for s in range(SLOTS)}
            for i in k.loop(15, {filled: 40, act_read: 4 * GROUP, t_split: 4 * GROUP, a_ready: 4 * GROUP,
                                 t_hi: 4 * GROUP, w_hi: 16, **per_group}):
                for g in range(2, 6):
                    group(g)
            group(GROUPS - 2)
            group(GROUPS - 1)
            for j in range(GROUP):
                high(S["V", GROUPS - 1, j])
            split[0] = S["V", GROUPS - 1, GROUP - 1] + 1
            for j in range(KD):
                act.wait_ge(res_ready, k.next(res_ready))
                square(XT, XF, j, T)
            root(("final", "x"), rt[:, 0:T], slice(0, T), D)
            act.wait_ge(ctx_loaded, k.at(ctx_loaded, 16))

            for l in range(LAYERS):
                upd = l < LAYERS - 1
                xc = ("x", "c") if upd else ("x",)
                w = A if upd else T
                for j in range(KD):
                    act.wait_ge(res_ready, k.next(res_ready))
                    square(X2, X2W, j, A)
                dma(x_dram[:, :, :], X2[:, :, :]).then_inc(x_kept, 16)
                for c in ("x", "c"):
                    root(("pre", l, c), rt[:, xcols(c)], slice(0, T if c == "x" else C), D)
                shift(X2W, H2h, lambda c, j: pre[:, l, 0 if c == "x" else 1, j:j + 1],
                      lambda c, j: mod[:, 48 + 24 * l + j, (1 if c == "x" else 2):(2 if c == "x" else 3)],
                      ("x", "c"), A)

                def queries_a():
                    for f in range(5):
                        if f >= 3:
                            act.wait_ge(dve_read, dve_at(("qap", l, f - 3)))
                        dst = qA[:, f, :] if f < 4 else kA[:, 0, :]
                        out_of(("qa", l, f, "x"), R4[:, f % 3, :], slice(0, T))
                        if upd or f == 4:
                            out_of(("qa", l, f, "c"), dst[:, T:A], slice(0, C))
                    for c in ("x", "c"):
                        out_of(("va", l, c), vT[:, 0, xcols(c)], slice(0, T if c == "x" else C))
                    out_of(("vat", l, "x"), vA[:, 0:TX, :], lambda b: b[:, :].rearrange("p (t n) -> p t n", t=TX))
                    out_of(("vat", l, "c"), vA[:, TX:TA, :], lambda b: b[:, 0:C].rearrange("p (t n) -> p t n", t=2))

                def project(h):
                    if h >= 2:
                        us = units("B", l)
                        old = max(n for n, u in enumerate(us) if u[0] == h - 2)
                        act.wait_ge(filled, filled_at(("S", "B", l, old, 1)))
                    if h >= 3:
                        act.wait_ge(dve_read, dve_at(("hqp", l, h - 3)))
                    elif h == 0:
                        act.wait_ge(dve_read, dve_at(("krbp", l)))
                    out_of(("hq", l, h, "x"), R4[0:QKB, h % 3, :], slice(0, T), rows=QKB)
                    if upd:
                        out_of(("hq", l, h, "c"), QH[0:QKB, h % 2, T:A], slice(0, C), rows=QKB)
                    for c in ("x", "c"):
                        out_of(("hk", l, h, c), KH[0:NOPE, h % 2, xcols(c)], slice(0, T if c == "x" else C), rows=NOPE)
                    act.activation(KH[NOPE:QKB, h % 2, :], KR[NOPE:QKB, 0, :], ACT.Copy).then_inc(kr_ready, k.inc(kr_ready))

                def attend(kind):
                    us = units(kind, l)
                    n = len(us)
                    for s in range(n + 3):
                        if s < n and kind == "B" and us[s][1] == 0:
                            if us[s][0] == 0:
                                project(0)
                            if us[s][0] + 1 < HB:
                                project(us[s][0] + 1)
                        if 2 <= s <= n + 1:
                            u = s - 2
                            _, _, lo, hi = us[u]
                            tiles = hi - lo + 2
                            if u >= 2:
                                act.wait_ge(filled, filled_at(("Y", kind, l, u - 2)))
                            for part in range(2):
                                t0, t1 = 4 * part, min(tiles, 4 * part + 4)
                                if t1 > t0:
                                    out_of(("T", kind, l, u, part),
                                           PT[kind][:, u % 2, t0:t1, :].rearrange("p a b -> p (a b)"),
                                           slice(0, (t1 - t0) * P))
                        if s < n:
                            h, qb, lo, hi = us[s]
                            W = (hi - lo) * P + C
                            m = s % 8
                            act.wait_ge(row_ready, k.next(row_ready))
                            if kind == "A":
                                act.activation(es[:, m:m + 1], V("sink", l * 8 + h), ACT.Exp, bias=nm[:, m:m + 1])\
                                    .then_inc(act_step, k.inc(act_step))
                            row = Srow[kind][s % 4][:, 0:W]
                            act.activation(row, row, ACT.Exp, bias=nm[:, m:m + 1], accum_out=sm[:, m:m + 1])\
                                .then_inc(p_ready, k.inc(p_ready))

                def branch(b):
                    for f in range(4):
                        for c in xc:
                            out_of((("z", b, l), f, c), yT[:, f, xcols(c)], slice(0, T if c == "x" else C), ACT.Silu)
                    for f in range(4):
                        act.wait_ge(dve_read, dve_at(("yt", b, l, f, xc[-1])))
                        high_tile(y2h[:, f, 0:w], yT[:, f, 0:w])
                    merge(b)

                def merge(b):
                    for f in range(8):
                        if f >= 2:
                            act.wait_ge(dve_read, dve_at(("br", b, l, f - 2, xc[-1])))
                        for c in xc:
                            out_of(("gate", b, l, f, c), SG[:, f % 2, xcols(c)], slice(0, T if c == "x" else C),
                                   ACT.Sigmoid)

                for f in range(QL):
                    for c in xc:
                        out_of((("lat", l), f, c), LAT[:, f, xcols(c)], slice(0, T if c == "x" else C))
                for f in range(KVL):
                    for c in ("x", "c"):
                        out_of((("latkv", l), f, c), LAT[:, QL + f, xcols(c)], slice(0, T if c == "x" else C))
                out_of(("krb", l, "x"), R4[0:QKB, 0, :], slice(0, T), rows=QKB)
                out_of(("krb", l, "c"), KR[0:QKB, 0, T:A], slice(0, C), rows=QKB)
                act.wait_ge(*k.own())
                for j in range(QL + KVL):
                    wj = A if upd or j >= QL else T
                    act.activation(lat_sq(j)[:, 0:wj], LAT[:, j, 0:wj], ACT.Square).then_inc(sq_ready, k.inc(sq_ready))
                for c in xc:
                    root(("qn", l, c), rt[:, xcols(c)], slice(0, T if c == "x" else C), QL * P)
                for c in ("x", "c"):
                    root(("kvn", l, c), rk[:, xcols(c)], slice(0, T if c == "x" else C), KVL * P)
                act.wait_ge(x_kept, k.at(x_kept, 16 * (l + 1)))
                for t in range(TA):
                    out_of(("vb", l, t), vB[:, t, :], slice(0, 512))
                attend("B")
                branch(1)
                queries_a()
                attend("A")
                branch(0)
                for f in range(5):
                    if f < 4:
                        if f >= 2:
                            act.wait_ge(c_ready, k.at(c_ready, 4 * l + f - 1))
                        for c in xc:
                            out_of(("cc", l, f, c), C1[:, f % 2, xcols(c)], slice(0, T if c == "x" else C))
                        for c in xc:
                            out_of(("zc", l, f, c), C2[:, f % 2, xcols(c)], slice(0, T if c == "x" else C), ACT.Silu)
                    if f:
                        act.wait_ge(c_ready, k.at(c_ready, 4 * l + f))
                        high_tile(y2h[:, f - 1, 0:w], yT[:, f - 1, 0:w])
                merge(2)
                act.wait_ge(filled, filled_at(("gate", 2, l, 7, xc[-1])))
                for f in range(8):
                    ahead(("br", 2, l, f, xc[-1]))
                    act.wait_ge(gated, k.next(gated))
                    high_tile(H2h[:, f, 0:w], M4[:, f, 0:w])
                for f in range(8):
                    for c in xc:
                        out_of((("wo", l), f, c), OF[:, f, xcols(c)], slice(0, T if c == "x" else C))
                    act.wait_ge(*k.own())
                    square(OF, OS, f, w)
                    if f == 0:
                        dma(X2[:, :, :], x_dram[:, :, :]).then_inc(x_back, 16)
                for c in xc:
                    root(("post", l, c), rt[:, xcols(c)], slice(0, T if c == "x" else C), D)
            act.wait_ge(res_ready, k.next(res_ready, KD))
            dma(out[:, :, :], X2[:, :, 0:T]).then_inc(out_done, 16)
            act.wait_ge(out_done, 16)

        @block.vector
        def _(dve):
            k = Counts(dve, plan)
            v = nc.vector
            v1 = v.scalar_tensor_tensor

            def low(n):
                dve.wait_ge(w_hi, k.at(w_hi, n + 1))
                if n >= SLOTS:
                    dve.wait_ge(filled, k.emptied(filled, n))
                v.tensor_tensor(WL[:, n % SLOTS, :, :].rearrange("p a b -> p (a b)"),
                                WR[:, plan.splits[n] % SLOTS, :, :].rearrange("p a b -> p (a b)"),
                                WH[:, n % SLOTS, :, :].rearrange("p a b -> p (a b)").bitcast(f32),
                                ALU.subtract).then_inc(w_split, k.inc(w_split))

            split = [0]

            def ahead(key):
                while split[0] <= min(plan.by_key[key].split, len(plan.splits) - 1):
                    low(split[0])
                    split[0] += 1

            def act_at(key):
                ahead(key)
                return k.reading(act_read, key)

            def bank_of(key):
                if k.turn is None:
                    ahead(key)
                dve.wait_ge(filled, k.filling(filled, key))
                j = plan.by_key[key]
                assert j.owner == "V" and (k.made.get(dve_read.name, 0) == j.rank or k.turn is not None), key
                return bank[j.bank]

            def low_tile(dst, src, hi):
                dve.wait_ge(t_hi, k.next(t_hi))
                v.tensor_tensor(dst, src, hi.bitcast(f32), ALU.subtract).then_inc(t_split, k.inc(t_split))

            v.memset(ones[:, :], 1.0).then_inc(dve_step, k.inc(dve_step))
            v.memset(epsc[:, :], EPS).then_inc(dve_step, k.inc(dve_step))
            dve.wait_ge(small_loaded, k.at(small_loaded, 16 * (1 + len(CONSTS))))

            def modulate(f, lo, hi):
                if f > lo:
                    v.tensor_scalar(mod[:, f - 1, :], bank_of(("modt", f - 1))[:, 0:3], V("bias", f - 1), None, ALU.add)\
                        .then_inc(dve_read, k.inc(dve_read))

            for f in range(MODS[0] + 1):
                modulate(f, 0, MODS[0])
            dve.wait_ge(*k.own())
            v1(scl1[:, :], mod[:, 8:16, 0], 1.0, V("norm1", 0, 8), ALU.add, ALU.mult)\
                .then_inc(mod_ready, k.inc(mod_ready))

            def normed(keys, x, work, hi, lo, w):
                for key in keys:
                    dve.wait_ge(act_read, act_at(key))
                v.reciprocal(rt[:, 0:w], rt[:, 0:w]).then_inc(dve_step, k.inc(dve_step))
                dve.wait_ge(*k.own())
                for j in range(KD + 3):
                    if j < KD:
                        v.tensor_tensor(work[:, j, 0:w], x[:, j, 0:w], rt[:, 0:w], ALU.mult)\
                            .then_inc(xr_ready, k.inc(xr_ready))
                    if j >= 3:
                        dve.wait_ge(t_hi, k.next(t_hi))
                        v.tensor_tensor(lo[:, j - 3, 0:w], work[:, j - 3, 0:w], hi[:, j - 3, 0:w].bitcast(f32),
                                        ALU.subtract).then_inc(h_ready, k.inc(h_ready))

            normed([("norm1", "x")], XT, XW, Hh, Hl, T)
            dve.wait_ge(tab_loaded, k.at(tab_loaded, 16))
            for f in range(8):
                dst = qT[:, f, :] if f < 4 else kT[:, f - 4, :]
                dve.wait_ge(act_read, act_at(("qk", f)))
                v.tensor_tensor(dst, R1[:, f % 3, :], cosR, ALU.mult).then_inc(dve_step, k.inc(dve_step))
                b = bank_of(("qkp", f))
                v.tensor_tensor(G1[:, f % 2, :], b[:, :], sinR, ALU.mult).then_inc(dve_read, k.inc(dve_read))
                dve.wait_ge(*k.own())
                done = keys_ready if f == 7 else dve_step
                v.tensor_tensor(dst, dst, G1[:, f % 2, :], ALU.add).then_inc(done, k.inc(done))
                modulate(MODS[0] + f + 1, MODS[0], MODS[1])
            for h in range(RET_H):
                for jt in range(TX):
                    if h >= 2:
                        dve.wait_ge(filled, k.filling(filled, ("y", h - 2, 1)))
                    b = bank_of(("s", h, jt))
                    v.tensor_tensor(ST[:, h % 2, jt, jt * P:T], b[:, 0:T - jt * P], decay[:, h, 0:T - jt * P],
                                    ALU.mult).then_inc(dve_read, k.inc(dve_read))
            for t in range(TX):
                dve.wait_ge(act_read, act_at(("sv", 3, t)))
                for half in range(2):
                    v.bn_stats(stats[:, t, half, :], SV[:, t, half * 512:(half + 1) * 512])\
                        .then_inc(dve_step, k.inc(dve_step))
            dve.wait_ge(*k.own())
            for t in range(TX):
                done = ln_row if t == TX - 1 else dve_step
                v.bn_aggr(mv[:, t, :], stats[:, t, :, :].rearrange("p a b -> p (a b)")).then_inc(done, k.inc(done))
            for h in range(RET_H):
                b = bank_of(("mean", h))
                v1(yT1[:, 2 * h, :], b[:, :], -1.0 / RET_DV, yT1[:, 2 * h, :], ALU.mult, ALU.add)\
                    .then_inc(dve_step, k.inc(dve_step))
                v1(yT1[:, 2 * h + 1, :], b[:, :], -1.0 / RET_DV, yT1[:, 2 * h + 1, :], ALU.mult, ALU.add)\
                    .then_inc(dve_read, k.inc(dve_read))
            dve.wait_ge(r_done, k.next(r_done))
            v.reciprocal(rs[:, :], rs[:, :]).then_inc(dve_step, k.inc(dve_step))
            dve.wait_ge(sgu_loaded, k.at(sgu_loaded, 64))
            dve.wait_ge(*k.own())
            for t in range(TX):
                v.tensor_scalar(SV[:, t, :], SV[:, t, :], mv[:, t, 0:1], rs[:, t:t + 1],
                                ALU.subtract, ALU.mult).then_inc(dve_step, k.inc(dve_step))
            ahead(("g_ret", 0, "x"))
            dve.wait_ge(*k.own())
            for t in range(TX):
                v.tensor_tensor(SV[:, t, :], SV[:, t, :], lng[:, :], ALU.mult).then_inc(dve_step, k.inc(dve_step))
            ahead(("g_ret", 1, "x"))
            dve.wait_ge(*k.own())
            for t in range(TX):
                v.tensor_tensor(SV[:, t, :], SV[:, t, :], lnb[:, :], ALU.add).then_inc(vn_ready, k.inc(vn_ready))
            for h in range(RET_H):
                dve.wait_ge(act_read, k.reading(act_read, ("var", h)))
                v.reciprocal(ST[:, 0, h, :], ST[:, 0, h, :]).then_inc(dve_step, k.inc(dve_step))
            dve.wait_ge(*k.own())
            for f in range(8):
                v1(yT1[:, f, :], yT1[:, f, :], V("retg", f), ST[:, 0, f // 2, :], ALU.mult, ALU.mult)\
                    .then_inc(dve_step, k.inc(dve_step))
            dve.wait_ge(*k.own())
            for f in range(8):
                dve.wait_ge(act_read, act_at(("g_ret", f, "x")))
                v.tensor_tensor(yT1[:, f, :], yT1[:, f, :], G1[:, f % 2, :], ALU.mult).then_inc(g_used, k.inc(g_used))
                modulate(MODS[1] + f, MODS[1], MODS[2])
            for f in range(MODS[1] + 8, MODS[2] + 1):
                modulate(f, MODS[1], MODS[2])
            dve.wait_ge(*k.own())
            v1(scl2[:, :], mod[:, 32:40, 0], 1.0, V("norm2", 0, 8), ALU.add, ALU.mult)\
                .then_inc(mod_ready, k.inc(mod_ready))
            for f in range(8):
                b = bank_of(("mix", f))
                g0 = (f // 2) * P
                v.tensor_tensor(ST[:, 1, f % 4, :].rearrange("p (n t) -> p n t", n=TX),
                                b[:, :].rearrange("p (n t) -> p n t", n=TX),
                                bs[:, g0:g0 + P].unsqueeze(1).to_broadcast([P, TX, P]), ALU.add)\
                    .then_inc(dve_read, k.inc(dve_read))
                dve.wait_ge(*k.own())
                dve.wait_ge(act_read, k.reading(act_read, ("u", f, "x")))
                v.tensor_tensor(uT[:, f, :], uT[:, f, :], ST[:, 1, f % 4, :], ALU.mult)\
                    .then_inc(ug_ready, k.inc(ug_ready))
            for f in range(8):
                low_tile(yl[:, f, :], yT1[:, f, :], yh[:, f, :])
            for f in range(8):
                dve.wait_ge(act_read, act_at(("gate_a", f, "x")))
                v.tensor_tensor(M1[:, f, :], bank_of(("ret_out", f, "x"))[:, :], G1[:, f % 2, :], ALU.mult)\
                    .then_inc(dve_read, k.inc(dve_read))
            for f in range(8):
                low_tile(ul[:, f, :], uT[:, f, :], uh[:, f, :])
            for f in range(10):
                if f < 8:
                    dve.wait_ge(act_read, act_at(("gate_b", f, "x")))
                    tmp = (rk if f % 2 else rt)[:, 0:T]
                    v.tensor_tensor(tmp, bank_of(("sgu_out", f, "x"))[:, :], G1[:, f % 2, :], ALU.mult)\
                        .then_inc(dve_read, k.inc(dve_read))
                    dve.wait_ge(*k.own())
                    v.tensor_tensor(M1[:, f, :], M1[:, f, :], tmp, ALU.add).then_inc(gated, k.inc(gated))
                if f >= 2:
                    low_tile(Ml[:, f - 2, :], M1[:, f - 2, :], Mh[:, f - 2, :])
            for f in range(8):
                b = bank_of(("w_out", f, "x"))
                v1(XT[:, f, :], b[:, :], mod[:, 16 + f, 0:1], XT[:, f, :], ALU.mult, ALU.add)\
                    .then_inc(dve_read, k.inc(dve_read))
            dve.wait_ge(*k.own())

            normed([("norm2", "x")], XT, XW, Hh, Hl, T)
            for f in range(MODS[2], MODS[3] + 1):
                modulate(f, MODS[2], MODS[3])
            dve.wait_ge(act_read, act_at(("sc", 15)))

            def choose(tt):
                for i in range(16):
                    yield v.max(top[:, i, 0:8], S2[:, tt, i, :]).then_inc(dve_step, k.inc(dve_step))
                dve.wait_ge(*k.own())
                for i in range(16):
                    yield v.max_index(topi[:, i, 0:8].bitcast(u32), top[:, i, 0:8], S2[:, tt, i, :])\
                        .then_inc(dve_step, k.inc(dve_step))
                    yield v.match_replace(Rw[:, i, :], top[:, i, 0:8], S2[:, tt, i, :], NEG)\
                        .then_inc(dve_step, k.inc(dve_step))
                dve.wait_ge(*k.own())
                for i in range(16):
                    yield v.max(top[:, i, 8:16], Rw[:, i, :]).then_inc(dve_step, k.inc(dve_step))
                dve.wait_ge(*k.own())
                for i in range(16):
                    yield v.max_index(topi[:, i, 8:16].bitcast(u32), top[:, i, 8:16], Rw[:, i, :])\
                        .then_inc(dve_step, k.inc(dve_step))
                dve.wait_ge(*k.own())
                yield v.tensor_copy(topf, topi.bitcast(u32)).then_inc(dve_step, k.inc(dve_step))
                halves = top.rearrange("p (h s) k -> p h s k", s=2)
                for h in range(PH):
                    yield v.tensor_tensor(cand[:, h, :].rearrange("p (a b) -> p a b", a=PK),
                                          halves[:, h, 0, :].unsqueeze(2).to_broadcast([P, PK, PK]),
                                          halves[:, h, 1, :].unsqueeze(1).to_broadcast([P, PK, PK]), ALU.add)\
                        .then_inc(dve_step, k.inc(dve_step))
                dve.wait_ge(*k.own())
                rest = Rw.rearrange("p a b -> p (a b)").rearrange("p (h n) -> p h n", h=PH)
                for h in range(PH):
                    yield v.max(cv[:, h, 0:8], cand[:, h, :]).then_inc(dve_step, k.inc(dve_step))
                dve.wait_ge(*k.own())
                for h in range(PH):
                    yield v.max_index(cpos[:, h, 0:8].bitcast(u32), cv[:, h, 0:8], cand[:, h, :])\
                        .then_inc(dve_step, k.inc(dve_step))
                    yield v.match_replace(rest[:, h, :], cv[:, h, 0:8], cand[:, h, :], NEG)\
                        .then_inc(dve_step, k.inc(dve_step))
                dve.wait_ge(*k.own())
                for h in range(PH):
                    yield v.max(cv[:, h, 8:16], rest[:, h, :]).then_inc(dve_step, k.inc(dve_step))
                dve.wait_ge(*k.own())
                for h in range(PH):
                    yield v.max_index(cpos[:, h, 8:16].bitcast(u32), cv[:, h, 8:16], rest[:, h, :])\
                        .then_inc(dve_step, k.inc(dve_step))
                if tt:
                    dve.wait_ge(filled, k.filling(filled, ("kt", tt - 1)))
                yield v.tensor_tensor(gg, cv, cv[:, :, 0:1].to_broadcast([P, PH, PK]), ALU.subtract)\
                    .then_inc(dve_step, k.inc(dve_step))
                dve.wait_ge(*k.own())
                yield v.tensor_scalar(cpa.bitcast(u32), cpos.bitcast(u32), 4, None, ALU.logical_shift_right)\
                    .then_inc(soft_in, k.inc(soft_in))
                yield v.tensor_scalar(cpos.bitcast(u32), cpos.bitcast(u32), 15, None, ALU.bitwise_and)\
                    .then_inc(dve_step, k.inc(dve_step))
                dve.wait_ge(*k.own())
                yield v.tensor_copy(ca, cpa.bitcast(u32)).then_inc(dve_step, k.inc(dve_step))
                yield v.tensor_copy(cb, cpos.bitcast(u32)).then_inc(dve_step, k.inc(dve_step))
                dve.wait_ge(*k.own())
                tf = topf.rearrange("p (h s) k -> p h s k", s=2)
                work = Rw.rearrange("p a b -> p (a b)").rearrange("p (j a) -> p j a", a=PK)
                for s, pos, dst in ((0, ca, kk1), (1, cb, kk2)):
                    yield v.tensor_tensor(work, consts["iota128"][:, 0:PK].unsqueeze(1).to_broadcast([P, PH * PK, PK]),
                                          pos.rearrange("p h j -> p (h j)").unsqueeze(2)
                                          .to_broadcast([P, PH * PK, PK]),
                                          ALU.is_equal).then_inc(dve_step, k.inc(dve_step))
                    dve.wait_ge(*k.own())
                    for h in range(PH):
                        yield v.tensor_tensor(work[:, h * PK:(h + 1) * PK, :], work[:, h * PK:(h + 1) * PK, :],
                                              tf[:, h, s, :].unsqueeze(1).to_broadcast([P, PK, PK]), ALU.mult)\
                            .then_inc(dve_step, k.inc(dve_step))
                    dve.wait_ge(*k.own())
                    yield v.tensor_reduce(dst.rearrange("p h j -> p (h j)"), work, AX, ALU.add)\
                        .then_inc(dve_step, k.inc(dve_step))
                    dve.wait_ge(*k.own())

            def gates():
                dve.wait_ge(exp_ready, k.next(exp_ready))
                v.tensor_reduce(gsum[:, 0, 0:8], gg, AX, ALU.add).then_inc(dve_step, k.inc(dve_step))
                dve.wait_ge(*k.own())
                v.reciprocal(gsum[:, 0, 8:16], gsum[:, 0, 0:8]).then_inc(dve_step, k.inc(dve_step))
                dve.wait_ge(*k.own())
                v.tensor_tensor(gg, gg, gsum[:, 0, 8:16].unsqueeze(2).to_broadcast([P, PH, PK]), ALU.mult)\
                    .then_inc(kt_ready, k.inc(kt_ready))

            following = choose(0)
            for f in range(MODS[3], MODS[4] + 1):
                modulate(f, MODS[3], MODS[4])
                for _ in range(7):
                    next(following, None)
            for _ in following:
                pass
            gates()
            for tt in range(TX):
                if tt >= 2:
                    dve.wait_ge(filled, k.filling(filled, ("g", tt - 2, 31)))
                b = bank_of(("kt", tt))
                v.tensor_copy(KT[:, tt % 2, :, :].rearrange("p a b -> p (a b)"), b[:, 0:3 * P])\
                    .then_inc(dve_read, k.inc(dve_read))
                dve.wait_ge(*k.own())
                following = choose(tt + 1) if tt + 1 < TX else iter(())
                for q in range(P // 4):
                    n = tt * (P // 4) + q
                    if n >= HOTS:
                        dve.wait_ge(filled, k.filling(filled, ("g", (n - HOTS) // 32, (n - HOTS) % 32)))
                    for t in range(4):
                        c = 4 * q + t
                        v.tensor_scalar(hotA[:, n % HOTS, t, :], consts["iota128"][:, :],
                                        KT[:, tt % 2, 0, c:c + 1], KT[:, tt % 2, 2, c:c + 1],
                                        ALU.is_equal, ALU.mult).then_inc(hot_a, k.inc(hot_a))
                    if q >= 3 and mod_with(tt, q - 3):
                        modulate(mod_with(tt, q - 3), MODS[4], MODS[5])
                    for _ in range(5):
                        next(following, None)
                for q in range(P // 4 - 3, P // 4):
                    if mod_with(tt, q):
                        modulate(mod_with(tt, q), MODS[4], MODS[5])
                for _ in following:
                    pass
                if tt + 1 < TX:
                    gates()
            dve.wait_ge(*k.own())
            for l in range(LAYERS):
                for c in range(2):
                    b0 = 48 + 24 * l
                    v1(pre[:, l, c, :], mod[:, b0 + 8:b0 + 16, 1 + c], 1.0, V(f"pre{l}", 0, 8), ALU.add, ALU.mult)\
                        .then_inc(dve_step, k.inc(dve_step))
                    v.tensor_tensor(post[:, l, c, :], mod[:, b0 + 16:b0 + 24, 1 + c], V(f"post{l}", 0, 8), ALU.mult)\
                        .then_inc(dve_step, k.inc(dve_step))

            assert k.made[t_split.name] == TILES
            S = plan.split_at
            for j in range(GROUP):
                low(S["U", 0, j])
            v.memset(ACC.rearrange("p a b -> p (a b)"), 0.0).then_inc(dve_step, k.inc(dve_step))

            def group(g):
                tile = g // GPT
                if g:
                    for j in range(GROUP):
                        low(S["V", g - 1, j])
                for j in range(GROUP):
                    dve.wait_ge(g_loaded[tile % 2], k.at(g_loaded[tile % 2], 16 * (tile // 2 + 1)))
                    dve.wait_ge(act_read, k.reading(act_read, ("U", g, j)))
                    inner = ge[:, g % 2, j, :].rearrange("p (n t) -> p n t", n=NTB)
                    v.tensor_tensor(inner, inner, Gt[tile % 2][:, :, (g % GPT) * GROUP + j, :], ALU.mult)\
                        .then_inc(a_ready, k.inc(a_ready))
                if g + 1 < GROUPS:
                    for j in range(GROUP):
                        low(S["U", g + 1, j])
                for j in range(GROUP):
                    if g >= 2:
                        dve.wait_ge(filled, k.filling(filled, ("V", g - 2, KD - 1)))
                    low_tile(al[:, g % 2, j, :], ge[:, g % 2, j, :], ah[:, g % 2, j, :])

            def add_up(g):
                for dd in range(KD):
                    b = bank_of(("V", g, dd))
                    if dd == 0:
                        dve.wait_ge(*k.own())
                    v.tensor_tensor(ACC[:, dd, :], b[:, :], ACC[:, dd, :], ALU.add).then_inc(dve_read, k.inc(dve_read))
            split[0] = len(plan.splits)
            group(0)
            group(1)
            add_up(0)
            for i in k.loop(15, {filled: 40, act_read: 4 * GROUP, dve_read: 4 * KD, a_ready: 4 * GROUP,
                                 t_hi: 4 * GROUP, t_split: 4 * GROUP, w_hi: 16, w_split: 16,
                                 g_loaded[0]: 16, g_loaded[1]: 16}):
                for g in range(2, 6):
                    group(g)
                    add_up(g - 1)
            for g in range(GROUPS - 2, GROUPS):
                group(g)
                add_up(g - 1)
            for j in range(GROUP):
                low(S["V", GROUPS - 1, j])
            add_up(GROUPS - 1)
            split[0] = S["V", GROUPS - 1, GROUP - 1] + 1
            dve.wait_ge(*k.own())
            for f in range(8):
                v1(XT[:, f, :], ACC[:, f, :], mod[:, 40 + f, 0:1], XT[:, f, :], ALU.mult, ALU.add)\
                    .then_inc(res_ready, k.inc(res_ready))
            dve.wait_ge(act_read, act_at(("final", "x")))
            v.reciprocal(rt[:, 0:T], rt[:, 0:T]).then_inc(dve_step, k.inc(dve_step))
            dve.wait_ge(tab2_loaded, k.at(tab2_loaded, 16))
            dve.wait_ge(ctx_loaded, k.at(ctx_loaded, 16))
            dve.wait_ge(*k.own())
            for f in range(8):
                v1(X2[:, f, 0:T], XT[:, f, :], V("final", f), rt[:, 0:T], ALU.mult, ALU.mult)\
                    .then_inc(res_ready, k.inc(res_ready))

            for l in range(LAYERS):
                upd = l < LAYERS - 1
                xc = ("x", "c") if upd else ("x",)
                w = A if upd else T
                normed([("pre", l, "x"), ("pre", l, "c")], X2, X2W, H2h, H2l, A)

                def queries_a():
                    for f in range(5):
                        dst = qA[:, f, :] if f < 4 else kA[:, 0, :]
                        tmp = SG[:, f % 2, 0:T]
                        dve.wait_ge(act_read, act_at(("qa", l, f, "x")))
                        v.tensor_tensor(dst[:, 0:T], R4[:, f % 3, :], cosA, ALU.mult)\
                            .then_inc(dve_step, k.inc(dve_step))
                        v.tensor_tensor(tmp, bank_of(("qap", l, f))[:, :], sinA, ALU.mult)\
                            .then_inc(dve_read, k.inc(dve_read))
                        dve.wait_ge(*k.own())
                        if f == 4:
                            dve.wait_ge(act_read, act_at(("vat", l, "c")))
                        done = qk_ready if f == 4 else dve_step
                        v.tensor_tensor(dst[:, 0:T], dst[:, 0:T], tmp, ALU.add).then_inc(done, k.inc(done))

                def project(h):
                    dve.wait_ge(act_read, act_at(("hq", l, h, "x")))
                    if h >= 2:
                        us = units("B", l)
                        old = max(n for n, u in enumerate(us) if u[0] == h - 2)
                        dve.wait_ge(filled, k.filling(filled, ("S", "B", l, old, 1)))
                    t_ = rt if h % 2 else rk
                    v.tensor_tensor(QH[0:QKB, h % 2, 0:T], R4[0:QKB, h % 3, :], cosB[0:QKB, :], ALU.mult)\
                        .then_inc(dve_step, k.inc(dve_step))
                    v.tensor_tensor(t_[0:QKB, 0:T], bank_of(("hqp", l, h))[0:QKB, :], sinB[0:QKB, :], ALU.mult)\
                        .then_inc(dve_read, k.inc(dve_read))
                    dve.wait_ge(*k.own())
                    dve.wait_ge(kr_ready, k.next(kr_ready))
                    v.tensor_tensor(QH[0:QKB, h % 2, 0:T], QH[0:QKB, h % 2, 0:T], t_[0:QKB, 0:T], ALU.add)\
                        .then_inc(qk_ready, k.inc(qk_ready))

                def attend(kind):
                    us = units(kind, l)
                    n = len(us)
                    scale = HDA ** -0.5 if kind == "A" else QKB ** -0.5
                    for s in range(n + 3):
                        if s < n and kind == "B" and us[s][1] == 0:
                            if us[s][0] == 0:
                                project(0)
                            if us[s][0] + 1 < HB:
                                project(us[s][0] + 1)
                        if s < n:
                            h, qb, lo, hi = us[s]
                            nl = (hi - lo) * P
                            W = nl + C
                            m = s % 8
                            row = Srow[kind][s % 4]
                            if s >= 4:
                                lo4, hi4 = us[s - 4][2:]
                                old = ("T", kind, l, s - 4, 1 if hi4 - lo4 > 2 else 0)
                                dve.wait_ge(filled, k.filling(filled, old))
                            if nl:
                                b = bank_of(("S", kind, l, s, 0))
                                if kind == "A":
                                    m0 = (lo - qb + 1) * P
                                    v1(row[:, 0:nl], b[:, 0:nl], scale, band[:, m0:m0 + nl], ALU.mult, ALU.add)\
                                        .then_inc(dve_read, k.inc(dve_read))
                                else:
                                    v.tensor_scalar(row[:, 0:nl], b[:, 0:nl], scale, None, ALU.mult)\
                                        .then_inc(dve_read, k.inc(dve_read))
                            b = bank_of(("S", kind, l, s, 1))
                            v.tensor_scalar(row[:, nl:W], b[:, 0:C], scale, None, ALU.mult)\
                                .then_inc(dve_read, k.inc(dve_read))
                            dve.wait_ge(*k.own())
                            v.reduce_max(mx[:, m:m + 1], row[:, 0:W], AX).then_inc(dve_step, k.inc(dve_step))
                            dve.wait_ge(*k.own())
                            if kind == "A":
                                v.tensor_scalar(nm[:, m:m + 1], mx[:, m:m + 1], V("sink", l * 8 + h), -1.0,
                                                ALU.max, ALU.mult).then_inc(row_ready, k.inc(row_ready))
                            else:
                                v.tensor_scalar(nm[:, m:m + 1], mx[:, m:m + 1], -1.0, None, ALU.mult)\
                                    .then_inc(row_ready, k.inc(row_ready))
                        if s >= 3:
                            u = s - 3
                            h, qb, lo, hi = us[u]
                            m = u % 8
                            dve.wait_ge(p_ready, k.next(p_ready))
                            if kind == "A":
                                v.tensor_tensor(sm[:, m:m + 1], sm[:, m:m + 1], es[:, m:m + 1], ALU.add)\
                                    .then_inc(dve_step, k.inc(dve_step))
                                dve.wait_ge(*k.own())
                            f, half = place_of(kind, h)
                            v.reciprocal(inv[:, qb, 2 * f + half:2 * f + half + 1], sm[:, m:m + 1])\
                                .then_inc(dve_step, k.inc(dve_step))
                            r0 = half * 64
                            b = bank_of(("Y", kind, l, u))
                            v.tensor_copy(YT[r0:r0 + 64, f, qb * P:(qb + 1) * P], b[r0:r0 + 64, 0:P])\
                                .then_inc(dve_read, k.inc(dve_read))

                def merge(b):
                    for f in range(8):
                        for c in xc:
                            n_ = T if c == "x" else C
                            dve.wait_ge(act_read, act_at(("gate", b, l, f, c)))
                            s_ = SG[:, f % 2, xcols(c)]
                            p_ = bank_of(("br", b, l, f, c))[:, 0:n_]
                            m_ = M4[:, f, xcols(c)]
                            if b == 1:
                                v.tensor_tensor(m_, p_, s_, ALU.mult).then_inc(dve_read, k.inc(dve_read))
                            else:
                                t_ = rt[:, xcols(c)] if f % 2 else rk[:, xcols(c)]
                                v.tensor_tensor(t_, p_, s_, ALU.mult).then_inc(dve_read, k.inc(dve_read))
                                dve.wait_ge(*k.own())
                                done = gated if b == 2 and c == xc[-1] else dve_step
                                v.tensor_tensor(m_, m_, t_, ALU.add).then_inc(done, k.inc(done))
                    dve.wait_ge(*k.own())

                def spread(f):
                    v.tensor_copy(SG[:, f % 2, 0:w].rearrange("p (t s n) -> p t s n", s=2, n=64),
                                  inv[:, 0:w // P, 2 * f:2 * f + 2].unsqueeze(3).to_broadcast([P, w // P, 2, 64]))\
                        .then_inc(inv_ready, k.inc(inv_ready))

                def branch(b):
                    dve.wait_ge(*k.own())
                    spread(0)
                    spread(1)
                    for f in range(4):
                        dve.wait_ge(act_read, act_at((("z", b, l), f, xc[-1])))
                        v.tensor_tensor(yT[:, f, 0:w], YT[:, f, 0:w], yT[:, f, 0:w], ALU.mult)\
                            .then_inc(dve_step, k.inc(dve_step))
                        dve.wait_ge(*k.own())
                        for c in xc:
                            n_ = T if c == "x" else C
                            v.tensor_tensor(yT[:, f, xcols(c)], bank_of(("yt", b, l, f, c))[:, 0:n_],
                                            yT[:, f, xcols(c)], ALU.mult).then_inc(dve_read, k.inc(dve_read))
                        if f + 2 < 4:
                            spread(f + 2)
                    for f in range(4):
                        low_tile(y2l[:, f, 0:w], yT[:, f, 0:w], y2h[:, f, 0:w])
                    merge(b)

                dve.wait_ge(act_read, act_at(("krb", l, "c")))
                v.tensor_tensor(KR[0:QKB, 0, 0:T], R4[0:QKB, 0, :], cosB[0:QKB, :], ALU.mult)\
                    .then_inc(dve_step, k.inc(dve_step))
                b = bank_of(("krbp", l))
                v.tensor_tensor(QH[0:QKB, 0, 0:T], b[0:QKB, :], sinB[0:QKB, :], ALU.mult)\
                    .then_inc(dve_step, k.inc(dve_step))
                dve.wait_ge(*k.own())
                v.tensor_tensor(KR[0:QKB, 0, 0:T], KR[0:QKB, 0, 0:T], QH[0:QKB, 0, 0:T], ALU.add)\
                    .then_inc(dve_read, k.inc(dve_read))
                for c in xc:
                    dve.wait_ge(act_read, act_at(("qn", l, c)))
                v.reciprocal(rt[:, 0:w], rt[:, 0:w]).then_inc(dve_step, k.inc(dve_step))
                for c in ("x", "c"):
                    dve.wait_ge(act_read, act_at(("kvn", l, c)))
                v.reciprocal(rk[:, :], rk[:, :]).then_inc(dve_step, k.inc(dve_step))
                dve.wait_ge(*k.own())
                for j in range(QL + KVL):
                    r_, w_, g_ = (rt, w, V(f"qa{l}", j)) if j < QL else (rk, A, V(f"kva{l}", j - QL))
                    v1(LAT[:, j, 0:w_], LAT[:, j, 0:w_], g_, r_[:, 0:w_], ALU.mult, ALU.mult)\
                        .then_inc(lat_ready, k.inc(lat_ready))
                dve.wait_ge(x_kept, k.at(x_kept, 16 * (l + 1)))
                attend("B")
                branch(1)
                queries_a()
                attend("A")
                branch(0)
                for f in range(4):
                    z, y = ZP[:, f % 2, :], yT[:, f, :]
                    if f < 2:
                        v.memset(z, 0.0).then_inc(dve_step, k.inc(dve_step))
                        dve.wait_ge(*k.own())
                    spans = [("x", 1, T)] + ([("c", T + 3, C)] if upd else [])
                    for c, z0, n_ in spans:
                        dve.wait_ge(act_read, act_at(("cc", l, f, c)))
                        v.tensor_tensor(z[:, z0:z0 + n_], bank_of(("uc", l, f, c))[:, 0:n_],
                                        C1[:, f % 2, xcols(c)], ALU.mult).then_inc(dve_read, k.inc(dve_read))
                    dve.wait_ge(*k.own())
                    for tap in range(3):
                        wcol = V(f"conv{l}", tap * 4 + f)
                        for c, z0, n_ in spans:
                            src = z[:, z0 - 1 + tap:z0 - 1 + tap + n_]
                            if tap == 0:
                                v.tensor_scalar(y[:, xcols(c)], src, wcol, None, ALU.mult)\
                                    .then_inc(dve_step, k.inc(dve_step))
                            else:
                                v1(y[:, xcols(c)], src, wcol, y[:, xcols(c)], ALU.mult, ALU.add)\
                                    .then_inc(dve_step, k.inc(dve_step))
                        dve.wait_ge(*k.own())
                    for c, _, n_ in spans:
                        v.tensor_tensor(y[:, xcols(c)], y[:, xcols(c)], bank_of(("bc", l, f, c))[:, 0:n_], ALU.mult)\
                            .then_inc(dve_read, k.inc(dve_read))
                    dve.wait_ge(*k.own())
                    for c, _, n_ in spans:
                        dve.wait_ge(act_read, act_at(("zc", l, f, c)))
                        done = c_ready if c == xc[-1] else dve_step
                        v.tensor_tensor(y[:, xcols(c)], y[:, xcols(c)], C2[:, f % 2, xcols(c)], ALU.mult)\
                            .then_inc(done, k.inc(done))
                    if f:
                        low_tile(y2l[:, f - 1, 0:w], yT[:, f - 1, 0:w], y2h[:, f - 1, 0:w])
                low_tile(y2l[:, 3, 0:w], yT[:, 3, 0:w], y2h[:, 3, 0:w])
                merge(2)
                for f in range(8):
                    low_tile(H2l[:, f, 0:w], M4[:, f, 0:w], H2h[:, f, 0:w])
                for c in xc:
                    dve.wait_ge(act_read, act_at(("post", l, c)))
                v.reciprocal(rt[:, 0:w], rt[:, 0:w]).then_inc(dve_step, k.inc(dve_step))
                dve.wait_ge(*k.own())
                dve.wait_ge(x_back, k.at(x_back, 16 * (l + 1)))
                for f in range(8):
                    for n_, c in enumerate(xc):
                        v1(OF[:, f, xcols(c)], OF[:, f, xcols(c)], post[:, l, n_, f:f + 1], rt[:, xcols(c)],
                           ALU.mult, ALU.mult).then_inc(dve_step, k.inc(dve_step))
                    dve.wait_ge(*k.own())
                    v.tensor_tensor(X2[:, f, 0:w], X2[:, f, 0:w], OF[:, f, 0:w], ALU.add)\
                        .then_inc(res_ready, k.inc(res_ready))
                dve.wait_ge(*k.own())


def tiles_of(w):
    k, n = w.shape
    return w.reshape(k // P, P, n).transpose(1, 0, 2).reshape(P, k // P * n)


def lay_chunk(what, a):
    kind, rest = what[0], what[1:]
    if kind == "mod":
        f = rest[0]
        w = a["w_ada"][0] if f < 48 else a["w_mod_2"][(f - 48) // 24]
        f = f if f < 48 else (f - 48) % 24
        return tiles_of(w[:, f * P:(f + 1) * P])
    if kind in ("w_in", "w_ret_out", "w_sgu_out", "w_out", "peer_w_q"):
        at = rest[0] + rest[1] * P
        return tiles_of(a[kind][0][:, at:at + P])
    if kind == "in2":
        at = rest[1] + (rest[2] * P if len(rest) > 2 else 0)
        return tiles_of(a["w_in_2"][rest[0]][:, at:at + P])
    if kind == "qa":
        w, f = a["w_in_2"][rest[0]], rest[1]
        if f == 4:
            return tiles_of(w[:, IN_AT["ka"]:IN_AT["ka"] + P])
        return tiles_of(np.concatenate([w[:, h * HDA:(h + 1) * HDA] for h in (f, f + 4)], axis=1))
    if kind == "za":
        w, f = a["w_in_2"][rest[0]][:, IN_AT["za"]:], rest[1]
        return tiles_of(np.concatenate([w[:, h * HDA:(h + 1) * HDA] for h in (f, f + 4)], axis=1))
    if kind == "U":
        return tiles_of(a["peer_u"][0][rest[0] * P:(rest[0] + 1) * P].T)
    if kind == "V":
        return a["peer_v"][0][rest[0] * P:(rest[0] + 1) * P]
    if kind == "br":
        l, b, f = rest
        w = a["w_branch_2"][l][b][:, f * 256:(f + 1) * 256]
        if b == 0:
            w = w.reshape(2, 4, HDA, 256).transpose(1, 0, 2, 3).reshape(4 * P, 256)
        return tiles_of(w)
    if kind == "w_o":
        return tiles_of(a["w_o_2"][rest[0]][:, rest[1] * P:(rest[1] + 1) * P])
    if kind == "krb":
        out = np.zeros((P, KD, P), np.float32)
        w = a["w_in_2"][rest[0]][:, IN_AT["krb"]:IN_AT["krb"] + ROPE]
        out[:, :, NOPE:QKB] = w.reshape(KD, P, ROPE).transpose(1, 0, 2)
        return out.reshape(P, KD * P)
    if kind == "vb":
        w = a["w_kvb_2"][rest[0]].reshape(KVL * P, HB, NOPE + VB)[:, :, NOPE:]
        return tiles_of(w.reshape(KVL * P, HB * VB))
    if kind == "hb":
        l, h = rest
        out = np.zeros((P, KD * P), np.float32)
        out[:, 0:QL * QKB] = tiles_of(a["w_qb_2"][l][:, h * QKB:(h + 1) * QKB])
        w = a["w_kvb_2"][l][:, h * (NOPE + VB):h * (NOPE + VB) + NOPE]
        out[:, QL * QKB:QL * QKB + KVL * NOPE] = tiles_of(w)
        return out
    raise ValueError(what)


def columns(v):
    return v.reshape(-1, P).T


def swap(n, half, at=0):
    m = np.zeros((P, n), np.float32)
    for b in range(at, n, 2 * half):
        for i in range(half):
            m[b + half + i, b + i] = -1.0
            m[b + i, b + half + i] = 1.0
    return m


def shape_constants():
    f = np.float32
    consts = np.concatenate([np.eye(P, dtype=f), swap(P, 64), swap(P, 32), swap(QKB, 16, NOPE),
                             np.tile(np.arange(P, dtype=f), (P, 1))], axis=1)
    pos = np.arange(T, dtype=f)
    inv = (f(10000.0) ** (-np.arange(64, dtype=f) * f(2.0) / f(128))).astype(f)
    ang = (pos[:, None] * inv[None, :]).astype(f)
    cos, sin = np.cos(ang).astype(f).T, np.sin(ang).astype(f).T
    gamma = 1.0 - 2.0 ** (-5.0 - np.arange(RET_H, dtype=np.float64))
    diff = np.arange(T)[None, :] - np.arange(P)[:, None]
    decay = [np.where(diff >= 0, g ** np.maximum(diff, 0), 0.0).astype(f) for g in gamma]
    tab1 = np.concatenate([np.tile(cos, (2, 1)), np.tile(sin, (2, 1))] + decay, axis=1)

    def axial(rot):
        row, c = np.repeat(np.arange(T // 64, dtype=f), 64), np.tile(np.arange(64, dtype=f), T // 64)
        ax = rot // 2
        iv = (f(10000.0) ** (-np.arange(0, ax, 2, dtype=f) / f(ax))).astype(f)
        an = np.concatenate([row[:, None] * iv, c[:, None] * iv], axis=-1).astype(f)
        return np.cos(an).astype(f).T, np.sin(an).astype(f).T
    ca, sa = axial(HDA)
    cb, sb_ = axial(ROPE)
    one, zero = np.ones((NOPE, T), f), np.zeros((NOPE, T), f)
    pad = np.zeros((P - QKB, T), f)
    i, j = np.arange(P)[:, None], np.arange(3 * P)[None, :]
    band = np.where(np.abs(j - (i + P)) <= P, 0.0, MASKED).astype(f)
    tab2 = np.concatenate([np.tile(ca, (4, 1)), np.tile(sa, (4, 1)), np.concatenate([one, cb, cb, pad]),
                           np.concatenate([zero, sb_, sb_, pad]), band], axis=1)
    return consts, tab1, tab2


def kernel(**inputs):
    import concourse.bacc as bacc
    from concourse.bass_utils import run_bass_kernel_spmd

    a = {n: np.asarray(v) for n, v in inputs.items()}
    plan = make_plan()
    weights = np.empty((len(plan.chunks), P, KD * P), np.float32)
    for n, what in enumerate(plan.chunks):
        weights[n] = lay_chunk(what, a)
    c3 = np.stack([columns(a["c"][0]), columns(a["c_2"][0]), columns(a["c_ctx_2"])], axis=2).reshape(P, 24)
    parts = [c3, columns(a["b_ada"][0]), columns(a["b_mod_2"][0]), columns(a["b_mod_2"][1]),
             columns(a["norm1_g"][0]), columns(a["ret_gn_g"][0]), columns(a["norm2_g"][0]), columns(a["final_g"]),
             np.tile(a["sink_2"].reshape(1, 16), (P, 1))]
    for l in range(LAYERS):
        parts += [columns(a["g_pre_2"][l]), columns(a["g_post_2"][l]), columns(a["g_qa_2"][l]),
                  columns(a["g_kva_2"][l]), columns(a["conv_w_2"][l].reshape(-1))]
    consts, tab1, tab2 = shape_constants()

    def spread(v):
        return np.tile(v.reshape(1, -1), (P, 1))
    arrays = {
        "weights": weights, "vec": np.concatenate(parts, axis=1), "consts": consts, "tab1": tab1, "tab2": tab2,
        "x": tiles_of(a["x"][0].T).reshape(P, KD, T), "ctx": tiles_of(a["ctx_2"][0].T).reshape(P, KD, C),
        "bs": spread(a["sgu_b"][0]), "ws": a["sgu_w"][0].transpose(2, 0, 1).reshape(P, 4 * P),
        "lng": spread(a["sgu_ln_g"][0]), "lnb": spread(a["sgu_ln_b"][0]),
        "sub": a["peer_sub_keys"][0].reshape(16, NK, P).transpose(2, 0, 1).reshape(P, 16 * NK),
    }
    nc = bacc.Bacc("TRN2", target_bir_lowering=False, num_devices=1)
    f32 = mybir.dt.float32
    arrays = {n: np.ascontiguousarray(v) for n, v in arrays.items()}
    d = {n: nc.dram_tensor(f"in_{n}", v.shape, f32, kind="ExternalInput").ap() for n, v in arrays.items()}
    out = nc.dram_tensor("out_features", (P, KD, T), f32, kind="ExternalOutput").ap()
    build(nc, plan, d, out)
    got = run_bass_kernel_spmd(nc, [{f"in_{n}": v for n, v in arrays.items()}], core_ids=[0])
    y = got.results[0]["out_features"]
    return np.ascontiguousarray(y.transpose(2, 1, 0).reshape(1, T, D))
```
